# Optimizing a Trainium2 kernel written in Bass

```python
import math
import jax, jax.numpy as jnp
from jax import lax
import numpy as np

'''Hybrid YOCO-style decoder trunk: retention layer(s) first, then native-sparse-attention layer(s)
that all read one shared K/V stream computed from the residual after the last retention layer.
Input x: (BATCH, SEQ, D_MODEL) float32. Output: (BATCH, SEQ, D_MODEL).'''

D_MODEL = 1024
BATCH = 1
SEQ = 512
DEPTH = 2

N_A = DEPTH // 2
N_B = DEPTH - N_A
RET_HEADS = 4
RET_DK = D_MODEL // RET_HEADS
RET_DV = 2 * RET_DK
RET_CHUNK = 128
RET_ROT_BASE = 10000.0
NSA_HEADS = 16
NSA_GROUPS = 4
NSA_HD = D_MODEL // NSA_HEADS
NSA_REP = NSA_HEADS // NSA_GROUPS
L_CMP = 32
CMP_STRIDE = 16
L_SLC = 64
N_SELECT = 16
WINDOW = 512
CMP_HIDDEN = 4 * NSA_HD
Q_BLOCK = 128
ROPE_THETA = 500000.0
ROPE_DIMS = NSA_HD // 4
D_FF = -(-(8 * D_MODEL) // (3 * 256)) * 256
EPS = 1e-6
NEG = -1e30
BIG = 1e9

kernel_name = 'yoco_retnet_nsa_hybrid'

def rmsnorm(x, g):
    xf = x.astype(jnp.float32)
    y = xf * lax.rsqrt(jnp.mean(xf * xf, axis=-1, keepdims=True) + EPS)
    return (y * g.astype(jnp.float32)).astype(x.dtype)

def apply_rotary(x, freqs):
    n = freqs.shape[0]
    pos = jnp.arange(x.shape[1], dtype=jnp.float32)
    ang = pos[:, None] * freqs[None, :]
    cos = jnp.cos(ang)[None, :, None, :]
    sin = jnp.sin(ang)[None, :, None, :]
    xf = x.astype(jnp.float32)
    x1 = xf[..., :n]
    x2 = xf[..., n:2 * n]
    out = jnp.concatenate([x1 * cos - x2 * sin, x1 * sin + x2 * cos, xf[..., 2 * n:]], axis=-1)
    return out.astype(x.dtype)

def partial_rope_freqs():
    return ROPE_THETA ** (-jnp.arange(0, ROPE_DIMS, 2, dtype=jnp.float32) / ROPE_DIMS)

def swiglu(h, w_in, w_out):
    g, u = jnp.split(h @ w_in, 2, axis=-1)
    return (jax.nn.silu(g) * u) @ w_out

def retention(h, w_in, gn, w_out):
    B, T, _ = h.shape
    Hh, dk, dv, C = RET_HEADS, RET_DK, RET_DV, RET_CHUNK
    n = T // C
    q, k, v, g = jnp.split(h @ w_in, [Hh * dk, 2 * Hh * dk, 2 * Hh * dk + Hh * dv], axis=-1)
    freqs = 1.0 / (RET_ROT_BASE ** jnp.linspace(0.0, 1.0, dk // 2, dtype=jnp.float32))
    q = apply_rotary(q.reshape(B, T, Hh, dk), freqs).astype(jnp.float32)
    k = apply_rotary(k.reshape(B, T, Hh, dk), freqs).astype(jnp.float32) * (dk ** -0.5)
    v = v.reshape(B, T, Hh, dv).astype(jnp.float32)

    def chunks(a):
        return a.reshape(B, n, C, Hh, a.shape[-1]).transpose(1, 0, 3, 2, 4)

    qc, kc, vc = chunks(q), chunks(k), chunks(v)
    log_g = jnp.log1p(-jnp.exp2(-5.0 - jnp.arange(Hh, dtype=jnp.float32)))
    idx = jnp.arange(C, dtype=jnp.float32)
    diff = idx[:, None] - idx[None, :]
    decay = jnp.where(diff >= 0, jnp.exp(log_g[:, None, None] * jnp.maximum(diff, 0.0)), 0.0)
    scores = jnp.einsum('nbhid,nbhjd->nbhij', qc, kc) * decay
    inner = jnp.einsum('nbhij,nbhjv->nbhiv', scores, vc)
    q_decay = jnp.exp(log_g[:, None] * (idx + 1.0))[:, :, None]
    k_decay = jnp.exp(log_g[:, None] * (C - 1.0 - idx))[:, :, None]
    chunk_decay = jnp.exp(log_g * C)[:, None, None]

    def step(state, xs):
        qi, ki, vi = xs
        cross = jnp.einsum('bhid,bhdv->bhiv', qi, state) * q_decay
        state = state * chunk_decay + jnp.einsum('bhjd,bhjv->bhdv', ki * k_decay, vi)
        return state, cross

    _, cross = lax.scan(step, jnp.zeros((B, Hh, dk, dv), jnp.float32), (qc, kc, vc))
    o = (inner + cross).transpose(1, 0, 3, 2, 4).reshape(B, T, Hh, dv)
    mu = jnp.mean(o, axis=-1, keepdims=True)
    var = jnp.mean(jnp.square(o - mu), axis=-1, keepdims=True)
    o = ((o - mu) * lax.rsqrt(var + EPS)).reshape(B, T, Hh * dv) * gn.astype(jnp.float32)
    y = (jax.nn.silu(g.astype(jnp.float32)) * o).astype(h.dtype)
    return y @ w_out

def nsa_shared_kv(x, kv_norm, w_kv, cmp_pos_k, cmp_pos_v, cmp_w1_k, cmp_w2_k, cmp_w1_v, cmp_w2_v):
    B, T, _ = x.shape
    G, d = NSA_GROUPS, NSA_HD
    hk = rmsnorm(x, kv_norm)
    k_c, v_c, k_s, v_s, k_w, v_w = [a.reshape(B, T, G, d) for a in jnp.split(hk @ w_kv, 6, axis=-1)]
    freqs = partial_rope_freqs()
    k_c = apply_rotary(k_c, freqs)
    k_s = apply_rotary(k_s, freqs)
    k_w = apply_rotary(k_w, freqs)
    n_cmp = (T - L_CMP) // CMP_STRIDE + 1
    idx = np.arange(n_cmp)[:, None] * CMP_STRIDE + np.arange(L_CMP)[None, :]

    def compress(a, pos, w1, w2):
        blocks = a[:, idx] + pos[None, None, :, None, :]
        blocks = blocks.transpose(0, 1, 3, 2, 4).reshape(B, n_cmp, G, L_CMP * d)
        return jax.nn.gelu(blocks @ w1) @ w2

    ck = compress(k_c, cmp_pos_k, cmp_w1_k, cmp_w2_k)
    cv = compress(v_c, cmp_pos_v, cmp_w1_v, cmp_w2_v)
    pad = ((0, 0), (WINDOW, 0), (0, 0), (0, 0))
    return (ck, cv, k_s.transpose(0, 2, 1, 3), v_s.transpose(0, 2, 1, 3),
            jnp.pad(k_w, pad), jnp.pad(v_w, pad))

def nsa_attention(h, w_in, w_out, shared):
    ck, cv, ks_all, vs_all, kw_pad, vw_pad = shared
    B, T, _ = h.shape
    H, G, R, d = NSA_HEADS, NSA_GROUPS, NSA_REP, NSA_HD
    nb = T // Q_BLOCK
    n_cmp = ck.shape[1]
    n_slc = T // L_SLC
    n_sel = min(N_SELECT, n_slc)
    proj = h @ w_in
    q = apply_rotary(proj[..., :H * d].reshape(B, T, H, d), partial_rope_freqs()) * (d ** -0.5)
    gates = jax.nn.sigmoid(proj[..., H * d:].astype(jnp.float32))
    q = q.reshape(B, nb, Q_BLOCK, G, R, d).transpose(1, 0, 2, 3, 4, 5)
    gates = gates.reshape(B, nb, Q_BLOCK, G, R, 3).transpose(1, 0, 2, 3, 4, 5)
    cmp_end = jnp.arange(n_cmp) * CMP_STRIDE + L_CMP - 1
    cs = np.arange(n_cmp)[:, None] * CMP_STRIDE
    ss = np.arange(n_slc)[None, :] * L_SLC
    overlap = np.clip(np.minimum(cs + L_CMP, ss + L_SLC) - np.maximum(cs, ss), 0, None) / CMP_STRIDE
    overlap = jnp.asarray(overlap, dtype=jnp.float32)
    slc_ids = jnp.arange(n_slc)
    gather = jax.vmap(jax.vmap(lambda a, i: a[i]))

    def block(xs):
        bi, qb, gb = xs
        t = bi * Q_BLOCK + jnp.arange(Q_BLOCK)
        s = jnp.einsum('bqgrd,bngd->bgrqn', qb, ck, preferred_element_type=jnp.float32)
        valid = cmp_end[None, :] <= t[:, None]
        p_c = jax.nn.softmax(jnp.where(valid, s, NEG), axis=-1) * jnp.any(valid, axis=-1)[:, None]
        o_c = jnp.einsum('bgrqn,bngd->bqgrd', p_c.astype(cv.dtype), cv)
        imp = jnp.einsum('bgqn,ns->bgqs', jnp.sum(p_c, axis=2), overlap)
        cur = t // L_SLC
        forced = (slc_ids[None, :] == 0) | (slc_ids[None, :] == cur[:, None]) | (slc_ids[None, :] == cur[:, None] - 1)
        causal_blk = slc_ids[None, :] * L_SLC <= t[:, None]
        imp = jnp.where(forced, BIG, jnp.where(causal_blk, imp, NEG))
        _, sel = lax.top_k(imp, n_sel)
        tok = (sel[..., None] * L_SLC + jnp.arange(L_SLC)).reshape(B, G, Q_BLOCK, n_sel * L_SLC)
        ks = gather(ks_all, tok)
        vs = gather(vs_all, tok)
        s = jnp.einsum('bqgrd,bgqkd->bgrqk', qb, ks, preferred_element_type=jnp.float32)
        p_s = jax.nn.softmax(jnp.where(tok[:, :, None] <= t[None, None, None, :, None], s, NEG), axis=-1)
        o_s = jnp.einsum('bgrqk,bgqkd->bqgrd', p_s.astype(vs.dtype), vs)
        kw = lax.dynamic_slice_in_dim(kw_pad, bi * Q_BLOCK, WINDOW + Q_BLOCK, axis=1)
        vw = lax.dynamic_slice_in_dim(vw_pad, bi * Q_BLOCK, WINDOW + Q_BLOCK, axis=1)
        spos = bi * Q_BLOCK - WINDOW + jnp.arange(WINDOW + Q_BLOCK)
        dist = t[:, None] - spos[None, :]
        wmask = (dist >= 0) & (dist < WINDOW) & (spos[None, :] >= 0)
        s = jnp.einsum('bqgrd,bsgd->bgrqs', qb, kw, preferred_element_type=jnp.float32)
        p_w = jax.nn.softmax(jnp.where(wmask, s, NEG), axis=-1)
        o_w = jnp.einsum('bgrqs,bsgd->bqgrd', p_w.astype(vw.dtype), vw)
        o = gb[..., 0:1] * o_c + gb[..., 1:2] * o_s + gb[..., 2:3] * o_w
        return o.astype(h.dtype)

    o = lax.map(block, (jnp.arange(nb), q, gates))
    o = o.transpose(1, 0, 2, 3, 4, 5).reshape(B, T, H * d)
    return o @ w_out

def setup_inputs(seed: int = 0) -> dict:
    key = jax.random.key(seed)
    ks = jax.random.split(key, 20)
    f32 = jnp.float32
    ret_in = 2 * RET_HEADS * RET_DK + 2 * RET_HEADS * RET_DV
    nsa_in = NSA_HEADS * NSA_HD + 3 * NSA_HEADS

    def w(k, shape, fan_in):
        return jax.random.normal(k, shape, f32) * (fan_in ** -0.5)

    def gain(k, shape):
        return 1.0 + 0.05 * jax.random.normal(k, shape, f32)

    return {
        'x': jax.random.normal(ks[0], (BATCH, SEQ, D_MODEL), f32),
        'norms': gain(ks[1], (DEPTH, 4, D_MODEL)),
        'ret_w_in': w(ks[2], (N_A, D_MODEL, ret_in), D_MODEL),
        'ret_gn': gain(ks[3], (N_A, RET_HEADS * RET_DV)),
        'ret_w_out': w(ks[4], (N_A, RET_HEADS * RET_DV, D_MODEL), RET_HEADS * RET_DV),
        'nsa_w_in': w(ks[5], (N_B, D_MODEL, nsa_in), D_MODEL),
        'nsa_w_out': w(ks[6], (N_B, NSA_HEADS * NSA_HD, D_MODEL), NSA_HEADS * NSA_HD),
        'kv_norm': gain(ks[7], (D_MODEL,)),
        'w_kv': w(ks[8], (D_MODEL, 6 * NSA_GROUPS * NSA_HD), D_MODEL),
        'cmp_pos_k': 0.1 * jax.random.normal(ks[9], (L_CMP, NSA_HD), f32),
        'cmp_pos_v': 0.1 * jax.random.normal(ks[10], (L_CMP, NSA_HD), f32),
        'cmp_w1_k': w(ks[11], (L_CMP * NSA_HD, CMP_HIDDEN), L_CMP * NSA_HD),
        'cmp_w2_k': w(ks[12], (CMP_HIDDEN, NSA_HD), CMP_HIDDEN),
        'cmp_w1_v': w(ks[13], (L_CMP * NSA_HD, CMP_HIDDEN), L_CMP * NSA_HD),
        'cmp_w2_v': w(ks[14], (CMP_HIDDEN, NSA_HD), CMP_HIDDEN),
        'ffn_w_in': w(ks[15], (DEPTH, D_MODEL, 2 * D_FF), D_MODEL),
        'ffn_w_out': w(ks[16], (DEPTH, D_FF, D_MODEL), D_FF),
    }

def reference(x, norms, ret_w_in, ret_gn, ret_w_out, nsa_w_in, nsa_w_out, kv_norm, w_kv,
              cmp_pos_k, cmp_pos_v, cmp_w1_k, cmp_w2_k, cmp_w1_v, cmp_w2_v, ffn_w_in, ffn_w_out):
    shared = None
    for layer in range(DEPTH):
        h = rmsnorm(x, norms[layer, 0])
        if layer < N_A:
            m = retention(h, ret_w_in[layer], ret_gn[layer], ret_w_out[layer])
        else:
            m = nsa_attention(h, nsa_w_in[layer - N_A], nsa_w_out[layer - N_A], shared)
        x = x + rmsnorm(m, norms[layer, 1])
        f = swiglu(rmsnorm(x, norms[layer, 2]), ffn_w_in[layer], ffn_w_out[layer])
        x = x + rmsnorm(f, norms[layer, 3])
        if layer == N_A - 1:
            shared = nsa_shared_kv(x, kv_norm, w_kv, cmp_pos_k, cmp_pos_v,
                                   cmp_w1_k, cmp_w2_k, cmp_w1_v, cmp_w2_v)
    return x


_drawn_inputs = setup_inputs


def setup_inputs(seed=0):
    import zlib

    import numpy as np

    out = dict(_drawn_inputs(seed))
    spreads = {}
    factors = {'cmp_pos_k': 4.803}
    for name, (base, spread) in spreads.items():
        noise = np.random.default_rng([zlib.crc32(name.encode()), seed]).standard_normal(out[name].shape)
        drawn = base * np.exp(spread * noise) if base else spread * noise
        out[name] = __import__('jax').numpy.asarray(drawn.astype(out[name].dtype))
    for name, factor in factors.items():
        out[name] = (out[name] * factor).astype(out[name].dtype)
    return out
```

```python
from contextlib import ExitStack

import numpy as np

import concourse.bass as bass
from concourse import mybir

F32 = mybir.dt.float32
F32R = mybir.dt.float32r
BF16 = mybir.dt.bfloat16
ALU = mybir.AluOpType
ACT = mybir.ActivationFunctionType
AX = mybir.AxisListType

P = 128
D = 1024
T = 512
TT = T // P
KD = D // P
W = 512
RH, DK, DV = 4, 256, 512
NH, NG, REP, HD = 16, 4, 4, 64
FF = 2816
FJ = FF // 256
KF = FF // P
NCMP = 31
CB = 32
LP = 16
ROT = 8
EPS = 1e-6
NEG = -1e30
RAW = 8
RING = 4

U_RET = 0
U_RO = U_RET + RH * 3 * KD
U_FI = [U_RO + 2 * 16, 0]
U_FO = [U_FI[0] + FJ * KD, 0]
U_KV = U_FO[0] + 2 * KF
U_Q0 = U_KV + 3 * KD
U_CMP = U_Q0 + KD
U_Q1 = U_CMP + LP
U_NO = U_Q1 + KD
U_FI[1] = U_NO + 2 * KD
U_FO[1] = U_FI[1] + FJ * KD
U_END = U_FO[1] + 2 * KF

SET_A, SET_B = 0, 4


def shape_constants():
    f = np.float32
    pos = np.arange(T, dtype=f)
    freqs = (f(1.0) / (f(10000.0) ** np.linspace(0.0, 1.0, DK // 2, dtype=f))).astype(f)
    ang = (pos[:, None] * freqs[None, :]).astype(f)
    ret = np.stack([np.cos(ang).T, np.sin(ang).T], axis=1).astype(f)
    log_g = np.log1p(-np.exp2(-5.0 - np.arange(RH, dtype=np.float64)))
    dist = np.arange(T)[None, :] - np.arange(P)[:, None]
    decay = np.where(dist[:, None, :] >= 0,
                     np.exp(log_g[None, :, None] * np.maximum(dist, 0)[:, None, :]), 0.0)
    decay = (decay * DK ** -0.5).astype(f)
    pf = (f(500000.0) ** (-np.arange(0, 2 * ROT, 2, dtype=f) / f(2 * ROT))).astype(f)
    pang = (pos[:, None] * pf[None, :]).astype(f)
    rope = np.stack([np.cos(pang), np.sin(pang)], axis=0).astype(f)
    rope = rope.reshape(2, TT, P, ROT).transpose(2, 0, 1, 3).reshape(P, 2 * TT * ROT)
    t = np.arange(T)
    end = np.arange(CB) * 16 + 31
    valid = (end[None, :] <= t[:, None]) & (np.arange(CB)[None, :] < NCMP)
    cmask = np.where(valid, 0.0, NEG).astype(f).reshape(TT, P, CB).transpose(1, 0, 2).reshape(P, TT * CB)
    some = valid.any(-1).astype(f).reshape(TT, P).T
    diag = (np.arange(P)[:, None] // CB == np.arange(P // CB)[None, :]).astype(f)
    ident = np.eye(P, dtype=f)
    causal = np.where(np.arange(P)[None, :] > np.arange(P)[:, None], NEG, 0.0).astype(f)
    small = np.concatenate([ident, rope, cmask, some, diag], axis=1)
    return {
        "c_ret": np.ascontiguousarray(ret.reshape(P, 2 * T)),
        "c_decay": np.ascontiguousarray(decay.reshape(P, RH * T)),
        "c_causal": causal,
        "c_small": np.ascontiguousarray(small.astype(f)),
    }


def lay_out_columns(norms, kv_norm, ret_gn, cmp_pos_k, cmp_pos_v):
    rows = [norms[0, 0], norms[0, 2], norms[1, 0], norms[1, 2], kv_norm, ret_gn[0]]
    cols = [r.reshape(-1, P).T for r in rows]
    cols += [p.reshape(LP, P).T for p in (cmp_pos_k, cmp_pos_v)]
    return np.ascontiguousarray(np.concatenate(cols, axis=1))


def yoco_kernel(nc, x, norms, ret_w_in, ret_w_out, nsa_w_in, nsa_w_out, w_kv,
                cmp_w1_k, cmp_w2_k, cmp_w1_v, cmp_w2_v, ffn_w_in, ffn_w_out, feature_columns,
                c_ret, c_decay, c_causal, c_small, out):
    with ExitStack() as ctx:
        def sb(name, shape, dt=F32, stack=ctx):
            return stack.enter_context(nc.sbuf_tensor(name, shape, dt))

        def sem(name):
            return ctx.enter_context(nc.semaphore(name))

        xs = sb("xs", [P, TT, D])
        raw = sb("raw", [P, RAW, W])
        whi = sb("whi", [P, RING, W], F32R)
        wlo = sb("wlo", [P, RING, W], F32R)
        work = sb("work", [P, 8, W])
        gain_row = sb("gain_row", [P, D])
        columns = sb("columns", [P, 5 * KD + 16 + 2 * LP])
        gains = columns[:, 0:5 * KD].rearrange("p (n k) -> p n k", n=5)
        ret_gain = columns[:, 5 * KD:5 * KD + 16]
        pos_sb = columns[:, 5 * KD + 16:].rearrange("p (c l) -> p c l", c=2)
        small = sb("small", [P, c_small.shape[1]])
        ident_b = sb("ident_b", [P, P], BF16)
        causal_b = sb("causal_b", [P, P], BF16)
        sums = sb("sums", [P, 8, TT])
        halves = sb("halves", [P, 4, 2, TT])
        var = sb("var", [P, 8, TT])
        std = sb("std", [P, 8, TT])
        rstd = sb("rstd", [P, 8, TT])
        normed_v = work[:, :, :].rearrange("p (t c) n -> p t (c n)", t=TT)
        at = 0
        ident = small[:, 0:P]
        at = P
        rope_tab = small[:, at:at + 2 * TT * ROT].rearrange("p (f t e) -> p f t e", f=2, t=TT)
        at += 2 * TT * ROT
        cmask = small[:, at:at + TT * CB].rearrange("p (t n) -> p t n", t=TT)
        at += TT * CB
        some = small[:, at:at + TT]
        at += TT
        diag4 = small[:, at:at + 4]

        with ExitStack() as s:
            hT_r = sb("hT_r", [P, 2, KD, T], F32R, s)
            qk_r = sb("qk_r", [P, 2, 2, 2, T], F32R, s)
            v_r = sb("v_r", [P, 2, TT, W], F32R, s)
            y = sb("y", [P, TT, RH * DV], F32, s)
            dec_r = sb("dec_r", [P, 2, 1280], F32R, s)
            rot_tab = sb("rot_tab", [P, 2, T], F32, s)
            decay = sb("decay", [P, RH * T], F32, s)
            gate_r = sb("gate_r", [P, TT, W], F32, s)
            causal = y[:, 0, 0:P]
            bn = sb("bn", [P, TT, 6], F32, s)
            mv = sb("mv", [P, TT, 2], F32, s)
            gvar = sb("gvar", [P, 3, TT], F32, s)
        with ExitStack() as s:
            yT = sb("yT", [P, 2, 16, T], F32R, s)
        with ExitStack() as s:
            hT_f = sb("hT_f", [P, 2, KD, T], F32R, s)
            aT = sb("aT", [P, 2, KF, T], F32R, s)
        with ExitStack() as s:
            kvT = sb("kvT", [P, 2, KD, T], F32R, s)
            hT_n = sb("hT_n", [P, 2, KD, T], F32R, s)
            kT2 = sb("kT2", [P, 2, NG, 2, T], F32R, s)
            v_all = sb("v_all", [P, 2, TT, NG * HD], F32, s)
            cv_bd = sb("cv_bd", [P, NG, REP, HD], F32, s)
            ck2 = sb("ck2", [P, 2, NG, CB], F32R, s)
            w2k = sb("w2k", [P, 2, 2, HD], F32, s)
            w2v = sb("w2v", [P, 2, HD], F32, s)
            gates = sb("gates", [P, TT, NH, 3], F32, s)
            nmax = sb("nmax", [P, 128], F32, s)
            lsum = sb("lsum", [P, 128], F32, s)
            linv = sb("linv", [P, 128], F32, s)
            cst = sb("cst", [P, 4, TT, NH], F32, s)
            with ExitStack() as s2:
                cT = sb("cT", [P, 8, T], F32, s2)
            with ExitStack() as s2:
                qs = sb("qs", [P, TT, 8, 2, HD], F32R, s2)
            with ExitStack() as s2:
                prob = sb("prob", [P, 4, W], F32, s2)
                probT = sb("probT", [P, 4, W], F32, s2)
            blank = s.enter_context(nc.sbuf_tensor("over_cT", [P, 8 * T], F32))
            rope_t = sb("rope_t", [P, 4, TT * 8 * ROT], F32, s)
            otmp = rope_t[:, 0:2, :]
            gwhi = sb("gwhi", [P, KD, 48], F32R, s)
            gwlo = sb("gwlo", [P, KD, 48], F32R, s)
        with ExitStack() as s:
            kd = sb("kd", [P, 2, TT, NG, 2, 2 * HD], F32R, s)
        with ExitStack() as s:
            qT2 = sb("qT2", [P, NH, T], F32R, s)
            oT = sb("oT", [P, 2, KD, T], F32R, s)
            bT = sb("bT", [P, 2, 2, LP, 124], F32R, s)
        gw = gain_row[:, 0:KD * 48].rearrange("p (k n) -> p k n", k=KD)
        hid_k = work[:, 4, 0:248].rearrange("p (h n) -> p h n", h=2)
        hid_v = work[:, 4, 256:504].rearrange("p (h n) -> p h n", h=2)
        hid_rep = work[:, 5:7, :].rearrange("p h (g r n) -> p h g r n", g=NG, r=REP)
        v_tok0 = work[:, 0:4, :]
        k_tok = work[:, 4:8, :].rearrange("p (c a) (b n) -> p c (a b) n", c=2, b=2)
        q_tok = work[:, :, :].rearrange("p (j t) n -> p j t n", j=2)
        o_acc = normed_v
        ps = ctx.enter_context(nc.psum_tensor("ps", [P, 8, W], F32))

        names = """x_in consts_in gain_in nsa_in w_hi w_lo w_used
            norm_sq norm_var norm_std norm_rstd normed hT_psum hT_hi hT_lo
            post_sq post_sum post_var post_std post_rstd post_mul x_ready masks
            rot_prod rot_sum qk_hi qk_lo v_hi v_lo s_full s_dec s_hi s_lo
            g_silu o_full o_bn o_mv o_var o_std o_rstd o_cent y_done yT_psum yT_hi yT_lo
            ff_silu ff_a ff_hi ff_lo
            kv_v kv_k rope_prod rope_done kd_hi kd_lo gw_hi gw_lo gate_full gate_done
            tp_full tp_act tp_dve shifted b_hi b_lo q_copied qs_hi qs_lo
            hid_done rep_zero rep_done ck_full ck_hi ck_lo cv_full cv_done
            cs_full cs_masked cs_max cs_sub cs_exp cs_sum cs_inv cs_some cs_coef cs_tp cs_pT cs_pv o_cmp
            sc_full max_done exp_done pt_full pt_act pt_dve pv_done l_inv a_coef a_scaled a_pair o_added
            oT_psum oT_hi oT_lo stored""".split()
        S = {n: sem(n) for n in names}
        raw_in = [sem(f"raw_in{i}") for i in range(RAW)]

        block = ctx.enter_context(nc.Block())

        def plus(c, it, per):
            return c if it is None else c + it * per

        @block.sync
        def _(sp):
            def load(u, src, it=None, per=0, cols=1):
                if u >= RAW or it is not None:
                    sp.wait_ge(S["w_lo"], plus(u - RAW + 1, it, per))
                dst = raw[:, u % RAW, :]
                if cols > 1:
                    dst = dst.rearrange("p (c n) -> p c n", c=cols)
                sp.dma_start(dst, src).then_inc(raw_in[u % RAW], 16)

            ret = ret_w_in[0].rearrange("(k p) n -> p k n", p=P)
            ret_qk = ret[:, :, 0:2 * RH * DK].rearrange("p k (c n) -> p k c n", c=2)

            def head_loads(h, it):
                for k in range(KD):
                    load(k, ret_qk[:, k, :, bass.ds(h * DK, DK)], it, 24, cols=2)
                for part in range(2):
                    col = 2 * RH * DK + part * RH * DV
                    for k in range(KD):
                        load(KD * (part + 1) + k, ret[:, k, bass.ds(h * DV + col, DV)], it, 24)

            for t in range(TT):
                sp.dma_start(xs[:, t, :], x[0, t * P:(t + 1) * P, :]).then_inc(S["x_in"], 16)
            head_loads(0, None)
            with sp.Fori(1, RH) as h:
                head_loads(h, h)

            def out_loads(u0, w, tiles):
                v = w.rearrange("(k p) n -> p k n", p=P)
                for half in range(2):
                    for k in range(tiles):
                        load(u0 + half * tiles + k, v[:, k, half * W:(half + 1) * W])

            out_loads(U_RO, ret_w_out[0], 16)

            def ffn_loads(layer):
                v = ffn_w_in[layer].rearrange("(k p) (c n) -> p k c n", p=P, c=2)
                u0 = U_FI[layer]
                with sp.Fori(0, FJ) as b:
                    for k in range(KD):
                        load(u0 + k, v[:, k, :, bass.ds(b * 256, 256)], b, KD, cols=2)
                out_loads(U_FO[layer], ffn_w_out[layer], KF)

            ffn_loads(0)
            kv = w_kv.rearrange("(k p) n -> p k n", p=P)
            for c in range(3):
                for k in range(KD):
                    load(U_KV + c * KD + k, kv[:, k, c * W:(c + 1) * W])
            wq = nsa_w_in[0].rearrange("(k p) n -> p k n", p=P)
            for k in range(KD):
                load(U_Q0 + k, wq[:, k, 0:W])
            for kv_i, w1 in enumerate((cmp_w1_k, cmp_w1_v)):
                v = w1.rearrange("(k p) n -> p k n", p=P)
                for k in range(LP // 2):
                    load(U_CMP + kv_i * 8 + k, v[:, 2 * k:2 * k + 2, :], cols=2)
            for k in range(KD):
                load(U_Q1 + k, wq[:, k, W:2 * W])
            out_loads(U_NO, nsa_w_out[0], KD)
            ffn_loads(1)
            for t in range(TT):
                sp.wait_ge(S["x_ready"], 12 + t + 1)
                sp.dma_start(out[0, t * P:(t + 1) * P, :], xs[:, t, :]).then_inc(S["stored"], 16)
            sp.wait_ge(S["stored"], 64)

        NCONST = 5

        @block.gpsimd
        def _(pool):
            def gain_load(i):
                layer, n = i // 2, 1 + 2 * (i % 2)
                pool.dma_start(gain_row[:], norms[layer, n:n + 1, :].broadcast_to([P, D])).then_inc(S["gain_in"], 16)

            def add_residual(i):
                for t in range(TT):
                    pool.wait_ge(S["post_mul"], 8 * i + 2 * t + 2)
                    nc.gpsimd.tensor_tensor(xs[:, t, :], xs[:, t, :], normed_v[:, t, :], ALU.add
                                            ).then_inc(S["x_ready"], 1)
                if i in (0, 2):
                    gain_load(i + 1)

            gain_load(0)
            with pool.Fori(0, RH) as h:
                for t in range(TT):
                    pool.wait_ge(S["g_silu"], h * 4 + (t + 1))
                    pool.wait_ge(S["o_cent"], h * 4 + (t + 1))
                    nc.gpsimd.tensor_tensor(y[:, t, bass.ds(h * DV, DV)], work[:, 4 + t, :], gate_r[:, t, :],
                                            ALU.mult).then_inc(S["y_done"], 1)
            add_residual(0)
            add_residual(1)
            pool.wait_ge(S["normed"], 12)
            for dup in range(2):
                pool.dma_start(w2k[:, :, dup, :], cmp_w2_k.rearrange("(h p) d -> p h d", p=P)
                               ).then_inc(S["nsa_in"], 16)
            pool.dma_start(w2v[:, :, :], cmp_w2_v.rearrange("(h p) d -> p h d", p=P)).then_inc(S["nsa_in"], 16)
            pool.dma_start(gw[:], nsa_w_in[0].rearrange("(k p) n -> p k n", p=P)[:, :, NH * HD:NH * HD + 48]
                           ).then_inc(S["nsa_in"], 16)
            pool.wait_ge(S["tp_act"], 4)
            pool.wait_ge(S["tp_dve"], 4)
            pool.dma_start(cT[HD:P, :, 0:T - 1], cT[0:HD, :, 1:T]).then_inc(S["shifted"], 16)
            pool.wait_ge(S["gw_lo"], 1)
            gain_load(2)
            pool.wait_ge(S["kd_lo"], 8)
            nc.gpsimd.memset(hid_rep[:], 0.0).then_inc(S["rep_zero"], 1)
            for ig in range(TT * NG):
                i, g = divmod(ig, NG)
                o = o_acc[:, i, g * 256:(g + 1) * 256]
                pool.wait_ge(S["a_scaled"], ig + 1)
                pool.wait_ge(S["o_cmp"], 2 * (i + 1))
                nc.gpsimd.tensor_tensor(otmp[:, 0, :], otmp[:, 0, :], otmp[:, 1, :], ALU.add
                                        ).then_inc(S["a_pair"], 1)
                pool.wait_ge(S["a_pair"], ig + 1)
                nc.gpsimd.tensor_tensor(o, o, otmp[:, 0, :], ALU.add).then_inc(S["o_added"], 1)
            add_residual(2)
            add_residual(3)

        @block.scalar
        def _(act):
            A = nc.scalar.activation

            def hi(u, it=None, per=0):
                act.wait_ge(raw_in[u % RAW], plus(16 * (u // RAW + 1), it, 16 * (per // RAW)))
                if u >= RING:
                    act.wait_ge(S["w_used"], plus(u - 3, it, per))
                A(whi[:, u % RING, :], raw[:, u % RAW, :], ACT.Copy).then_inc(S["w_hi"], 1)

            def root(j):
                act.wait_ge(S["norm_var"], j + 1)
                A(std[:, j, :], var[:, j, :], ACT.Sqrt).then_inc(S["norm_std"], 1)

            def pre_norm(j, dests):
                for t in range(TT):
                    if j == 0:
                        act.wait_ge(S["x_in"], 64)
                    else:
                        act.wait_ge(S["x_ready"], 4 * (j - 1) + t + 1)
                    A(normed_v[:, t, :], xs[:, t, :], ACT.Square, accum_out=sums[:, j, t:t + 1]
                      ).then_inc(S["norm_sq"], 1)
                root(j)
                if j == 0:
                    act.wait_ge(S["consts_in"], 16 * NCONST)
                for k in range(KD):
                    act.wait_ge(S["hT_psum"], 8 * j + k + 1)
                    for dst, gain in dests:
                        ins = A(dst[:, 0, k, :], ps[:, SET_B + k % 4, :], ACT.Copy,
                                scale=gains[:, gain, k:k + 1])
                    ins.then_inc(S["hT_hi"], 1)

            def half_squares(i, u_end, half, bank):
                act.wait_ge(S["w_used"], u_end)
                for t in range(TT):
                    A(normed_v[:, t, half * W:(half + 1) * W], ps[:, bank + t, :], ACT.Square,
                      accum_out=halves[:, i, half, t:t + 1]).then_inc(S["post_sq"], 1)

            def post_root(i):
                act.wait_ge(S["post_var"], i + 1)
                A(std[:, 4 + i, :], var[:, 4 + i, :], ACT.Sqrt).then_inc(S["post_std"], 1)

            def out_phase(i, u0, tiles, banks, before=None):
                for n in range(4, 2 * tiles):
                    hi(u0 + n)
                    if before is not None and n - 4 + 4 < tiles:
                        before(n - 4 + 4)
                    if n == tiles + 3:
                        half_squares(i, u0 + tiles, 0, banks[0])
                half_squares(i, u0 + 2 * tiles, 1, banks[1])
                post_root(i)
                if i < 3:
                    for n in range(4):
                        hi(u0 + 2 * tiles + n)

            act.dma_start(small[:], c_small).then_inc(S["consts_in"], 16)
            act.dma_start(rot_tab[:].rearrange("p a b -> p (a b)"), c_ret).then_inc(S["consts_in"], 16)
            act.dma_start(causal, c_causal).then_inc(S["consts_in"], 16)
            act.dma_start(decay[:], c_decay).then_inc(S["consts_in"], 16)
            act.dma_start(columns[:], feature_columns).then_inc(S["consts_in"], 16)
            for u in range(4):
                hi(u)
            pre_norm(0, [(hT_r, 0)])

            with act.Fori(0, 2) as it:
                for p in range(2):
                    u0 = 24 * p
                    xb, yb = (SET_A, SET_B) if p == 0 else (SET_B, SET_A)

                    def n4(c):
                        return it * 8 + (4 * p + c)
                    for n in range(4, 12):
                        hi(u0 + n, it, 48)
                    for m in range(4):
                        act.wait_ge(S["rot_sum"], n4(m + 1))
                        A(qk_r[:, 0, m // 2, m % 2, :], work[:, 4 * (m // 2) + 2 * (m % 2), :], ACT.Copy
                          ).then_inc(S["qk_hi"], 1)
                    for n in range(12, 20):
                        hi(u0 + n, it, 48)
                    act.wait_ge(S["w_used"], it * 48 + (u0 + 16))
                    for t in range(TT):
                        A(v_r[:, 0, t, :], ps[:, yb + t, :], ACT.Copy).then_inc(S["v_hi"], 1)
                    at_col = 0
                    for j in range(TT):
                        w = T - j * P
                        act.wait_ge(S["s_dec"], n4(j + 1))
                        A(dec_r[:, 0, at_col:at_col + w], work[:, j, 0:w], ACT.Copy).then_inc(S["s_hi"], 1)
                        at_col += w
                    for n in range(20, 28):
                        hi(u0 + n, it, 48)
                    act.wait_ge(S["w_used"], it * 48 + (u0 + 24))
                    if p == 1:
                        act.wait_ge(S["y_done"], n4(0))
                    for t in range(TT):
                        A(gate_r[:, t, :], ps[:, yb + t, :], ACT.Silu).then_inc(S["g_silu"], 1)
                    act.wait_ge(S["o_var"], it * 2 + (p + 1))
                    A(gvar[:, 1, :], gvar[:, 0, :], ACT.Sqrt).then_inc(S["o_std"], 1)
                act.wait_ge(S["y_done"], it * 8 + 8)

            def yT_hi(k):
                act.wait_ge(S["yT_psum"], k + 1)
                A(yT[:, 0, k, :], ps[:, SET_B + k % 4, :], ACT.Copy, scale=ret_gain[:, k:k + 1]
                  ).then_inc(S["yT_hi"], 1)

            for k in range(4):
                yT_hi(k)
            out_phase(0, U_RO, 16, (SET_A, SET_B), yT_hi)

            def ffn(layer):
                pre_norm(1 + 2 * layer, [(hT_f, 1 + 2 * layer)])
                f0 = FJ * layer
                u0 = U_FI[layer]

                def job(b, par, first=False, it=None):
                    bank = SET_A if par % 2 == 0 else SET_B
                    q = par % 2
                    for n in range(4, 12):
                        hi(u0 + 8 * b + n, it, 16)
                    act.wait_ge(S["w_used"], plus(u0 + 8 * b + 8, it, 16))
                    if not first:
                        act.wait_ge(S["ff_a"], plus(2 * (f0 + b - 1), it, 4))
                    for f in range(2):
                        A(work[:, 2 * q + f, :], ps[:, bank + f, :], ACT.Silu).then_inc(S["ff_silu"], 1)
                    for f in range(2):
                        act.wait_ge(S["ff_a"], plus(2 * (f0 + b) + f + 1, it, 4))
                        if it is None:
                            dst = aT[:, 0, 2 * b + f, :]
                        else:
                            dst = aT[:, 0, bass.ds(it * 4 + (2 * b + f), 1), :]
                        A(dst, work[:, 4 + 2 * q + f, :] if it is None else work[:, 4 + 2 * q + f:5 + 2 * q + f, :],
                          ACT.Copy).then_inc(S["ff_hi"], 1)
                job(0, 0, True)
                job(1, 1, True)
                with act.Fori(0, 4) as it:
                    job(2, 0, it=it)
                    job(3, 1, it=it)
                job(10, 0)
                out_phase(1 + 2 * layer, U_FO[layer], KF, (SET_B, SET_A))

            ffn(0)

            pre_norm(2, [(kvT, 4), (hT_n, 2)])

            def v_copies(c):
                bank = (SET_A, SET_B, SET_A)[c]
                act.wait_ge(S["w_used"], U_KV + KD * (c + 1))
                for t in range(TT):
                    dst = v_tok0[:, t, 256:512] if c == 0 else v_all[:, c - 1, t, :]
                    A(dst, ps[:, bank + t, 256:512], ACT.Copy).then_inc(S["kv_v"], 1)

            def tp_dst(m):
                if m < 8:
                    return cT[0:HD, m, :], HD
                if m < 24:
                    c, g, part = (m - 8) // 8, (m - 8) % 8 // 2, m % 2
                    return kT2[:, c, g, part, :], P
                return qT2[:, m - 24, :], P

            def tp_items(lo_m, hi_m):
                for m in range(lo_m, hi_m):
                    if m % 2 == 1:
                        dst, n = tp_dst(m)
                        act.wait_ge(S["tp_full"], m + 1)
                        A(dst, ps[0:n, (SET_A if m < 8 else SET_B) + m % 4, :], ACT.Copy).then_inc(S["tp_act"], 1)

            for n in range(4, 12):
                hi(U_KV + n)
            v_copies(0)
            for n in range(12, 16):
                hi(U_KV + n)
            for n in range(16, 20):
                hi(U_KV + n)
            v_copies(1)
            tp_items(0, 8)
            act.wait_ge(S["nsa_in"], 16 * 4)
            A(gwhi[:], gw[:], ACT.Copy).then_inc(S["gw_hi"], 1)
            for n in range(20, 28):
                hi(U_KV + n)
            v_copies(2)
            act.wait_ge(S["shifted"], 16)
            for n in range(8):
                hi(U_Q0 + 4 + n)
                for m in range(4 * n, 4 * n + 4):
                    kv_i, lp = divmod(m, LP)
                    A(bT[:, 0, kv_i, lp, :].rearrange("p (g n) -> p g n", g=NG),
                      cT[:, kv_i * 4:kv_i * 4 + 4, 2 * lp:2 * lp + 481:16], ACT.Identity,
                      bias=pos_sb[:, kv_i, lp:lp + 1]).then_inc(S["b_hi"], 1)

            def q_copies(j, bank):
                act.wait_ge(S["w_used"], (U_Q0, U_Q1)[j] + KD)
                for t in range(TT):
                    A(q_tok[:, j, t, :], ps[:, bank + t, :], ACT.Copy, scale=HD ** -0.5).then_inc(S["q_copied"], 1)

            def qs_hi(j):
                act.wait_ge(S["rope_done"], 2 * (4 + j))
                for t in range(TT):
                    A(qs[:, t, :, 0, :], q_tok[:, j, t, :].rearrange("p (h d) -> p h d", h=8), ACT.Copy
                      ).then_inc(S["qs_hi"], 1)

            q_copies(0, SET_B)
            act.wait_ge(S["gate_full"], 1)
            A(gates[:].rearrange("p t h c -> p (t h c)"), ps[:, SET_A, 0:192], ACT.Sigmoid
              ).then_inc(S["gate_done"], 1)
            for n in range(16):
                hi(U_CMP + 4 + n)
                if n < 8:
                    c, t = divmod(n, TT)
                    act.wait_ge(S["rope_done"], 2 * (c + 2))
                    A(kd[:, c, t, :, 0, :].rearrange("p g (u d) -> p g u d", u=2),
                      k_tok[:, c, t, :].rearrange("p (g d) -> p g d", g=NG).unsqueeze(2)
                      .broadcast_to([P, NG, 2, HD]), ACT.Copy).then_inc(S["kd_hi"], 1)
                if n == 8:
                    qs_hi(0)
            act.wait_ge(S["w_used"], U_CMP + LP)
            act.wait_ge(S["rep_zero"], 1)
            for kv_i, dst in ((0, hid_k), (1, hid_v)):
                for ht in range(2):
                    A(dst[:, ht, :], ps[:, SET_A + kv_i * 2 + ht, 0:124], ACT.Gelu_apprx_tanh
                      ).then_inc(S["hid_done"], 1)
            tp_items(8, 24)
            act.wait_ge(S["ck_full"], 1)
            A(ck2[:, 0, :, 0:NCMP], ps[:, SET_A, 0:124].rearrange("p (g n) -> p g n", g=NG), ACT.Copy
              ).then_inc(S["ck_hi"], 1)
            for n in range(8):
                hi(U_Q1 + 4 + n)
            q_copies(1, SET_A)
            tp_items(24, 32)
            qs_hi_wait = 32
            act.wait_ge(S["tp_full"], qs_hi_wait)
            qs_hi(1)
            tp_items(32, 40)
            for i in range(TT):
                act.wait_ge(S["cs_sub"], i + 1)
                A(prob[:, i, :], prob[:, i, :], ACT.Exp).then_inc(S["cs_exp"], 1)
            for i in range(TT):
                act.wait_ge(S["cs_tp"], i + 1)
                A(probT[:, i, :], ps[:, 4 + i % 2, :], ACT.Copy).then_inc(S["cs_pT"], 1)

            def p_copy(n):
                w = (n // 32 + 1) * P
                act.wait_ge(S["pt_full"], n + 1)
                if n >= 4:
                    act.wait_ge(S["pv_done"], n - 3)
                A(probT[:, n % 4, 0:w], ps[:, 5, 0:w], ACT.Copy).then_inc(S["pt_act"], 1)

            for s in range(64):
                w = (s // 16 + 1) * P
                act.wait_ge(S["max_done"], s + 1)
                for n in (2 * s, 2 * s + 1):
                    if n < 4:
                        act.wait_ge(S["cs_tp"], TT)
                    else:
                        act.wait_ge(S["pt_full"], n - 3)
                    A(prob[:, n % 4, 0:w], ps[:, 2 * (s % 2) + n % 2, 0:w], ACT.Exp, bias=nmax[:, n:n + 1],
                      accum_out=lsum[:, n:n + 1]).then_inc(S["exp_done"], 1)
                if s >= 1:
                    p_copy(2 * s - 1)
            p_copy(127)

            def oT_hi(k):
                act.wait_ge(S["oT_psum"], k + 1)
                A(oT[:, 0, k, :], ps[:, SET_B + k % 4, :], ACT.Copy).then_inc(S["oT_hi"], 1)

            for k in range(4):
                oT_hi(k)
            out_phase(2, U_NO, KD, (SET_A, SET_B), oT_hi)
            ffn(1)

        @block.vector
        def _(dve):
            V = nc.vector

            def lo(u, it=None, per=0):
                dve.wait_ge(S["w_hi"], plus(u + 1, it, per))
                V.tensor_tensor(wlo[:, u % RING, :], raw[:, u % RAW, :], whi[:, u % RING, :].bitcast(F32),
                                ALU.subtract).then_inc(S["w_lo"], 1)

            def pre_norm(j, dests, splits):
                dve.wait_ge(S["norm_sq"], 4 * (j + 1))
                V.tensor_scalar(var[:, j, :], sums[:, j, :], 1.0 / D, EPS, ALU.mult, ALU.add
                                ).then_inc(S["norm_var"], 1)
                dve.wait_ge(S["norm_std"], j + 1)
                V.reciprocal(rstd[:, j, :], std[:, j, :]).then_inc(S["norm_rstd"], 1)
                dve.wait_ge(S["norm_rstd"], j + 1)
                for t in range(TT):
                    V.tensor_scalar(normed_v[:, t, :], xs[:, t, :], rstd[:, j, t:t + 1], None, ALU.mult
                                    ).then_inc(S["normed"], 1)
                for u in splits:
                    lo(u)
                for k in range(KD):
                    dve.wait_ge(S["hT_hi"], 8 * j + k + 1)
                    for dst, gain in dests:
                        ins = V.scalar_tensor_tensor(
                            out=dst[:, 1, k, :], in0=ps[:, SET_B + k % 4, :], scalar=gains[:, gain, k:k + 1],
                            in1=dst[:, 0, k, :].bitcast(F32), op0=ALU.mult, op1=ALU.subtract)
                    ins.then_inc(S["hT_lo"], 1)

            def post_norm(i, banks):
                dve.wait_ge(S["post_sq"], 8 * (i + 1))
                V.tensor_tensor(sums[:, 4 + i, :], halves[:, i, 0, :], halves[:, i, 1, :], ALU.add
                                ).then_inc(S["post_sum"], 1)
                dve.wait_ge(S["post_sum"], i + 1)
                V.tensor_scalar(var[:, 4 + i, :], sums[:, 4 + i, :], 1.0 / D, EPS, ALU.mult, ALU.add
                                ).then_inc(S["post_var"], 1)
                dve.wait_ge(S["post_std"], i + 1)
                V.reciprocal(rstd[:, 4 + i, :], std[:, 4 + i, :]).then_inc(S["post_rstd"], 1)
                dve.wait_ge(S["post_rstd"], i + 1)
                dve.wait_ge(S["gain_in"], 16 * (i + 1))
                for t in range(TT):
                    for half in range(2):
                        V.scalar_tensor_tensor(
                            out=normed_v[:, t, half * W:(half + 1) * W], in0=ps[:, banks[half] + t, :],
                            scalar=rstd[:, 4 + i, t:t + 1], in1=gain_row[:, half * W:(half + 1) * W],
                            op0=ALU.mult, op1=ALU.mult).then_inc(S["post_mul"], 1)

            def out_phase(i, u0, tiles, banks, before=None):
                for n in range(4, 2 * tiles):
                    lo(u0 + n)
                    if before is not None and n < tiles:
                        before(n)
                post_norm(i, banks)

            for u in range(4):
                lo(u)
            dve.wait_ge(S["consts_in"], 16 * NCONST)
            V.tensor_copy(ident_b[:], ident).then_inc(S["masks"], 1)
            V.tensor_copy(causal_b[:], causal).then_inc(S["masks"], 1)
            pre_norm(0, [(hT_r, 0)], [])

            with dve.Fori(0, 2) as it:
                for p in range(2):
                    u0 = 24 * p
                    xb, yb = (SET_A, SET_B) if p == 0 else (SET_B, SET_A)

                    def n4(c):
                        return it * 8 + (4 * p + c)

                    def n1(c=1):
                        return it * 2 + (p + c)
                    for n in range(4, 12):
                        lo(u0 + n, it, 48)
                    dve.wait_ge(S["w_used"], it * 48 + (u0 + 8))
                    if p == 1:
                        dve.wait_ge(S["y_done"], n4(0))
                    for m in range(2):
                        a, b = ps[:, xb + 2 * m, :], ps[:, xb + 2 * m + 1, :]
                        for n, (src, f) in enumerate(((a, 0), (b, 1), (a, 1), (b, 0))):
                            V.tensor_tensor(work[:, 4 * m + n, :], src, rot_tab[:, f, :], ALU.mult
                                            ).then_inc(S["rot_prod"], 1)
                        dve.wait_ge(S["rot_prod"], it * 16 + (8 * p + 4 * m + 4))
                        V.tensor_tensor(work[:, 4 * m, :], work[:, 4 * m, :], work[:, 4 * m + 1, :], ALU.subtract
                                        ).then_inc(S["rot_sum"], 1)
                        V.tensor_tensor(work[:, 4 * m + 2, :], work[:, 4 * m + 2, :], work[:, 4 * m + 3, :],
                                        ALU.add).then_inc(S["rot_sum"], 1)
                    for m in range(4):
                        dve.wait_ge(S["qk_hi"], n4(m + 1))
                        V.tensor_tensor(qk_r[:, 1, m // 2, m % 2, :], work[:, 4 * (m // 2) + 2 * (m % 2), :],
                                        qk_r[:, 0, m // 2, m % 2, :].bitcast(F32), ALU.subtract
                                        ).then_inc(S["qk_lo"], 1)
                    for n in range(12, 20):
                        lo(u0 + n, it, 48)
                    for t in range(TT):
                        dve.wait_ge(S["v_hi"], n4(t + 1))
                        V.tensor_tensor(v_r[:, 1, t, :], ps[:, yb + t, :], v_r[:, 0, t, :].bitcast(F32),
                                        ALU.subtract).then_inc(S["v_lo"], 1)
                    dve.wait_ge(S["s_full"], n1())
                    for j in range(TT):
                        w = T - j * P
                        V.tensor_tensor(work[:, j, 0:w], ps[:, xb + j, 0:w],
                                        decay[:, bass.ds(it * 2 * T + p * T, w)], ALU.mult
                                        ).then_inc(S["s_dec"], 1)
                    at_col = 0
                    for j in range(TT):
                        w = T - j * P
                        dve.wait_ge(S["s_hi"], n4(j + 1))
                        V.tensor_tensor(dec_r[:, 1, at_col:at_col + w], work[:, j, 0:w],
                                        dec_r[:, 0, at_col:at_col + w].bitcast(F32), ALU.subtract
                                        ).then_inc(S["s_lo"], 1)
                        at_col += w
                    for n in range(20, 28):
                        lo(u0 + n, it, 48)
                    dve.wait_ge(S["o_full"], n1())
                    for t in range(TT):
                        V.bn_stats(bn[:, t, :], ps[:, xb + t, :]).then_inc(S["o_bn"], 1)
                    for t in range(TT):
                        dve.wait_ge(S["o_bn"], n4(t + 1))
                        dve.nop(nofuse=True)
                        V.bn_aggr(mv[:, t, :], bn[:, t, :]).then_inc(S["o_mv"], 1)
                    dve.wait_ge(S["o_mv"], n4(TT))
                    V.tensor_scalar(gvar[:, 0, :], mv[:, :, 1], EPS, None, ALU.add).then_inc(S["o_var"], 1)
                    dve.wait_ge(S["o_std"], n1())
                    V.reciprocal(gvar[:, 2, :], gvar[:, 1, :]).then_inc(S["o_rstd"], 1)
                    dve.wait_ge(S["o_rstd"], n1())
                    for t in range(TT):
                        V.tensor_scalar(work[:, 4 + t, :], ps[:, xb + t, :], mv[:, t, 0:1], gvar[:, 2, t:t + 1],
                                        ALU.subtract, ALU.mult).then_inc(S["o_cent"], 1)
                dve.wait_ge(S["y_done"], it * 8 + 8)

            def yT_lo(k):
                dve.wait_ge(S["yT_hi"], k + 1)
                V.scalar_tensor_tensor(out=yT[:, 1, k, :], in0=ps[:, SET_B + k % 4, :],
                                       scalar=ret_gain[:, k:k + 1], in1=yT[:, 0, k, :].bitcast(F32),
                                       op0=ALU.mult, op1=ALU.subtract).then_inc(S["yT_lo"], 1)

            for k in range(4):
                yT_lo(k)
            out_phase(0, U_RO, 16, (SET_A, SET_B), yT_lo)

            def ffn(layer):
                u0 = U_FI[layer]
                pre_norm(1 + 2 * layer, [(hT_f, 1 + 2 * layer)], range(u0, u0 + 4))
                f0 = FJ * layer

                def job(b, par, it=None):
                    bank = SET_A if par % 2 == 0 else SET_B
                    q = par % 2
                    for n in range(4, 12):
                        lo(u0 + 8 * b + n, it, 16)
                    for f in range(2):
                        dve.wait_ge(S["ff_silu"], plus(2 * (f0 + b) + f + 1, it, 4))
                        V.tensor_tensor(work[:, 4 + 2 * q + f, :], ps[:, bank + 2 + f, :], work[:, 2 * q + f, :],
                                        ALU.mult).then_inc(S["ff_a"], 1)
                    for f in range(2):
                        dve.wait_ge(S["ff_hi"], plus(2 * (f0 + b) + f + 1, it, 4))
                        if it is None:
                            a_hi, a_lo, src = aT[:, 0, 2 * b + f, :], aT[:, 1, 2 * b + f, :], work[:, 4 + 2 * q + f, :]
                        else:
                            k = bass.ds(it * 4 + (2 * b + f), 1)
                            a_hi, a_lo, src = aT[:, 0, k, :], aT[:, 1, k, :], work[:, 4 + 2 * q + f:5 + 2 * q + f, :]
                        V.tensor_tensor(a_lo, src, a_hi.bitcast(F32), ALU.subtract).then_inc(S["ff_lo"], 1)
                job(0, 0)
                job(1, 1)
                with dve.Fori(0, 4) as it:
                    job(2, 0, it)
                    job(3, 1, it)
                job(10, 0)
                out_phase(1 + 2 * layer, U_FO[layer], KF, (SET_B, SET_A))

            ffn(0)
            pre_norm(2, [(kvT, 4), (hT_n, 2)], range(U_KV, U_KV + 4))

            def rope(buf, heads, r):
                v = buf.rearrange("p t (h d) -> p t h d", d=HD)
                a, b = v[:, :, :, 0:ROT], v[:, :, :, ROT:2 * ROT]
                cos = rope_tab[:, 0].unsqueeze(2).broadcast_to([P, TT, heads, ROT])
                sin = rope_tab[:, 1].unsqueeze(2).broadcast_to([P, TT, heads, ROT])
                t = [rope_t[:, n, 0:TT * heads * ROT].rearrange("p (t h e) -> p t h e", t=TT, h=heads)
                     for n in range(4)]
                for n, (src, f) in enumerate(((a, cos), (b, sin), (a, sin), (b, cos))):
                    V.tensor_tensor(t[n], src, f, ALU.mult).then_inc(S["rope_prod"], 1)
                dve.wait_ge(S["rope_prod"], 4 * (r + 1))
                V.tensor_tensor(a, t[0], t[1], ALU.subtract).then_inc(S["rope_done"], 1)
                V.tensor_tensor(b, t[2], t[3], ALU.add).then_inc(S["rope_done"], 1)

            def kv_job(c):
                bank = (SET_A, SET_B, SET_A)[c]
                dst = v_tok0[:, :, 0:256] if c == 0 else k_tok[:, c - 1]
                for t in range(TT):
                    dve.wait_ge(S["kv_v"], 4 * c + t + 1)
                    V.tensor_copy(dst[:, t, :], ps[:, bank + t, 0:256]).then_inc(S["kv_k"], 1)
                dve.wait_ge(S["kv_k"], 4 * (c + 1))
                rope(dst, NG, c)

            def tp_items(lo_m, hi_m):
                for m in range(lo_m, hi_m):
                    if m % 2 == 0:
                        if m < 8:
                            dst, n = cT[0:HD, m, :], HD
                        elif m < 24:
                            dst, n = kT2[:, (m - 8) // 8, (m - 8) % 8 // 2, 0, :], P
                        else:
                            dst, n = qT2[:, m - 24, :], P
                        dve.wait_ge(S["tp_full"], m + 1)
                        V.tensor_copy(dst, ps[0:n, (SET_A if m < 8 else SET_B) + m % 4, :]).then_inc(S["tp_dve"], 1)

            for n in range(4, 12):
                lo(U_KV + n)
            kv_job(0)
            for n in range(12, 20):
                lo(U_KV + n)
            kv_job(1)
            tp_items(0, 8)
            dve.wait_ge(S["gw_hi"], 1)
            V.tensor_tensor(gwlo[:], gw[:], gwhi[:].bitcast(F32), ALU.subtract).then_inc(S["gw_lo"], 1)
            V.memset(ck2[:].bitcast(F32), 0.0).then_inc(S["masks"], 1)
            for n in range(20, 28):
                lo(U_KV + n)
            kv_job(2)
            for n in range(8):
                lo(U_Q0 + 4 + n)
                for m in range(4 * n, 4 * n + 4):
                    kv_i, lp = divmod(m, LP)
                    dve.wait_ge(S["b_hi"], m + 1)
                    V.scalar_tensor_tensor(
                        out=bT[:, 1, kv_i, lp, :].rearrange("p (g n) -> p g n", g=NG),
                        in0=cT[:, kv_i * 4:kv_i * 4 + 4, 2 * lp:2 * lp + 481:16],
                        scalar=pos_sb[:, kv_i, lp:lp + 1],
                        in1=bT[:, 0, kv_i, lp, :].bitcast(F32).rearrange("p (g n) -> p g n", g=NG),
                        op0=ALU.add, op1=ALU.subtract).then_inc(S["b_lo"], 1)

            def qs_lo(j):
                for t in range(TT):
                    dve.wait_ge(S["qs_hi"], 4 * j + t + 1)
                    V.tensor_tensor(qs[:, t, :, 1, :], q_tok[:, j, t, :].rearrange("p (h d) -> p h d", h=8),
                                    qs[:, t, :, 0, :].bitcast(F32), ALU.subtract).then_inc(S["qs_lo"], 1)

            dve.wait_ge(S["q_copied"], 4)
            rope(q_tok[:, 0], 8, 3)
            for n in range(16):
                lo(U_CMP + 4 + n)
                if n < 8:
                    c, t = divmod(n, TT)
                    dve.wait_ge(S["kd_hi"], n + 1)
                    V.tensor_tensor(kd[:, c, t, :, 1, :].rearrange("p g (u d) -> p g u d", u=2),
                                    k_tok[:, c, t, :].rearrange("p (g d) -> p g d", g=NG).unsqueeze(2)
                                    .broadcast_to([P, NG, 2, HD]),
                                    kd[:, c, t, :, 0, :].bitcast(F32).rearrange("p g (u d) -> p g u d", u=2),
                                    ALU.subtract).then_inc(S["kd_lo"], 1)
                if n == 8:
                    qs_lo(0)
            dve.wait_ge(S["hid_done"], 4)
            for ht in range(2):
                V.tensor_copy(hid_rep[:, ht, :, :, 0:NCMP],
                              hid_v[:, ht, :].rearrange("p (g n) -> p g n", g=NG).unsqueeze(2)
                              .broadcast_to([P, NG, REP, NCMP])).then_inc(S["rep_done"], 1)
            tp_items(8, 24)
            dve.wait_ge(S["ck_hi"], 1)
            V.tensor_tensor(ck2[:, 1, :, 0:NCMP], ps[:, SET_A, 0:124].rearrange("p (g n) -> p g n", g=NG),
                            ck2[:, 0, :, 0:NCMP].bitcast(F32), ALU.subtract).then_inc(S["ck_lo"], 1)
            dve.wait_ge(S["cv_full"], 1)
            for g in range(NG):
                V.tensor_tensor(cv_bd[:, g], ps[:, SET_A + 1, g * HD:(g + 1) * HD].unsqueeze(1)
                                .broadcast_to([P, REP, HD]),
                                diag4.unsqueeze(2).broadcast_to([P, REP, HD]), ALU.mult
                                ).then_inc(S["cv_done"], 1)
            for n in range(8):
                lo(U_Q1 + 4 + n)
            dve.wait_ge(S["q_copied"], 8)
            rope(q_tok[:, 1], 8, 4)
            tp_items(24, 32)
            qs_lo(1)
            tp_items(32, 40)
            for i in range(TT):
                sc = prob[:, i, :].rearrange("p (h n) -> p h n", h=NH)
                dve.wait_ge(S["cs_full"], i + 1)
                V.tensor_tensor(sc, ps[:, i, :].rearrange("p (h n) -> p h n", h=NH),
                                cmask[:, i].unsqueeze(1).broadcast_to([P, NH, CB]), ALU.add
                                ).then_inc(S["cs_masked"], 1)
                dve.wait_ge(S["cs_masked"], i + 1)
                V.tensor_reduce(cst[:, 0, i, :], sc, AX.X, ALU.max).then_inc(S["cs_max"], 1)
                dve.wait_ge(S["cs_max"], i + 1)
                V.tensor_tensor(sc, sc, cst[:, 0, i, :].unsqueeze(2).broadcast_to([P, NH, CB]), ALU.subtract
                                ).then_inc(S["cs_sub"], 1)
            for i in range(TT):
                sc = prob[:, i, :].rearrange("p (h n) -> p h n", h=NH)
                dve.wait_ge(S["cs_exp"], i + 1)
                V.tensor_reduce(cst[:, 1, i, :], sc, AX.X, ALU.add).then_inc(S["cs_sum"], 1)
                dve.wait_ge(S["cs_sum"], i + 1)
                V.reciprocal(cst[:, 2, i, :], cst[:, 1, i, :]).then_inc(S["cs_inv"], 1)
                dve.wait_ge(S["cs_inv"], i + 1)
                V.scalar_tensor_tensor(out=cst[:, 3, i, :], in0=cst[:, 2, i, :], scalar=some[:, i:i + 1],
                                       in1=gates[:, i, :, 0], op0=ALU.mult, op1=ALU.mult
                                       ).then_inc(S["cs_coef"], 1)
            for i in range(TT):
                dve.wait_ge(S["cs_coef"], i + 1)
                dve.wait_ge(S["cs_pv"], i + 1)
                for b in range(2):
                    V.tensor_tensor(o_acc[:, i, b * W:(b + 1) * W].rearrange("p (h d) -> p h d", h=8),
                                    ps[:, 6 + b, :].rearrange("p (h d) -> p h d", h=8),
                                    cst[:, 3, i, 8 * b:8 * b + 8].unsqueeze(2).broadcast_to([P, 8, HD]), ALU.mult
                                    ).then_inc(S["o_cmp"], 1)

            def p_copy(n):
                w = (n // 32 + 1) * P
                dve.wait_ge(S["pt_full"], n + 1)
                if n >= 4:
                    dve.wait_ge(S["pv_done"], n - 3)
                V.tensor_copy(probT[:, n % 4, 0:w], ps[:, 4, 0:w]).then_inc(S["pt_dve"], 1)

            def scale_out(ig):
                i, g = divmod(ig, NG)
                c = slice(8 * ig, 8 * ig + 8)
                dve.wait_ge(S["exp_done"], 8 * (ig + 1))
                V.reciprocal(linv[:, c], lsum[:, c]).then_inc(S["l_inv"], 1)
                dve.wait_ge(S["l_inv"], ig + 1)
                V.tensor_tensor(linv[:, c].rearrange("p (b r) -> p b r", b=2),
                                linv[:, c].rearrange("p (b r) -> p b r", b=2),
                                gates[:, i, g * REP:(g + 1) * REP, 1:3].rearrange("p r b -> p b r"), ALU.mult
                                ).then_inc(S["a_coef"], 1)
                dve.wait_ge(S["a_coef"], ig + 1)
                dve.wait_ge(S["pv_done"], 8 * (ig + 1))
                if ig >= 1:
                    dve.wait_ge(S["o_added"], ig)
                V.tensor_tensor(otmp.rearrange("p b (r d) -> p (b r) d", r=REP),
                                ps[:, 6 + ig % 2, :].rearrange("p (u d) -> p u d", d=HD),
                                linv[:, c].unsqueeze(2).broadcast_to([P, 8, HD]), ALU.mult
                                ).then_inc(S["a_scaled"], 1)

            for s in range(64):
                w = (s // 16 + 1) * P
                dve.wait_ge(S["sc_full"], s + 1)
                b = 2 * (s % 2)
                V.tensor_reduce(nmax[:, 2 * s:2 * s + 2], ps[:, b:b + 2, 0:w], AX.X, ALU.max, negate=True
                                ).then_inc(S["max_done"], 1)
                if s >= 1:
                    p_copy(2 * s - 2)
                if s >= 6 and (s - 6) % 4 == 0:
                    scale_out((s - 6) // 4)
            p_copy(126)
            scale_out(15)

            def oT_lo(k):
                dve.wait_ge(S["oT_hi"], k + 1)
                V.tensor_tensor(oT[:, 1, k, :], ps[:, SET_B + k % 4, :], oT[:, 0, k, :].bitcast(F32),
                                ALU.subtract).then_inc(S["oT_lo"], 1)

            for k in range(4):
                oT_lo(k)
            out_phase(2, U_NO, KD, (SET_A, SET_B), oT_lo)
            ffn(1)

        @block.tensor
        def _(pe):
            M = nc.tensor.matmul

            def unit(u, it=None, per=0):
                pe.wait_ge(S["w_lo"], plus(u + 1, it, per))

            def by_token(bank, h, k, u, start, stop):
                r = u % RING
                for t in range(TT):
                    a_hi, a_lo = h[:, 0, k, t * P:(t + 1) * P], h[:, 1, k, t * P:(t + 1) * P]
                    M(ps[:, bank + t, :], a_hi, whi[:, r, :], start=start, stop=False)
                    M(ps[:, bank + t, :], a_hi, wlo[:, r, :], start=False, stop=False)
                    last = M(ps[:, bank + t, :], a_lo, whi[:, r, :], start=False, stop=stop)
                last.then_inc(S["w_used"], 1)

            def by_feature(bank, h, k, u, start, stop):
                r = u % RING
                for f in range(4):
                    c = slice(f * P, (f + 1) * P)
                    M(ps[:, bank + f, :], whi[:, r, c], h[:, 0, k, :], start=start, stop=False)
                    M(ps[:, bank + f, :], whi[:, r, c], h[:, 1, k, :], start=False, stop=False)
                    last = M(ps[:, bank + f, :], wlo[:, r, c], h[:, 0, k, :], start=False, stop=stop)
                last.then_inc(S["w_used"], 1)

            def job(kind, bank, h, u0, it=None, per=0, parts=None):
                for k in range(KD):
                    unit(u0 + k, it, per)
                    if parts is not None:
                        pe.wait_ge(S["hT_lo"], parts + k + 1)
                    kind(bank, h, k, u0 + k, k == 0, k == KD - 1)

            def pre_norm(j):
                pe.wait_ge(S["normed"], 4 * (j + 1))
                if j == 0:
                    pe.wait_ge(S["consts_in"], 16 * NCONST)
                for k in range(KD):
                    if k >= 4:
                        pe.wait_ge(S["hT_lo"], 8 * j + k - 3)
                    for t in range(TT):
                        last = nc.tensor.transpose(ps[:, SET_B + k % 4, t * P:(t + 1) * P],
                                                   normed_v[:, t, k * P:(k + 1) * P], ident)
                    last.then_inc(S["hT_psum"], 1)

            def turn(src, k, name):
                for t in range(TT):
                    last = nc.tensor.transpose(ps[:, SET_B + k % 4, t * P:(t + 1) * P],
                                               src[:, t, k * P:(k + 1) * P], ident)
                last.then_inc(S[name + "_psum"], 1)

            def out_proj(i, h, u0, tiles, banks, name, base, src=None):
                for half in range(2):
                    for k in range(tiles):
                        u = u0 + half * tiles + k
                        unit(u)
                        if half == 0:
                            pe.wait_ge(S[name + "_lo"], base + k + 1)
                        by_token(banks[half], h, k, u, k == 0, k == tiles - 1)
                        if src is not None and half == 0 and k + 4 < tiles:
                            turn(src, k + 4, name)

            pre_norm(0)
            with pe.Fori(0, 2) as it:
                for p in range(2):
                    u0 = 24 * p
                    xb, yb = (SET_A, SET_B) if p == 0 else (SET_B, SET_A)

                    def n4(c):
                        return it * 8 + (4 * p + c)
                    if p == 1:
                        pe.wait_ge(S["g_silu"], n4(0))
                    job(by_feature, xb, hT_r, u0, it, 48, parts=0)
                    if p == 1:
                        pe.wait_ge(S["o_cent"], n4(0))
                    job(by_token, yb, hT_r, u0 + 8, it, 48)
                    pe.wait_ge(S["qk_lo"], n4(4))
                    for j in range(TT):
                        for n, (a, b) in enumerate(((0, 0), (0, 1), (1, 0))):
                            for d in range(2):
                                last = M(ps[:, xb + j, 0:T - j * P], qk_r[:, a, 1, d, j * P:(j + 1) * P],
                                         qk_r[:, b, 0, d, j * P:T], start=(n == 0 and d == 0),
                                         stop=(n == 2 and d == 1))
                    last.then_inc(S["s_full"], 1)
                    pe.wait_ge(S["v_lo"], n4(4))
                    job(by_token, yb, hT_r, u0 + 16, it, 48)
                    pe.wait_ge(S["s_lo"], n4(4))
                    for i in range(TT):
                        for j in range(i + 1):
                            c0 = j * T - P * (j * (j - 1) // 2) + (i - j) * P
                            for n, (a, b) in enumerate(((0, 0), (0, 1), (1, 0))):
                                last = M(ps[:, xb + i, :], dec_r[:, a, c0:c0 + P], v_r[:, b, j, :],
                                         start=(j == 0 and n == 0), stop=(j == i and n == 2))
                    last.then_inc(S["o_full"], 1)
                pe.wait_ge(S["g_silu"], it * 8 + 8)
                pe.wait_ge(S["o_cent"], it * 8 + 8)

            pe.wait_ge(S["y_done"], 16)
            pe.wait_ge(S["g_silu"], 16)
            for k in range(4):
                turn(y, k, "yT")
            out_proj(0, yT, U_RO, 16, (SET_A, SET_B), "yT", 0, y)

            def ffn(layer):
                j = 1 + 2 * layer
                pre_norm(j)
                u0, f0 = U_FI[layer], FJ * layer
                job(by_feature, SET_A, hT_f, u0, parts=8 * j)
                job(by_feature, SET_B, hT_f, u0 + 8)
                with pe.Fori(0, 4) as it:
                    for q in range(2):
                        pe.wait_ge(S["ff_a"], it * 4 + 2 * (f0 + q + 1))
                        job(by_feature, (SET_A, SET_B)[q], hT_f, u0 + 16 + 8 * q, it, 16)
                pe.wait_ge(S["ff_a"], 2 * (f0 + 9))
                job(by_feature, SET_A, hT_f, u0 + 80)
                pe.wait_ge(S["ff_a"], 2 * (f0 + 10))
                out_proj(j, aT, U_FO[layer], KF, (SET_B, SET_A), "ff", KF * layer)

            ffn(0)

            pre_norm(2)
            job(by_token, SET_A, kvT, U_KV, parts=16)
            job(by_token, SET_B, kvT, U_KV + 8)

            def items(lo_m, hi_m):
                for m in range(lo_m, hi_m):
                    if m - 4 >= lo_m:
                        pe.wait_ge(S["tp_act" if m % 2 else "tp_dve"], (m - 4) // 2 + 1)
                    for t in range(TT):
                        if m < 8:
                            src, n = v_tok0[:, t, (m // 4) * 256 + (m % 4) * HD:][:, 0:HD], HD
                        elif m < 24:
                            src, n = kd[:, (m - 8) // 8, t, (m - 8) % 8 // 2, m % 2, :].bitcast(F32), P
                        else:
                            src, n = qs[:, t, (m - 24) % 8].rearrange("p a d -> p (a d)").bitcast(F32), P
                        last = nc.tensor.transpose(ps[0:n, (SET_A if m < 8 else SET_B) + m % 4, t * P:(t + 1) * P],
                                                   src, ident)
                    last.then_inc(S["tp_full"], 1)

            pe.wait_ge(S["rope_done"], 2)
            items(0, 8)
            pe.wait_ge(S["tp_act"], 4)
            pe.wait_ge(S["tp_dve"], 4)
            job(by_token, SET_A, kvT, U_KV + 16)
            pe.wait_ge(S["kv_k"], 8)
            job(by_token, SET_B, hT_n, U_Q0)
            pe.wait_ge(S["kv_k"], 12)
            pe.wait_ge(S["gw_lo"], 1)
            for t in range(TT):
                for k in range(KD):
                    c = slice(t * P, (t + 1) * P)
                    o = ps[:, SET_A, 48 * t:48 * t + 48]
                    M(o, hT_n[:, 0, k, c], gwhi[:, k, :], start=(k == 0), stop=False)
                    M(o, hT_n[:, 0, k, c], gwlo[:, k, :], start=False, stop=False)
                    last = M(o, hT_n[:, 1, k, c], gwhi[:, k, :], start=False, stop=(k == KD - 1))
            last.then_inc(S["gate_full"], 1)
            pe.wait_ge(S["gate_done"], 1)
            for kv_i in range(2):
                for n in range(8):
                    u = U_CMP + 8 * kv_i + n
                    unit(u)
                    pe.wait_ge(S["b_lo"], 16 * kv_i + 2 * n + 2)
                    r = u % RING
                    for c in range(2):
                        lp = 2 * n + c
                        for ht in range(2):
                            o = ps[:, SET_A + 2 * kv_i + ht, 0:124]
                            cols = slice(c * 256 + ht * P, c * 256 + (ht + 1) * P)
                            M(o, whi[:, r, cols], bT[:, 0, kv_i, lp, :], start=(lp == 0), stop=False)
                            M(o, whi[:, r, cols], bT[:, 1, kv_i, lp, :], start=False, stop=False)
                            last = M(o, wlo[:, r, cols], bT[:, 0, kv_i, lp, :], start=False, stop=(lp == LP - 1))
                    last.then_inc(S["w_used"], 1)
            pe.wait_ge(S["kd_lo"], 8)
            pe.wait_ge(S["q_copied"], 4)
            items(8, 24)
            pe.wait_ge(S["hid_done"], 4)
            pe.wait_ge(S["nsa_in"], 16 * 4)
            for ht in range(2):
                last = M(ps[:, SET_A, 0:124], w2k[:, ht].rearrange("p u d -> p (u d)"), hid_k[:, ht, :],
                         start=(ht == 0), stop=(ht == 1))
            last.then_inc(S["ck_full"], 1)
            pe.wait_ge(S["rep_done"], 2)
            for g in range(NG):
                for ht in range(2):
                    last = M(ps[:, SET_A + 1, g * HD:(g + 1) * HD], hid_rep[:, ht, g].rearrange("p r n -> p (r n)"),
                             w2v[:, ht, :], start=(ht == 0), stop=(ht == 1))
            last.then_inc(S["cv_full"], 1)
            pe.wait_ge(S["ck_lo"], 1)
            pe.wait_ge(S["cv_done"], 4)
            job(by_token, SET_A, hT_n, U_Q1)
            pe.wait_ge(S["qs_lo"], 4)
            pe.wait_ge(S["tp_act"], 12)
            pe.wait_ge(S["tp_dve"], 12)
            items(24, 32)
            pe.wait_ge(S["q_copied"], 8)
            pe.wait_ge(S["qs_lo"], 8)
            pe.wait_ge(S["tp_act"], 16)
            pe.wait_ge(S["tp_dve"], 16)
            items(32, 40)
            pe.wait_ge(S["ck_lo"], 1)
            pe.wait_ge(S["cv_done"], 4)
            pe.wait_ge(S["tp_act"], 20)
            pe.wait_ge(S["tp_dve"], 20)
            for i in range(TT):
                for hd in range(NH):
                    for part in range(2):
                        last = M(ps[:, i, hd * CB:(hd + 1) * CB], qT2[:, hd, i * P:(i + 1) * P],
                                 ck2[:, part, hd // REP, :], start=(part == 0), stop=(part == 1))
                last.then_inc(S["cs_full"], 1)
            for i in range(TT):
                pe.wait_ge(S["cs_exp"], i + 1)
                if i >= 2:
                    pe.wait_ge(S["cs_pT"], i - 1)
                for g in range(NG):
                    last = nc.tensor.transpose(ps[:, 4 + i % 2, g * P:(g + 1) * P], prob[:, i, g * P:(g + 1) * P],
                                               ident)
                last.then_inc(S["cs_tp"], 1)
            for i in range(TT):
                pe.wait_ge(S["cs_pT"], i + 1)
                if i >= 1:
                    pe.wait_ge(S["o_cmp"], 2 * i)
                for g in range(NG):
                    last = M(ps[:, 6 + g // 2, (g % 2) * 256:(g % 2) * 256 + 256], probT[:, i, g * P:(g + 1) * P],
                             cv_bd[:, g].rearrange("p r d -> p (r d)"), start=True, stop=True)
                last.then_inc(S["cs_pv"], 1)

            def where(n):
                ig, u = divmod(n, 8)
                i, g = divmod(ig, NG)
                return i, g, u // REP, u % REP, ig, u

            def scores(s):
                if s >= 2:
                    pe.wait_ge(S["exp_done"], 2 * s - 2)
                for n in (2 * s, 2 * s + 1):
                    i, g, b, r, ig, u = where(n)
                    w = (i + 1) * P
                    bank = 2 * (s % 2) + n % 2
                    q = qT2[:, g * REP + r, i * P:(i + 1) * P]
                    M(ps[:, bank, 0:w], q, kT2[:, b, g, 0, 0:w], start=True, stop=False)
                    M(ps[:, bank, 0:w], q, kT2[:, b, g, 1, 0:w], start=False, stop=False)
                    last = M(ps[:, bank, w - P:w], ident_b[:], causal_b[:], start=False, stop=True)
                last.then_inc(S["sc_full"], 1)

            def turn_probs(n):
                i = n // 32
                pe.wait_ge(S["exp_done"], n + 1)
                if n >= 2:
                    pe.wait_ge(S["pt_act" if n % 2 else "pt_dve"], (n - 2) // 2 + 1)
                for j in range(i + 1):
                    last = nc.tensor.transpose(ps[:, 4 + n % 2, j * P:(j + 1) * P], prob[:, n % 4, j * P:(j + 1) * P],
                                               ident)
                last.then_inc(S["pt_full"], 1)

            def values(n):
                i, g, b, r, ig, u = where(n)
                pe.wait_ge(S["pt_act" if n % 2 else "pt_dve"], n // 2 + 1)
                if u == 0 and ig >= 2:
                    pe.wait_ge(S["a_scaled"], ig - 1)
                for j in range(i + 1):
                    last = M(ps[:, 6 + ig % 2, u * HD:(u + 1) * HD], probT[:, n % 4, j * P:(j + 1) * P],
                             v_all[:, b, j, g * HD:(g + 1) * HD], start=(j == 0), stop=(j == i))
                last.then_inc(S["pv_done"], 1)

            pe.wait_ge(S["cs_masked"], TT)
            pe.wait_ge(S["cs_pT"], TT)
            pe.wait_ge(S["o_cmp"], 2 * TT)
            for s in range(64 + 2):
                if s < 64:
                    scores(s)
                if 1 <= s <= 64:
                    turn_probs(2 * s - 2)
                    turn_probs(2 * s - 1)
                if s >= 2:
                    values(2 * s - 4)
                    values(2 * s - 3)
            pe.wait_ge(S["o_added"], TT * NG)
            for k in range(4):
                turn(o_acc, k, "oT")
            out_proj(2, oT, U_NO, KD, (SET_A, SET_B), "oT", 0, o_acc)
            ffn(1)


_INS = ['x', 'norms', 'ret_w_in', 'ret_w_out', 'nsa_w_in', 'nsa_w_out', 'w_kv', 'cmp_w1_k', 'cmp_w2_k', 'cmp_w1_v', 'cmp_w2_v', 'ffn_w_in', 'ffn_w_out']
_OUTS = [((1, T, D), 'float32')]


def kernel(**inputs):
    import numpy as _np
    import concourse.bacc as _bacc
    from concourse import mybir as _mybir
    from concourse.bass_utils import run_bass_kernel_spmd as _run

    nc = _bacc.Bacc("TRN2", target_bir_lowering=False, num_devices=1)
    arrays, args = {}, []
    feeds = [(name, _np.ascontiguousarray(inputs[name])) for name in _INS]
    feeds.append(("feature_columns", lay_out_columns(*(_np.asarray(inputs[n]) for n in (
        "norms", "kv_norm", "ret_gn", "cmp_pos_k", "cmp_pos_v")))))
    feeds += shape_constants().items()
    for name, a in feeds:
        arrays[f"in_{name}_dram"] = a
        args.append(nc.dram_tensor(f"in_{name}_dram", a.shape, _mybir.dt.from_np(a.dtype), kind="ExternalInput").ap())
    for i, (shape, dtype) in enumerate(_OUTS):
        dt = _mybir.dt.from_np(_np.dtype(dtype))
        args.append(nc.dram_tensor(f"out_{i}_dram", shape, dt, kind="ExternalOutput").ap())
    yoco_kernel(nc, *args)
    r = _run(nc, [arrays], core_ids=[0])
    got = tuple(r.results[0][f"out_{i}_dram"] for i in range(len(_OUTS)))
    return got[0]
```

```python
from contextlib import ExitStack

import numpy as np

import concourse.bass as bass
from concourse import mybir

F32 = mybir.dt.float32
F32R = mybir.dt.float32r
BF16 = mybir.dt.bfloat16
ALU = mybir.AluOpType
ACT = mybir.ActivationFunctionType
AX = mybir.AxisListType

P = 128
D = 1024
T = 512
TT = T // P
KD = D // P
W = 512
RH, DK, DV = 4, 256, 512
NH, NG, REP, HD = 16, 4, 4, 64
FF = 2816
FJ = FF // 256
KF = FF // P
NCMP = 31
CB = 32
LP = 16
ROT = 8
EPS = 1e-6
NEG = -1e30
RAW = 8
RING = 4

U_RET = 0
U_RO = U_RET + RH * 3 * KD
U_FI = [U_RO + 2 * 16, 0]
U_FO = [U_FI[0] + FJ * KD, 0]
U_KV = U_FO[0] + 2 * KF
U_Q0 = U_KV + 3 * KD
U_CMP = U_Q0 + KD
U_Q1 = U_CMP + LP
U_NO = U_Q1 + KD
U_FI[1] = U_NO + 2 * KD
U_FO[1] = U_FI[1] + FJ * KD
U_END = U_FO[1] + 2 * KF

SET_A, SET_B = 0, 4


def shape_constants():
    f = np.float32
    pos = np.arange(T, dtype=f)
    freqs = (f(1.0) / (f(10000.0) ** np.linspace(0.0, 1.0, DK // 2, dtype=f))).astype(f)
    ang = (pos[:, None] * freqs[None, :]).astype(f)
    ret = np.stack([np.cos(ang).T, np.sin(ang).T], axis=1).astype(f)
    log_g = np.log1p(-np.exp2(-5.0 - np.arange(RH, dtype=np.float64)))
    dist = np.arange(T)[None, :] - np.arange(P)[:, None]
    decay = np.where(dist[:, None, :] >= 0,
                     np.exp(log_g[None, :, None] * np.maximum(dist, 0)[:, None, :]), 0.0)
    decay = (decay * DK ** -0.5).astype(f)
    pf = (f(500000.0) ** (-np.arange(0, 2 * ROT, 2, dtype=f) / f(2 * ROT))).astype(f)
    pang = (pos[:, None] * pf[None, :]).astype(f)
    rope = np.stack([np.cos(pang), np.sin(pang)], axis=0).astype(f)
    rope = rope.reshape(2, TT, P, ROT).transpose(2, 0, 1, 3).reshape(P, 2 * TT * ROT)
    t = np.arange(T)
    end = np.arange(CB) * 16 + 31
    valid = (end[None, :] <= t[:, None]) & (np.arange(CB)[None, :] < NCMP)
    cmask = np.where(valid, 0.0, NEG).astype(f).reshape(TT, P, CB).transpose(1, 0, 2).reshape(P, TT * CB)
    some = valid.any(-1).astype(f).reshape(TT, P).T
    diag = (np.arange(P)[:, None] // CB == np.arange(P // CB)[None, :]).astype(f)
    ident = np.eye(P, dtype=f)
    causal = np.where(np.arange(P)[None, :] > np.arange(P)[:, None], NEG, 0.0).astype(f)
    small = np.concatenate([ident, rope, cmask, some, diag], axis=1)
    return {
        "c_ret": np.ascontiguousarray(ret.reshape(P, 2 * T)),
        "c_decay": np.ascontiguousarray(decay.reshape(P, RH * T)),
        "c_causal": causal,
        "c_small": np.ascontiguousarray(small.astype(f)),
    }


def lay_out_columns(norms, kv_norm, ret_gn, cmp_pos_k, cmp_pos_v):
    rows = [norms[0, 0], norms[0, 2], norms[1, 0], norms[1, 2], kv_norm, ret_gn[0]]
    cols = [r.reshape(-1, P).T for r in rows]
    cols += [p.reshape(LP, P).T for p in (cmp_pos_k, cmp_pos_v)]
    return np.ascontiguousarray(np.concatenate(cols, axis=1))


def yoco_kernel(nc, x, norms, ret_w_in, ret_w_out, nsa_w_in, nsa_w_out, w_kv,
                cmp_w1_k, cmp_w2_k, cmp_w1_v, cmp_w2_v, ffn_w_in, ffn_w_out, feature_columns,
                c_ret, c_decay, c_causal, c_small, out):
    with ExitStack() as ctx:
        def sb(name, shape, dt=F32, stack=ctx):
            return stack.enter_context(nc.sbuf_tensor(name, shape, dt))

        def sem(name):
            return ctx.enter_context(nc.semaphore(name))

        xs = sb("xs", [P, TT, D])
        raw = sb("raw", [P, RAW, W])
        whi = sb("whi", [P, RING, W], F32R)
        wlo = sb("wlo", [P, RING, W], F32R)
        work = sb("work", [P, 8, W])
        gain_row = sb("gain_row", [P, D])
        columns = sb("columns", [P, 5 * KD + 16 + 2 * LP])
        gains = columns[:, 0:5 * KD].rearrange("p (n k) -> p n k", n=5)
        ret_gain = columns[:, 5 * KD:5 * KD + 16]
        pos_sb = columns[:, 5 * KD + 16:].rearrange("p (c l) -> p c l", c=2)
        small = sb("small", [P, c_small.shape[1]])
        ident_b = sb("ident_b", [P, P], BF16)
        causal_b = sb("causal_b", [P, P], BF16)
        means = sb("means", [P, 4, TT])
        halves = sb("halves", [P, 4, 2, TT])
        base = sb("base", [P, 4, TT])
        eps = sb("eps", [P, 1])
        std = sb("std", [P, 8, TT])
        rstd = sb("rstd", [P, 8, TT])
        normed_v = work[:, :, :].rearrange("p (t c) n -> p t (c n)", t=TT)
        at = 0
        ident = small[:, 0:P]
        at = P
        rope_tab = small[:, at:at + 2 * TT * ROT].rearrange("p (f t e) -> p f t e", f=2, t=TT)
        at += 2 * TT * ROT
        cmask = small[:, at:at + TT * CB].rearrange("p (t n) -> p t n", t=TT)
        at += TT * CB
        some = small[:, at:at + TT]
        at += TT
        diag4 = small[:, at:at + 4]

        with ExitStack() as s:
            hT_r = sb("hT_r", [P, 2, KD, T], F32R, s)
            qk_r = sb("qk_r", [P, 2, 2, 2, T], F32R, s)
            v_r = sb("v_r", [P, 2, TT, W], F32R, s)
            y = sb("y", [P, TT, RH * DV], F32, s)
            dec_r = sb("dec_r", [P, 2, 1280], F32R, s)
            rot_tab = sb("rot_tab", [P, 2, T], F32, s)
            decay = sb("decay", [P, RH * T], F32, s)
            gate_r = sb("gate_r", [P, TT, W], F32, s)
            causal = y[:, 0, 0:P]
            bn = sb("bn", [P, TT, 6], F32, s)
            mv = sb("mv", [P, TT, 2], F32, s)
            gvar = sb("gvar", [P, 3, TT], F32, s)
        with ExitStack() as s:
            yT = sb("yT", [P, 2, 16, T], F32R, s)
        with ExitStack() as s:
            hT_f = sb("hT_f", [P, 2, KD, T], F32R, s)
            aT = sb("aT", [P, 2, KF, T], F32R, s)
        with ExitStack() as s:
            kvT = sb("kvT", [P, 2, KD, T], F32R, s)
            hT_n = sb("hT_n", [P, 2, KD, T], F32R, s)
            kT2 = sb("kT2", [P, 2, NG, 2, T], F32R, s)
            v_all = sb("v_all", [P, 2, TT, NG * HD], F32, s)
            cv_bd = sb("cv_bd", [P, NG, REP, HD], F32, s)
            ck2 = sb("ck2", [P, 2, NG, CB], F32R, s)
            w2k = sb("w2k", [P, 2, 2, HD], F32, s)
            w2v = sb("w2v", [P, 2, HD], F32, s)
            gates = sb("gates", [P, TT, NH, 3], F32, s)
            with ExitStack() as s2:
                gate_T = sb("gate_T", [P, T], F32, s2)
            nmax = sb("nmax", [P, 128], F32, s)
            lsum = sb("lsum", [P, 128], F32, s)
            linv = sb("linv", [P, 128], F32, s)
            cst = sb("cst", [P, 4, TT, NH], F32, s)
            with ExitStack() as s2:
                cT = sb("cT", [P, 8, T], F32, s2)
            with ExitStack() as s2:
                qs = sb("qs", [P, TT, 8, 2, HD], F32R, s2)
            with ExitStack() as s2:
                prob = sb("prob", [P, 4, W], F32, s2)
                probT = sb("probT", [P, 4, W], F32, s2)
            blank = s.enter_context(nc.sbuf_tensor("over_cT", [P, 8 * T], F32))
            rope_t = sb("rope_t", [P, 4, TT * 8 * ROT], F32, s)
            otmp = rope_t[:, 0:2, :]
            gwhi = sb("gwhi", [P, KD, 48], F32R, s)
            gwlo = sb("gwlo", [P, KD, 48], F32R, s)
        with ExitStack() as s:
            kd = sb("kd", [P, 2, TT, NG, 2, 2 * HD], F32R, s)
        with ExitStack() as s:
            qT2 = sb("qT2", [P, NH, T], F32R, s)
            with ExitStack() as s2:
                ckz = sb("ckz", [P, 2, NG, REP, P], F32R, s2)
            oT = sb("oT", [P, 2, KD, T], F32R, s)
            bT = sb("bT", [P, 2, 2, LP, 124], F32R, s)
        gw = gain_row[:, 0:KD * 48].rearrange("p (k n) -> p k n", k=KD)
        hid = work[:, 7, :].rearrange("p (c n) -> p c n", c=2)
        hid_k = work[:, 4, 0:248].rearrange("p (h n) -> p h n", h=2)
        hid_rep = work[:, 5:7, :].rearrange("p h (g r n) -> p h g r n", g=NG, r=REP)
        v_tok0 = work[:, 0:4, :]
        k_tok = work[:, 4:8, :].rearrange("p (c a) (b n) -> p c (a b) n", c=2, b=2)
        q_tok = work[:, :, :].rearrange("p (j t) n -> p j t n", j=2)
        cs_T = work[:, 0:4, :]
        o_acc = normed_v
        ps = ctx.enter_context(nc.psum_tensor("ps", [P, 8, W], F32))

        names = """consts_in tables_in gain_in nsa_in w_hi w_lo w_used
            norm_sq norm_std norm_rstd normed hT_psum hT_hi hT_lo
            tile_out post_sq post_base post_std post_rstd post_gain x_ready masks casts
            rot_prod rot_sum qk_hi qk_lo v_hi v_lo s_full s_dec s_hi s_lo
            g_silu o_full o_bn o_mv o_var o_std o_rstd o_cent y_done yT_psum yT_hi yT_lo
            ff_silu ff_a ff_hi ff_lo
            kv_v kv_k rope_prod rope_done kd_hi kd_lo gw_hi gw_lo gate_full gate_done
            tp_full tp_act tp_dve shifted b_hi b_lo q_copied qs_hi qs_lo
            gate_sig gate_T_full hid_done hid_T_full hid_k_done rep_zero rep_done ckz_zero ckz_done cT_full cT_act cT_dve ck_full ck_hi ck_lo cv_full cv_done
            cs_full cs_masked cs_max cs_sub cs_exp cs_sum cs_inv cs_some cs_coef cs_tp cs_pT cs_pv o_cmp
            sc_full max_done exp_done pt_full pt_act pt_dve pv_done l_inv a_coef a_scaled a_pair o_added
            oT_psum oT_hi oT_lo stored""".split()
        S = {n: sem(n) for n in names}
        x_in = [sem(f"x_in{t}") for t in range(TT)]
        raw_in = [sem(f"raw_in{i}") for i in range(RAW)]

        block = ctx.enter_context(nc.Block())
        T_LAG, V_LAG = 3, 5

        def by_act(n):
            return n % 3 == 0

        def copies(n, act_copies):
            return sum(by_act(m) == act_copies for m in range(n + 1))

        def plus(c, it, per):
            return c if it is None else c + it * per

        @block.sync
        def _(sp):
            def load(u, src, it=None, per=0, cols=1):
                if u >= RAW or it is not None:
                    sp.wait_ge(S["w_lo"], plus(u - RAW + 1, it, per))
                dst = raw[:, u % RAW, :]
                if cols > 1:
                    dst = dst.rearrange("p (c n) -> p c n", c=cols)
                sp.dma_start(dst, src).then_inc(raw_in[u % RAW], 16)

            ret = ret_w_in[0].rearrange("(k p) n -> p k n", p=P)
            ret_qk = ret[:, :, 0:2 * RH * DK].rearrange("p k (c n) -> p k c n", c=2)

            def head_loads(h, it):
                for k in range(KD):
                    load(k, ret_qk[:, k, :, bass.ds(h * DK, DK)], it, 24, cols=2)
                for part in range(2):
                    col = 2 * RH * DK + part * RH * DV
                    for k in range(KD):
                        load(KD * (part + 1) + k, ret[:, k, bass.ds(h * DV + col, DV)], it, 24)

            for t in range(TT):
                sp.dma_start(xs[:, t, :], x[0, t * P:(t + 1) * P, :]).then_inc(x_in[t], 16)
            head_loads(0, None)
            with sp.Fori(1, RH) as h:
                head_loads(h, h)

            def out_loads(u0, w, tiles):
                v = w.rearrange("(k p) n -> p k n", p=P)
                for half in range(2):
                    for k in range(tiles):
                        load(u0 + half * tiles + k, v[:, k, half * W:(half + 1) * W])

            out_loads(U_RO, ret_w_out[0], 16)

            def ffn_loads(layer):
                v = ffn_w_in[layer].rearrange("(k p) (c n) -> p k c n", p=P, c=2)
                u0 = U_FI[layer]
                with sp.Fori(0, FJ) as b:
                    for k in range(KD):
                        load(u0 + k, v[:, k, :, bass.ds(b * 256, 256)], b, KD, cols=2)
                out_loads(U_FO[layer], ffn_w_out[layer], KF)

            ffn_loads(0)
            kv = w_kv.rearrange("(k p) n -> p k n", p=P)
            for c in range(3):
                for k in range(KD):
                    load(U_KV + c * KD + k, kv[:, k, c * W:(c + 1) * W])
            wq = nsa_w_in[0].rearrange("(k p) n -> p k n", p=P)
            for k in range(KD):
                load(U_Q0 + k, wq[:, k, 0:W])
            for kv_i, w1 in enumerate((cmp_w1_k, cmp_w1_v)):
                v = w1.rearrange("(k p) n -> p k n", p=P)
                for k in range(LP // 2):
                    load(U_CMP + kv_i * 8 + k, v[:, 2 * k:2 * k + 2, :], cols=2)
            for k in range(KD):
                load(U_Q1 + k, wq[:, k, W:2 * W])
            out_loads(U_NO, nsa_w_out[0], KD)
            ffn_loads(1)
            for t in range(TT):
                sp.wait_ge(S["x_ready"], 12 + t + 1)
                sp.dma_start(out[0, t * P:(t + 1) * P, :], xs[:, t, :]).then_inc(S["stored"], 16)
            sp.wait_ge(S["stored"], 64)

        @block.gpsimd
        def _(pool):
            def gain_load(i):
                layer, n = i // 2, 1 + 2 * (i % 2)
                pool.dma_start(gain_row[:], norms[layer, n:n + 1, :].broadcast_to([P, D])).then_inc(S["gain_in"], 16)

            gain_load(0)
            pool.wait_ge(S["consts_in"], 32)
            nc.gpsimd.tensor_copy(ident_b[:], ident).then_inc(S["y_done"], 1)
            with pool.Fori(0, RH) as h:
                for t in range(TT):
                    pool.wait_ge(S["g_silu"], h * 4 + (t + 1))
                    pool.wait_ge(S["o_cent"], h * 4 + (t + 2))
                    nc.gpsimd.tensor_tensor(y[:, t, bass.ds(h * DV, DV)], work[:, 4 + t, :], gate_r[:, t, :],
                                            ALU.mult).then_inc(S["y_done"], 1)
            pool.wait_ge(S["x_ready"], 4)
            gain_load(1)
            pool.wait_ge(S["normed"], 12)
            for dup in range(2):
                pool.dma_start(w2k[:, :, dup, :], cmp_w2_k.rearrange("(h p) d -> p h d", p=P)
                               ).then_inc(S["nsa_in"], 16)
            pool.dma_start(w2v[:, :, :], cmp_w2_v.rearrange("(h p) d -> p h d", p=P)).then_inc(S["nsa_in"], 16)
            pool.dma_start(gw[:], nsa_w_in[0].rearrange("(k p) n -> p k n", p=P)[:, :, NH * HD:NH * HD + 48]
                           ).then_inc(S["nsa_in"], 16)
            pool.wait_ge(S["tp_act"], 4)
            pool.wait_ge(S["tp_dve"], 4)
            pool.dma_start(cT[HD:P, :, 0:T - 1], cT[0:HD, :, 1:T]).then_inc(S["shifted"], 16)
            pool.wait_ge(S["gw_lo"], 1)
            gain_load(2)
            pool.wait_ge(S["kd_lo"], 8)
            nc.gpsimd.memset(hid_rep[:], 0.0).then_inc(S["rep_zero"], 1)
            pool.wait_ge(S["w_used"], U_Q1 + KD)
            nc.gpsimd.memset(ckz[:].bitcast(F32), 0.0).then_inc(S["ckz_zero"], 1)
            pool.wait_ge(S["ckz_zero"], 1)
            pool.wait_ge(S["ck_lo"], 1)
            for part in range(2):
                for r in range(REP):
                    nc.gpsimd.tensor_copy(ckz[:, part, :, r, r * CB:r * CB + NCMP],
                                          ck2[:, part, :, 0:NCMP].bitcast(F32)).then_inc(S["ckz_done"], 1)
            for ig in range(TT * NG):
                i, g = divmod(ig, NG)
                o = o_acc[:, i, g * 256:(g + 1) * 256]
                pool.wait_ge(S["a_scaled"], ig + 1)
                pool.wait_ge(S["o_cmp"], 2 * (i + 1))
                nc.gpsimd.tensor_tensor(otmp[:, 0, :], otmp[:, 0, :], otmp[:, 1, :], ALU.add
                                        ).then_inc(S["a_pair"], 1)
                pool.wait_ge(S["a_pair"], ig + 1)
                nc.gpsimd.tensor_tensor(o, o, otmp[:, 0, :], ALU.add).then_inc(S["o_added"], 1)
            pool.wait_ge(S["x_ready"], 12)
            gain_load(3)

        @block.scalar
        def _(act):
            A = nc.scalar.activation

            def hi(u, it=None, per=0):
                act.wait_ge(raw_in[u % RAW], plus(16 * (u // RAW + 1), it, 16 * (per // RAW)))
                if u >= RING:
                    act.wait_ge(S["w_used"], plus(u - 3, it, per))
                A(whi[:, u % RING, :], raw[:, u % RAW, :], ACT.Copy).then_inc(S["w_hi"], 1)

            def x_squares(j, t):
                A(normed_v[:, t, :], xs[:, t, :], ACT.Square, scale=D ** -0.5, accum_out=means[:, j, t:t + 1]
                  ).then_inc(S["norm_sq"], 1)
                act.wait_ge(S["norm_sq"], 4 * j + t + 1)
                A(std[:, j, t:t + 1], means[:, j, t:t + 1], ACT.Sqrt, bias=eps[:, 0:1]).then_inc(S["norm_std"], 1)

            def hT_hi(j, dests):
                if j == 0:
                    act.wait_ge(S["consts_in"], 32)
                for k in range(KD):
                    act.wait_ge(S["hT_psum"], 8 * j + k + 1)
                    for dst, gain in dests:
                        ins = A(dst[:, 0, k, :], ps[:, SET_B + k % 4, :], ACT.Copy,
                                scale=gains[:, gain, k:k + 1])
                    ins.then_inc(S["hT_hi"], 1)

            def half_square(i, half, t):
                A(normed_v[:, t, half * W:(half + 1) * W], ps[:, (SET_B, SET_A)[half] + t, :], ACT.Square,
                  scale=D ** -0.5, accum_out=halves[:, i, half, t:t + 1]).then_inc(S["post_sq"], 1)

            def out_phase(i, u0, tiles, before=None):
                for n in range(4, 2 * tiles):
                    hi(u0 + n)
                    if before is not None and n < tiles:
                        before(n)
                    if n == tiles + 3:
                        act.wait_ge(S["w_used"], u0 + tiles)
                        for t in range(TT):
                            half_square(i, 0, t)
                        act.wait_ge(S["post_base"], i + 1)
                for t in range(TT + 1):
                    if t < TT:
                        if t < TT - 1:
                            act.wait_ge(S["tile_out"], 3 * i + t + 1)
                        else:
                            act.wait_ge(S["w_used"], u0 + 2 * tiles)
                        half_square(i, 1, t)
                        act.wait_ge(S["post_sq"], 8 * i + 5 + t)
                        A(std[:, 4 + i, t:t + 1], halves[:, i, 1, t:t + 1], ACT.Sqrt, bias=base[:, i, t:t + 1]
                          ).then_inc(S["post_std"], 1)
                    if t >= 1 and i < 3:
                        act.wait_ge(S["x_ready"], 4 * i + t)
                        x_squares(i + 1, t - 1)
                if i < 3:
                    for n in range(4):
                        hi(u0 + 2 * tiles + n)

            act.dma_start(small[:], c_small).then_inc(S["consts_in"], 16)
            act.dma_start(columns[:], feature_columns).then_inc(S["consts_in"], 16)
            act.dma_start(rot_tab[:].rearrange("p a b -> p (a b)"), c_ret).then_inc(S["tables_in"], 16)
            act.dma_start(causal, c_causal).then_inc(S["tables_in"], 16)
            act.dma_start(decay[:], c_decay).then_inc(S["tables_in"], 16)
            act.wait_ge(S["masks"], 1)
            for t in range(TT):
                act.wait_ge(x_in[t], 16)
                x_squares(0, t)
            for u in range(4):
                hi(u)
            hT_hi(0, [(hT_r, 0)])

            with act.Fori(0, 2) as it:
                for p in range(2):
                    u0 = 24 * p
                    xb, yb = (SET_A, SET_B) if p == 0 else (SET_B, SET_A)

                    def n4(c):
                        return it * 8 + (4 * p + c)
                    for n in range(4, 12):
                        hi(u0 + n, it, 48)
                    for m in range(4):
                        act.wait_ge(S["rot_sum"], n4(m + 1))
                        A(qk_r[:, 0, m // 2, m % 2, :], work[:, 4 * (m // 2) + 2 * (m % 2), :], ACT.Copy
                          ).then_inc(S["qk_hi"], 1)
                    for n in range(12, 20):
                        hi(u0 + n, it, 48)
                    act.wait_ge(S["w_used"], it * 48 + (u0 + 16))
                    for t in range(TT):
                        A(v_r[:, 0, t, :], ps[:, yb + t, :], ACT.Copy).then_inc(S["v_hi"], 1)
                    at_col = 0
                    for j in range(TT):
                        w = T - j * P
                        act.wait_ge(S["s_dec"], n4(j + 1))
                        A(dec_r[:, 0, at_col:at_col + w], work[:, j, 0:w], ACT.Copy).then_inc(S["s_hi"], 1)
                        at_col += w
                    for n in range(20, 28):
                        hi(u0 + n, it, 48)
                    act.wait_ge(S["w_used"], it * 48 + (u0 + 24))
                    act.wait_ge(S["y_done"], n4(1))
                    for t in range(TT):
                        A(gate_r[:, t, :], ps[:, yb + t, :], ACT.Silu).then_inc(S["g_silu"], 1)
                    act.wait_ge(S["o_var"], it * 2 + (p + 1))
                    A(gvar[:, 1, :], gvar[:, 0, :], ACT.Sqrt).then_inc(S["o_std"], 1)

            def yT_hi(k):
                act.wait_ge(S["yT_psum"], k + 1)
                A(yT[:, 0, k, :], ps[:, SET_A + k % 4, :], ACT.Copy, scale=ret_gain[:, k:k + 1]
                  ).then_inc(S["yT_hi"], 1)

            for k in range(4):
                yT_hi(k)
            out_phase(0, U_RO, 16, yT_hi)

            def ffn(layer):
                hT_hi(1 + 2 * layer, [(hT_f, 1 + 2 * layer)])
                f0 = FJ * layer
                u0 = U_FI[layer]

                def job(b, par, first=False, it=None):
                    bank = SET_A if par % 2 == 0 else SET_B
                    q = par % 2
                    for n in range(4, 12):
                        hi(u0 + 8 * b + n, it, 16)
                    act.wait_ge(S["w_used"], plus(u0 + 8 * b + 8, it, 16))
                    if not first:
                        act.wait_ge(S["ff_a"], plus(2 * (f0 + b - 1), it, 4))
                    for f in range(2):
                        A(work[:, 2 * q + f, :], ps[:, bank + f, :], ACT.Silu).then_inc(S["ff_silu"], 1)
                    for f in range(2):
                        act.wait_ge(S["ff_a"], plus(2 * (f0 + b) + f + 1, it, 4))
                        if it is None:
                            dst = aT[:, 0, 2 * b + f, :]
                        else:
                            dst = aT[:, 0, bass.ds(it * 4 + (2 * b + f), 1), :]
                        A(dst, work[:, 4 + 2 * q + f, :] if it is None else work[:, 4 + 2 * q + f:5 + 2 * q + f, :],
                          ACT.Copy).then_inc(S["ff_hi"], 1)
                job(0, 0, True)
                job(1, 1, True)
                with act.Fori(0, 4) as it:
                    job(2, 0, it=it)
                    job(3, 1, it=it)
                job(10, 0)
                nc.scalar.preload_act_table(ACT.Sqrt)
                out_phase(1 + 2 * layer, U_FO[layer], KF)

            ffn(0)

            hT_hi(2, [(kvT, 4), (hT_n, 2)])

            def v_copies(c):
                bank = (SET_A, SET_B, SET_A)[c]
                act.wait_ge(S["w_used"], U_KV + KD * (c + 1))
                for t in range(TT):
                    dst = v_tok0[:, t, 256:512] if c == 0 else v_all[:, c - 1, t, :]
                    A(dst, ps[:, bank + t, 256:512], ACT.Copy).then_inc(S["kv_v"], 1)

            def tp_dst(m):
                if m < 8:
                    return cT[0:HD, m, :], HD
                if m < 24:
                    c, g, part = (m - 8) // 8, (m - 8) % 8 // 2, m % 2
                    return kT2[:, c, g, part, :], P
                return qT2[:, m - 24, :], P

            def tp_items(lo_m, hi_m):
                for m in range(lo_m, hi_m):
                    if m % 2 == 1:
                        dst, n = tp_dst(m)
                        act.wait_ge(S["tp_full"], m + 1)
                        A(dst, ps[0:n, (SET_A if m < 8 else SET_B) + m % 4, :], ACT.Copy).then_inc(S["tp_act"], 1)

            for n in range(4, 12):
                hi(U_KV + n)
            v_copies(0)
            for n in range(12, 16):
                hi(U_KV + n)
            for n in range(16, 20):
                hi(U_KV + n)
            v_copies(1)
            tp_items(0, 8)
            act.wait_ge(S["nsa_in"], 16 * 4)
            A(gwhi[:], gw[:], ACT.Copy).then_inc(S["gw_hi"], 1)
            for n in range(20, 28):
                hi(U_KV + n)
            v_copies(2)
            act.wait_ge(S["shifted"], 16)
            for n in range(8):
                hi(U_Q0 + 4 + n)
                for m in range(4 * n, 4 * n + 4):
                    kv_i, lp = divmod(m, LP)
                    A(bT[:, 0, kv_i, lp, :].rearrange("p (g n) -> p g n", g=NG),
                      cT[:, kv_i * 4:kv_i * 4 + 4, 2 * lp:2 * lp + 481:16], ACT.Identity,
                      bias=pos_sb[:, kv_i, lp:lp + 1]).then_inc(S["b_hi"], 1)

            def q_copies(j, bank):
                act.wait_ge(S["w_used"], (U_Q0, U_Q1)[j] + KD)
                for t in range(TT):
                    A(q_tok[:, j, t, :], ps[:, bank + t, :], ACT.Copy, scale=HD ** -0.5).then_inc(S["q_copied"], 1)

            def qs_hi(j):
                act.wait_ge(S["rope_done"], 2 * (4 + j))
                for t in range(TT):
                    A(qs[:, t, :, 0, :], q_tok[:, j, t, :].rearrange("p (h d) -> p h d", h=8), ACT.Copy
                      ).then_inc(S["qs_hi"], 1)

            q_copies(0, SET_B)
            act.wait_ge(S["gate_full"], 1)
            A(gate_T[0:48, :], ps[0:48, SET_A, :], ACT.Sigmoid).then_inc(S["gate_sig"], 1)
            act.wait_ge(S["gate_T_full"], 1)
            A(gates[:].rearrange("p t h c -> p (t h c)"), ps[:, SET_A + 1, 0:192], ACT.Copy
              ).then_inc(S["gate_done"], 1)
            for n in range(16):
                hi(U_CMP + 4 + n)
                if n < 8:
                    c, t = divmod(n, TT)
                    act.wait_ge(S["rope_done"], 2 * (c + 2))
                    A(kd[:, c, t, :, 0, :].rearrange("p g (u d) -> p g u d", u=2),
                      k_tok[:, c, t, :].rearrange("p (g d) -> p g d", g=NG).unsqueeze(2)
                      .broadcast_to([P, NG, 2, HD]), ACT.Copy).then_inc(S["kd_hi"], 1)
                if n == 8:
                    qs_hi(0)
            act.wait_ge(S["w_used"], U_CMP + LP)
            act.wait_ge(S["rep_zero"], 1)
            for kv_i in range(2):
                A(hid[0:124, kv_i, :], ps[0:124, SET_A + kv_i, 0:256], ACT.Gelu_apprx_tanh
                  ).then_inc(S["hid_done"], 1)
            tp_items(8, 24)
            act.wait_ge(S["ck_full"], 1)
            A(ck2[:, 0, :, 0:NCMP], ps[:, SET_A, 0:124].rearrange("p (g n) -> p g n", g=NG), ACT.Copy
              ).then_inc(S["ck_hi"], 1)
            for n in range(8):
                hi(U_Q1 + 4 + n)
            q_copies(1, SET_A)
            tp_items(24, 32)
            qs_hi_wait = 32
            act.wait_ge(S["tp_full"], qs_hi_wait)
            qs_hi(1)
            tp_items(32, 40)
            for g in (1, 3):
                act.wait_ge(S["cT_full"], g + 1)
                A(cs_T[:, g, :], ps[:, SET_A + g, :], ACT.Copy).then_inc(S["cT_act"], 1)
            for i in range(TT):
                act.wait_ge(S["cs_sub"], i + 1)
                A(prob[:, i, :], prob[:, i, :], ACT.Exp).then_inc(S["cs_exp"], 1)
            for i in range(TT):
                act.wait_ge(S["cs_tp"], i + 1)
                A(probT[:, i, :], ps[:, i % 2, :], ACT.Copy).then_inc(S["cs_pT"], 1)

            def p_copy(n):
                w = (n // 32 + 1) * P
                act.wait_ge(S["pt_full"], n + 1)
                if n >= 4:
                    act.wait_ge(S["pv_done"], n - 3)
                A(probT[:, n % 4, 0:w], ps[:, 4 + n % 2, 0:w], ACT.Copy).then_inc(S["pt_act"], 1)

            for n in range(128 + T_LAG):
                if n >= T_LAG and by_act(n - T_LAG):
                    p_copy(n - T_LAG)
                if n < 128:
                    w = (n // 32 + 1) * P
                    act.wait_ge(S["max_done"], n + 1)
                    if n < 4:
                        act.wait_ge(S["cs_tp"], TT)
                    else:
                        act.wait_ge(S["pt_full"], n - 3)
                    A(prob[:, n % 4, 0:w], ps[:, n % 4, 0:w], ACT.Exp, bias=nmax[:, n:n + 1],
                      accum_out=lsum[:, n:n + 1]).then_inc(S["exp_done"], 1)

            def oT_hi(k):
                act.wait_ge(S["oT_psum"], k + 1)
                A(oT[:, 0, k, :], ps[:, SET_A + k % 4, :], ACT.Copy).then_inc(S["oT_hi"], 1)

            nc.scalar.preload_act_table(ACT.Sqrt)
            for k in range(4):
                oT_hi(k)
            out_phase(2, U_NO, KD, oT_hi)
            ffn(1)

        @block.vector
        def _(dve):
            V = nc.vector

            def lo(u, it=None, per=0):
                dve.wait_ge(S["w_hi"], plus(u + 1, it, per))
                V.tensor_tensor(wlo[:, u % RING, :], raw[:, u % RAW, :], whi[:, u % RING, :].bitcast(F32),
                                ALU.subtract).then_inc(S["w_lo"], 1)

            def normalise(j, t):
                dve.wait_ge(S["norm_std"], 4 * j + t + 1)
                V.reciprocal(rstd[:, j, t:t + 1], std[:, j, t:t + 1]).then_inc(S["norm_rstd"], 1)
                dve.wait_ge(S["norm_rstd"], 4 * j + t + 1)
                V.tensor_scalar(normed_v[:, t, :], xs[:, t, :], rstd[:, j, t:t + 1], None, ALU.mult
                                ).then_inc(S["normed"], 1)

            def hT_lo(j, dests):
                for k in range(KD):
                    dve.wait_ge(S["hT_hi"], 8 * j + k + 1)
                    for dst, gain in dests:
                        ins = V.scalar_tensor_tensor(
                            out=dst[:, 1, k, :], in0=ps[:, SET_B + k % 4, :], scalar=gains[:, gain, k:k + 1],
                            in1=dst[:, 0, k, :].bitcast(F32), op0=ALU.mult, op1=ALU.subtract)
                    ins.then_inc(S["hT_lo"], 1)

            def gained(i, half, t):
                V.tensor_tensor(normed_v[:, t, half * W:(half + 1) * W], ps[:, (SET_B, SET_A)[half] + t, :],
                                gain_row[:, half * W:(half + 1) * W], ALU.mult).then_inc(S["post_gain"], 1)

            def out_phase(i, u0, tiles, before=None):
                for n in range(4, 2 * tiles):
                    lo(u0 + n)
                    if before is not None and n < tiles:
                        before(n)
                    if n == tiles + 3:
                        dve.wait_ge(S["post_sq"], 8 * i + 4)
                        V.tensor_scalar(base[:, i, :], halves[:, i, 0, :], EPS, None, ALU.add
                                        ).then_inc(S["post_base"], 1)
                        dve.wait_ge(S["gain_in"], 16 * (i + 1))
                        for t in range(TT):
                            gained(i, 0, t)
                for t in range(TT + 1):
                    if t < TT:
                        dve.wait_ge(S["post_sq"], 8 * i + 5 + t)
                        gained(i, 1, t)
                        dve.wait_ge(S["post_std"], 4 * i + t + 1)
                        V.reciprocal(rstd[:, 4 + i, t:t + 1], std[:, 4 + i, t:t + 1]).then_inc(S["post_rstd"], 1)
                        dve.wait_ge(S["post_rstd"], 4 * i + t + 1)
                        dve.wait_ge(S["post_gain"], 8 * i + 5 + t)
                        V.scalar_tensor_tensor(out=xs[:, t, :], in0=normed_v[:, t, :],
                                               scalar=rstd[:, 4 + i, t:t + 1], in1=xs[:, t, :],
                                               op0=ALU.mult, op1=ALU.add).then_inc(S["x_ready"], 1)
                    if t >= 1 and i < 3:
                        normalise(i + 1, t - 1)
                if i < 3:
                    for n in range(4):
                        lo(u0 + 2 * tiles + n)

            V.memset(eps[:], EPS).then_inc(S["masks"], 1)
            for t in range(TT):
                normalise(0, t)
            for u in range(4):
                lo(u)
            dve.wait_ge(S["consts_in"], 32)
            hT_lo(0, [(hT_r, 0)])
            dve.wait_ge(S["tables_in"], 48)
            V.tensor_copy(causal_b[:], causal).then_inc(S["o_cent"], 1)

            with dve.Fori(0, 2) as it:
                for p in range(2):
                    u0 = 24 * p
                    xb, yb = (SET_A, SET_B) if p == 0 else (SET_B, SET_A)

                    def n4(c):
                        return it * 8 + (4 * p + c)

                    def n1(c=1):
                        return it * 2 + (p + c)
                    for n in range(4, 12):
                        lo(u0 + n, it, 48)
                    dve.wait_ge(S["w_used"], it * 48 + (u0 + 8))
                    dve.wait_ge(S["y_done"], n4(1))
                    for m in range(2):
                        a, b = ps[:, xb + 2 * m, :], ps[:, xb + 2 * m + 1, :]
                        for n, (src, f) in enumerate(((a, 0), (b, 1), (a, 1), (b, 0))):
                            V.tensor_tensor(work[:, 4 * m + n, :], src, rot_tab[:, f, :], ALU.mult
                                            ).then_inc(S["rot_prod"], 1)
                        dve.wait_ge(S["rot_prod"], it * 16 + (8 * p + 4 * m + 4))
                        V.tensor_tensor(work[:, 4 * m, :], work[:, 4 * m, :], work[:, 4 * m + 1, :], ALU.subtract
                                        ).then_inc(S["rot_sum"], 1)
                        V.tensor_tensor(work[:, 4 * m + 2, :], work[:, 4 * m + 2, :], work[:, 4 * m + 3, :],
                                        ALU.add).then_inc(S["rot_sum"], 1)
                    for m in range(4):
                        dve.wait_ge(S["qk_hi"], n4(m + 1))
                        V.tensor_tensor(qk_r[:, 1, m // 2, m % 2, :], work[:, 4 * (m // 2) + 2 * (m % 2), :],
                                        qk_r[:, 0, m // 2, m % 2, :].bitcast(F32), ALU.subtract
                                        ).then_inc(S["qk_lo"], 1)
                    for n in range(12, 20):
                        lo(u0 + n, it, 48)
                    for t in range(TT):
                        dve.wait_ge(S["v_hi"], n4(t + 1))
                        V.tensor_tensor(v_r[:, 1, t, :], ps[:, yb + t, :], v_r[:, 0, t, :].bitcast(F32),
                                        ALU.subtract).then_inc(S["v_lo"], 1)
                    dve.wait_ge(S["s_full"], n1())
                    for j in range(TT):
                        w = T - j * P
                        V.tensor_tensor(work[:, j, 0:w], ps[:, xb + j, 0:w],
                                        decay[:, bass.ds(it * 2 * T + p * T, w)], ALU.mult
                                        ).then_inc(S["s_dec"], 1)
                    at_col = 0
                    for j in range(TT):
                        w = T - j * P
                        dve.wait_ge(S["s_hi"], n4(j + 1))
                        V.tensor_tensor(dec_r[:, 1, at_col:at_col + w], work[:, j, 0:w],
                                        dec_r[:, 0, at_col:at_col + w].bitcast(F32), ALU.subtract
                                        ).then_inc(S["s_lo"], 1)
                        at_col += w
                    for n in range(20, 28):
                        lo(u0 + n, it, 48)
                    dve.wait_ge(S["o_full"], n1())
                    for t in range(TT):
                        V.bn_stats(bn[:, t, :], ps[:, xb + t, :]).then_inc(S["o_bn"], 1)
                    for t in range(TT):
                        dve.wait_ge(S["o_bn"], n4(t + 1))
                        dve.nop(nofuse=True)
                        V.bn_aggr(mv[:, t, :], bn[:, t, :]).then_inc(S["o_mv"], 1)
                    dve.wait_ge(S["o_mv"], n4(TT))
                    V.tensor_scalar(gvar[:, 0, :], mv[:, :, 1], EPS, None, ALU.add).then_inc(S["o_var"], 1)
                    dve.wait_ge(S["o_std"], n1())
                    V.reciprocal(gvar[:, 2, :], gvar[:, 1, :]).then_inc(S["o_rstd"], 1)
                    dve.wait_ge(S["o_rstd"], n1())
                    for t in range(TT):
                        V.tensor_scalar(work[:, 4 + t, :], ps[:, xb + t, :], mv[:, t, 0:1], gvar[:, 2, t:t + 1],
                                        ALU.subtract, ALU.mult).then_inc(S["o_cent"], 1)

            def yT_lo(k):
                dve.wait_ge(S["yT_hi"], k + 1)
                V.scalar_tensor_tensor(out=yT[:, 1, k, :], in0=ps[:, SET_A + k % 4, :],
                                       scalar=ret_gain[:, k:k + 1], in1=yT[:, 0, k, :].bitcast(F32),
                                       op0=ALU.mult, op1=ALU.subtract).then_inc(S["yT_lo"], 1)

            for k in range(4):
                yT_lo(k)
            out_phase(0, U_RO, 16, yT_lo)

            def ffn(layer):
                u0 = U_FI[layer]
                hT_lo(1 + 2 * layer, [(hT_f, 1 + 2 * layer)])
                f0 = FJ * layer

                def job(b, par, it=None):
                    bank = SET_A if par % 2 == 0 else SET_B
                    q = par % 2
                    for n in range(4, 12):
                        lo(u0 + 8 * b + n, it, 16)
                    for f in range(2):
                        dve.wait_ge(S["ff_silu"], plus(2 * (f0 + b) + f + 1, it, 4))
                        V.tensor_tensor(work[:, 4 + 2 * q + f, :], ps[:, bank + 2 + f, :], work[:, 2 * q + f, :],
                                        ALU.mult).then_inc(S["ff_a"], 1)
                    for f in range(2):
                        dve.wait_ge(S["ff_hi"], plus(2 * (f0 + b) + f + 1, it, 4))
                        if it is None:
                            a_hi, a_lo, src = aT[:, 0, 2 * b + f, :], aT[:, 1, 2 * b + f, :], work[:, 4 + 2 * q + f, :]
                        else:
                            k = bass.ds(it * 4 + (2 * b + f), 1)
                            a_hi, a_lo, src = aT[:, 0, k, :], aT[:, 1, k, :], work[:, 4 + 2 * q + f:5 + 2 * q + f, :]
                        V.tensor_tensor(a_lo, src, a_hi.bitcast(F32), ALU.subtract).then_inc(S["ff_lo"], 1)
                job(0, 0)
                job(1, 1)
                with dve.Fori(0, 4) as it:
                    job(2, 0, it)
                    job(3, 1, it)
                job(10, 0)
                out_phase(1 + 2 * layer, U_FO[layer], KF)

            ffn(0)
            hT_lo(2, [(kvT, 4), (hT_n, 2)])

            def rope(buf, heads, r):
                v = buf.rearrange("p t (h d) -> p t h d", d=HD)
                a, b = v[:, :, :, 0:ROT], v[:, :, :, ROT:2 * ROT]
                cos = rope_tab[:, 0].unsqueeze(2).broadcast_to([P, TT, heads, ROT])
                sin = rope_tab[:, 1].unsqueeze(2).broadcast_to([P, TT, heads, ROT])
                t = [rope_t[:, n, 0:TT * heads * ROT].rearrange("p (t h e) -> p t h e", t=TT, h=heads)
                     for n in range(4)]
                for n, (src, f) in enumerate(((a, cos), (b, sin), (a, sin), (b, cos))):
                    V.tensor_tensor(t[n], src, f, ALU.mult).then_inc(S["rope_prod"], 1)
                dve.wait_ge(S["rope_prod"], 4 * (r + 1))
                V.tensor_tensor(a, t[0], t[1], ALU.subtract).then_inc(S["rope_done"], 1)
                V.tensor_tensor(b, t[2], t[3], ALU.add).then_inc(S["rope_done"], 1)

            def kv_job(c):
                bank = (SET_A, SET_B, SET_A)[c]
                dst = v_tok0[:, :, 0:256] if c == 0 else k_tok[:, c - 1]
                for t in range(TT):
                    dve.wait_ge(S["kv_v"], 4 * c + t + 1)
                    V.tensor_copy(dst[:, t, :], ps[:, bank + t, 0:256]).then_inc(S["kv_k"], 1)
                dve.wait_ge(S["kv_k"], 4 * (c + 1))
                rope(dst, NG, c)

            def tp_items(lo_m, hi_m):
                for m in range(lo_m, hi_m):
                    if m % 2 == 0:
                        if m < 8:
                            dst, n = cT[0:HD, m, :], HD
                        elif m < 24:
                            dst, n = kT2[:, (m - 8) // 8, (m - 8) % 8 // 2, 0, :], P
                        else:
                            dst, n = qT2[:, m - 24, :], P
                        dve.wait_ge(S["tp_full"], m + 1)
                        V.tensor_copy(dst, ps[0:n, (SET_A if m < 8 else SET_B) + m % 4, :]).then_inc(S["tp_dve"], 1)

            for n in range(4, 12):
                lo(U_KV + n)
            kv_job(0)
            for n in range(12, 20):
                lo(U_KV + n)
            kv_job(1)
            tp_items(0, 8)
            dve.wait_ge(S["gw_hi"], 1)
            V.tensor_tensor(gwlo[:], gw[:], gwhi[:].bitcast(F32), ALU.subtract).then_inc(S["gw_lo"], 1)
            for n in range(20, 28):
                lo(U_KV + n)
            kv_job(2)
            for n in range(8):
                lo(U_Q0 + 4 + n)
                for m in range(4 * n, 4 * n + 4):
                    kv_i, lp = divmod(m, LP)
                    dve.wait_ge(S["b_hi"], m + 1)
                    V.scalar_tensor_tensor(
                        out=bT[:, 1, kv_i, lp, :].rearrange("p (g n) -> p g n", g=NG),
                        in0=cT[:, kv_i * 4:kv_i * 4 + 4, 2 * lp:2 * lp + 481:16],
                        scalar=pos_sb[:, kv_i, lp:lp + 1],
                        in1=bT[:, 0, kv_i, lp, :].bitcast(F32).rearrange("p (g n) -> p g n", g=NG),
                        op0=ALU.add, op1=ALU.subtract).then_inc(S["b_lo"], 1)

            def qs_lo(j):
                for t in range(TT):
                    dve.wait_ge(S["qs_hi"], 4 * j + t + 1)
                    V.tensor_tensor(qs[:, t, :, 1, :], q_tok[:, j, t, :].rearrange("p (h d) -> p h d", h=8),
                                    qs[:, t, :, 0, :].bitcast(F32), ALU.subtract).then_inc(S["qs_lo"], 1)

            dve.wait_ge(S["q_copied"], 4)
            rope(q_tok[:, 0], 8, 3)
            for n in range(16):
                lo(U_CMP + 4 + n)
                if n < 8:
                    c, t = divmod(n, TT)
                    dve.wait_ge(S["kd_hi"], n + 1)
                    V.tensor_tensor(kd[:, c, t, :, 1, :].rearrange("p g (u d) -> p g u d", u=2),
                                    k_tok[:, c, t, :].rearrange("p (g d) -> p g d", g=NG).unsqueeze(2)
                                    .broadcast_to([P, NG, 2, HD]),
                                    kd[:, c, t, :, 0, :].bitcast(F32).rearrange("p g (u d) -> p g u d", u=2),
                                    ALU.subtract).then_inc(S["kd_lo"], 1)
                if n == 8:
                    qs_lo(0)
            tp_items(8, 24)
            dve.wait_ge(S["rep_zero"], 1)
            dve.wait_ge(S["hid_T_full"], 1)
            V.tensor_copy(hid_k, ps[:, SET_A + 2, 0:248].rearrange("p (h n) -> p h n", h=2)
                          ).then_inc(S["hid_k_done"], 1)
            for ht in range(2):
                V.tensor_copy(hid_rep[:, ht, :, :, 0:NCMP],
                              ps[:, SET_A + 2, 248 + 124 * ht:372 + 124 * ht]
                              .rearrange("p (g n) -> p g n", g=NG).unsqueeze(2)
                              .broadcast_to([P, NG, REP, NCMP])).then_inc(S["rep_done"], 1)
            dve.wait_ge(S["ck_hi"], 1)
            V.tensor_tensor(ck2[:, 1, :, 0:NCMP], ps[:, SET_A, 0:124].rearrange("p (g n) -> p g n", g=NG),
                            ck2[:, 0, :, 0:NCMP].bitcast(F32), ALU.subtract).then_inc(S["ck_lo"], 1)
            dve.wait_ge(S["cv_full"], 1)
            for g in range(NG):
                V.tensor_tensor(cv_bd[:, g], ps[:, SET_A + 1, g * HD:(g + 1) * HD].unsqueeze(1)
                                .broadcast_to([P, REP, HD]),
                                diag4.unsqueeze(2).broadcast_to([P, REP, HD]), ALU.mult
                                ).then_inc(S["cv_done"], 1)
            for n in range(8):
                lo(U_Q1 + 4 + n)
            dve.wait_ge(S["q_copied"], 8)
            rope(q_tok[:, 1], 8, 4)
            tp_items(24, 32)
            qs_lo(1)
            tp_items(32, 40)
            for g in (0, 2):
                dve.wait_ge(S["cT_full"], g + 1)
                V.tensor_copy(cs_T[:, g, :], ps[:, SET_A + g, :]).then_inc(S["cT_dve"], 1)
            for i in range(TT):
                sc = prob[:, i, :].rearrange("p (h n) -> p h n", h=NH)
                dve.wait_ge(S["cs_full"], i + 1)
                V.tensor_tensor(sc, ps[:, SET_B + i, :].rearrange("p (h n) -> p h n", h=NH),
                                cmask[:, i].unsqueeze(1).broadcast_to([P, NH, CB]), ALU.add
                                ).then_inc(S["cs_masked"], 1)
                dve.wait_ge(S["cs_masked"], i + 1)
                V.tensor_reduce(cst[:, 0, i, :], sc, AX.X, ALU.max).then_inc(S["cs_max"], 1)
                dve.wait_ge(S["cs_max"], i + 1)
                V.tensor_tensor(sc, sc, cst[:, 0, i, :].unsqueeze(2).broadcast_to([P, NH, CB]), ALU.subtract
                                ).then_inc(S["cs_sub"], 1)
            for i in range(TT):
                sc = prob[:, i, :].rearrange("p (h n) -> p h n", h=NH)
                dve.wait_ge(S["cs_exp"], i + 1)
                V.tensor_reduce(cst[:, 1, i, :], sc, AX.X, ALU.add).then_inc(S["cs_sum"], 1)
                dve.wait_ge(S["cs_sum"], i + 1)
                V.reciprocal(cst[:, 2, i, :], cst[:, 1, i, :]).then_inc(S["cs_inv"], 1)
                dve.wait_ge(S["cs_inv"], i + 1)
                V.scalar_tensor_tensor(out=cst[:, 3, i, :], in0=cst[:, 2, i, :], scalar=some[:, i:i + 1],
                                       in1=gates[:, i, :, 0], op0=ALU.mult, op1=ALU.mult
                                       ).then_inc(S["cs_coef"], 1)
            for i in range(TT):
                dve.wait_ge(S["cs_coef"], i + 1)
                dve.wait_ge(S["cs_pv"], i + 1)
                for b in range(2):
                    V.tensor_tensor(o_acc[:, i, b * W:(b + 1) * W].rearrange("p (h d) -> p h d", h=8),
                                    ps[:, 2 + 4 * (i % 2) + b, :].rearrange("p (h d) -> p h d", h=8),
                                    cst[:, 3, i, 8 * b:8 * b + 8].unsqueeze(2).broadcast_to([P, 8, HD]), ALU.mult
                                    ).then_inc(S["o_cmp"], 1)

            def p_copy(n):
                w = (n // 32 + 1) * P
                dve.wait_ge(S["pt_full"], n + 1)
                if n >= 4:
                    dve.wait_ge(S["pv_done"], n - 3)
                V.tensor_copy(probT[:, n % 4, 0:w], ps[:, 4 + n % 2, 0:w]).then_inc(S["pt_dve"], 1)

            def scale_out(ig):
                i, g = divmod(ig, NG)
                c = slice(8 * ig, 8 * ig + 8)
                dve.wait_ge(S["exp_done"], 8 * (ig + 1))
                V.reciprocal(linv[:, c], lsum[:, c]).then_inc(S["l_inv"], 1)
                dve.wait_ge(S["l_inv"], ig + 1)
                V.tensor_tensor(linv[:, c].rearrange("p (b r) -> p b r", b=2),
                                linv[:, c].rearrange("p (b r) -> p b r", b=2),
                                gates[:, i, g * REP:(g + 1) * REP, 1:3].rearrange("p r b -> p b r"), ALU.mult
                                ).then_inc(S["a_coef"], 1)
                dve.wait_ge(S["a_coef"], ig + 1)
                dve.wait_ge(S["pv_done"], 8 * (ig + 1))
                if ig >= 1:
                    dve.wait_ge(S["o_added"], ig)
                V.tensor_tensor(otmp.rearrange("p b (r d) -> p (b r) d", r=REP),
                                ps[:, 6 + ig % 2, :].rearrange("p (u d) -> p u d", d=HD),
                                linv[:, c].unsqueeze(2).broadcast_to([P, 8, HD]), ALU.mult
                                ).then_inc(S["a_scaled"], 1)

            for n in range(128 + V_LAG + 1):
                if n < 128:
                    w = (n // 32 + 1) * P
                    dve.wait_ge(S["sc_full"], n + 1)
                    V.tensor_reduce(nmax[:, n:n + 1], ps[:, n % 4, 0:w], AX.X, ALU.max, negate=True
                                    ).then_inc(S["max_done"], 1)
                if T_LAG <= n < 128 + T_LAG and not by_act(n - T_LAG):
                    p_copy(n - T_LAG)
                if n >= V_LAG + 8 and (n - V_LAG) % 8 == 0:
                    scale_out((n - V_LAG) // 8 - 1)

            def oT_lo(k):
                dve.wait_ge(S["oT_hi"], k + 1)
                V.tensor_tensor(oT[:, 1, k, :], ps[:, SET_A + k % 4, :], oT[:, 0, k, :].bitcast(F32),
                                ALU.subtract).then_inc(S["oT_lo"], 1)

            for k in range(4):
                oT_lo(k)
            out_phase(2, U_NO, KD, oT_lo)
            ffn(1)

        @block.tensor
        def _(pe):
            M = nc.tensor.matmul

            def unit(u, it=None, per=0):
                pe.wait_ge(S["w_lo"], plus(u + 1, it, per))

            def rows(bank, h, k, u, t, start, stop):
                r = u % RING
                a_hi, a_lo = h[:, 0, k, t * P:(t + 1) * P], h[:, 1, k, t * P:(t + 1) * P]
                M(ps[:, bank + t, :], a_hi, whi[:, r, :], start=start, stop=False)
                M(ps[:, bank + t, :], a_hi, wlo[:, r, :], start=False, stop=False)
                return M(ps[:, bank + t, :], a_lo, whi[:, r, :], start=False, stop=stop)

            def by_token(bank, h, k, u, start, stop):
                for t in range(TT):
                    last = rows(bank, h, k, u, t, start, stop)
                last.then_inc(S["w_used"], 1)

            def by_feature(bank, h, k, u, start, stop):
                r = u % RING
                for f in range(4):
                    c = slice(f * P, (f + 1) * P)
                    M(ps[:, bank + f, :], whi[:, r, c], h[:, 0, k, :], start=start, stop=False)
                    M(ps[:, bank + f, :], whi[:, r, c], h[:, 1, k, :], start=False, stop=False)
                    last = M(ps[:, bank + f, :], wlo[:, r, c], h[:, 0, k, :], start=False, stop=stop)
                last.then_inc(S["w_used"], 1)

            def job(kind, bank, h, u0, it=None, per=0, parts=None):
                for k in range(KD):
                    unit(u0 + k, it, per)
                    if parts is not None:
                        pe.wait_ge(S["hT_lo"], parts + k + 1)
                    kind(bank, h, k, u0 + k, k == 0, k == KD - 1)

            def h_tile(k, t):
                return nc.tensor.transpose(ps[:, SET_B + k % 4, t * P:(t + 1) * P],
                                           normed_v[:, t, k * P:(k + 1) * P], ident)

            def pre_norm(j):
                if j == 0:
                    pe.wait_ge(S["consts_in"], 32)
                for t in range(TT):
                    pe.wait_ge(S["normed"], 4 * j + t + 1)
                    for k in range(4):
                        last = h_tile(k, t)
                        if t == TT - 1:
                            last.then_inc(S["hT_psum"], 1)
                for k in range(4, KD):
                    pe.wait_ge(S["hT_lo"], 8 * j + k - 3)
                    for t in range(TT):
                        last = h_tile(k, t)
                    last.then_inc(S["hT_psum"], 1)

            def turn(src, k, name):
                for t in range(TT):
                    last = nc.tensor.transpose(ps[:, SET_A + k % 4, t * P:(t + 1) * P],
                                               src[:, t, k * P:(k + 1) * P], ident)
                last.then_inc(S[name + "_psum"], 1)

            def out_proj(h, u0, tiles, name, base, src=None):
                for half in range(2):
                    bank = (SET_B, SET_A)[half]
                    for k in range(tiles - 4 * half):
                        u = u0 + half * tiles + k
                        unit(u)
                        if half == 0:
                            pe.wait_ge(S[name + "_lo"], base + k + 1)
                        elif k == 0:
                            pe.wait_ge(S[name + "_lo"], base + tiles)
                        by_token(bank, h, k, u, k == 0, k == tiles - 1)
                        if src is not None and half == 0 and k + 4 < tiles:
                            turn(src, k + 4, name)
                unit(u0 + 2 * tiles - 1)
                for t in range(TT):
                    for k in range(tiles - 4, tiles):
                        last = rows(SET_A, h, k, u0 + tiles + k, t, k == 0, k == tiles - 1)
                        if t == TT - 1:
                            last.then_inc(S["w_used"], 1)
                    if t < TT - 1:
                        last.then_inc(S["tile_out"], 1)

            pre_norm(0)
            with pe.Fori(0, 2) as it:
                for p in range(2):
                    u0 = 24 * p
                    xb, yb = (SET_A, SET_B) if p == 0 else (SET_B, SET_A)

                    def n4(c):
                        return it * 8 + (4 * p + c)
                    if p == 1:
                        pe.wait_ge(S["g_silu"], n4(0))
                    job(by_feature, xb, hT_r, u0, it, 48, parts=0)
                    pe.wait_ge(S["o_cent"], n4(1))
                    job(by_token, yb, hT_r, u0 + 8, it, 48)
                    pe.wait_ge(S["qk_lo"], n4(4))
                    for j in range(TT):
                        for n, (a, b) in enumerate(((0, 0), (0, 1), (1, 0))):
                            for d in range(2):
                                last = M(ps[:, xb + j, 0:T - j * P], qk_r[:, a, 1, d, j * P:(j + 1) * P],
                                         qk_r[:, b, 0, d, j * P:T], start=(n == 0 and d == 0),
                                         stop=(n == 2 and d == 1))
                    last.then_inc(S["s_full"], 1)
                    pe.wait_ge(S["v_lo"], n4(4))
                    job(by_token, yb, hT_r, u0 + 16, it, 48)
                    pe.wait_ge(S["s_lo"], n4(4))
                    for i in range(TT):
                        for j in range(i + 1):
                            c0 = j * T - P * (j * (j - 1) // 2) + (i - j) * P
                            for n, (a, b) in enumerate(((0, 0), (0, 1), (1, 0))):
                                last = M(ps[:, xb + i, :], dec_r[:, a, c0:c0 + P], v_r[:, b, j, :],
                                         start=(j == 0 and n == 0), stop=(j == i and n == 2))
                    last.then_inc(S["o_full"], 1)
                pe.wait_ge(S["g_silu"], it * 8 + 8)

            pe.wait_ge(S["y_done"], 13)
            for k in range(4):
                turn(y, k, "yT")
            pe.wait_ge(S["o_cent"], 17)
            pe.wait_ge(S["y_done"], 17)
            out_proj(yT, U_RO, 16, "yT", 0, y)

            def ffn(layer):
                j = 1 + 2 * layer
                pre_norm(j)
                u0, f0 = U_FI[layer], FJ * layer
                job(by_feature, SET_A, hT_f, u0, parts=8 * j)
                job(by_feature, SET_B, hT_f, u0 + 8)
                with pe.Fori(0, 4) as it:
                    for q in range(2):
                        pe.wait_ge(S["ff_a"], it * 4 + 2 * (f0 + q + 1))
                        job(by_feature, (SET_A, SET_B)[q], hT_f, u0 + 16 + 8 * q, it, 16)
                pe.wait_ge(S["ff_a"], 2 * (f0 + 9))
                job(by_feature, SET_A, hT_f, u0 + 80)
                pe.wait_ge(S["ff_a"], 2 * (f0 + 10))
                out_proj(aT, U_FO[layer], KF, "ff", KF * layer)

            ffn(0)

            pre_norm(2)
            job(by_token, SET_A, kvT, U_KV, parts=16)
            job(by_token, SET_B, kvT, U_KV + 8)

            def items(lo_m, hi_m):
                for m in range(lo_m, hi_m):
                    if m - 4 >= lo_m:
                        pe.wait_ge(S["tp_act" if m % 2 else "tp_dve"], (m - 4) // 2 + 1)
                    for t in range(TT):
                        if m < 8:
                            src, n = v_tok0[:, t, (m // 4) * 256 + (m % 4) * HD:][:, 0:HD], HD
                        elif m < 24:
                            src, n = kd[:, (m - 8) // 8, t, (m - 8) % 8 // 2, m % 2, :].bitcast(F32), P
                        else:
                            src, n = qs[:, t, (m - 24) % 8].rearrange("p a d -> p (a d)").bitcast(F32), P
                        last = nc.tensor.transpose(ps[0:n, (SET_A if m < 8 else SET_B) + m % 4, t * P:(t + 1) * P],
                                                   src, ident)
                    last.then_inc(S["tp_full"], 1)

            pe.wait_ge(S["rope_done"], 2)
            items(0, 8)
            pe.wait_ge(S["tp_act"], 4)
            pe.wait_ge(S["tp_dve"], 4)
            job(by_token, SET_A, kvT, U_KV + 16)
            pe.wait_ge(S["kv_k"], 8)
            job(by_token, SET_B, hT_n, U_Q0)
            pe.wait_ge(S["kv_k"], 12)
            pe.wait_ge(S["gw_lo"], 1)
            for k in range(KD):
                o = ps[0:48, SET_A, :]
                M(o, gwhi[:, k, :], hT_n[:, 0, k, :], start=(k == 0), stop=False)
                M(o, gwhi[:, k, :], hT_n[:, 1, k, :], start=False, stop=False)
                last = M(o, gwlo[:, k, :], hT_n[:, 0, k, :], start=False, stop=(k == KD - 1))
            last.then_inc(S["gate_full"], 1)
            pe.wait_ge(S["gate_sig"], 1)
            for t in range(TT):
                last = nc.tensor.transpose(ps[:, SET_A + 1, 48 * t:48 * t + 48], gate_T[0:48, t * P:(t + 1) * P],
                                           ident[0:48, 0:48])
            last.then_inc(S["gate_T_full"], 1)
            pe.wait_ge(S["gate_done"], 1)
            for kv_i in range(2):
                for n in range(8):
                    u = U_CMP + 8 * kv_i + n
                    unit(u)
                    pe.wait_ge(S["b_lo"], 16 * kv_i + 2 * n + 2)
                    r = u % RING
                    for c in range(2):
                        lp = 2 * n + c
                        o = ps[0:124, SET_A + kv_i, 0:256]
                        w = slice(c * 256, (c + 1) * 256)
                        M(o, bT[:, 0, kv_i, lp, :], whi[:, r, w], start=(lp == 0), stop=False)
                        M(o, bT[:, 0, kv_i, lp, :], wlo[:, r, w], start=False, stop=False)
                        last = M(o, bT[:, 1, kv_i, lp, :], whi[:, r, w], start=False, stop=(lp == LP - 1))
                    last.then_inc(S["w_used"], 1)
            pe.wait_ge(S["kd_lo"], 8)
            pe.wait_ge(S["q_copied"], 4)
            items(8, 24)
            pe.wait_ge(S["hid_done"], 2)
            for kv_i in range(2):
                for ht in range(2):
                    c = 248 * kv_i + 124 * ht
                    last = nc.tensor.transpose(ps[:, SET_A + 2, c:c + 124],
                                               hid[0:124, kv_i, ht * P:(ht + 1) * P], ident[0:124, 0:124])
            last.then_inc(S["hid_T_full"], 1)
            pe.wait_ge(S["nsa_in"], 16 * 4)
            pe.wait_ge(S["hid_k_done"], 1)
            for ht in range(2):
                last = M(ps[:, SET_A, 0:124], w2k[:, ht].rearrange("p u d -> p (u d)"), hid_k[:, ht, :],
                         start=(ht == 0), stop=(ht == 1))
            last.then_inc(S["ck_full"], 1)
            pe.wait_ge(S["rep_done"], 2)
            for g in range(NG):
                for ht in range(2):
                    last = M(ps[:, SET_A + 1, g * HD:(g + 1) * HD], hid_rep[:, ht, g].rearrange("p r n -> p (r n)"),
                             w2v[:, ht, :], start=(ht == 0), stop=(ht == 1))
            last.then_inc(S["cv_full"], 1)
            pe.wait_ge(S["ck_lo"], 1)
            pe.wait_ge(S["cv_done"], 4)
            job(by_token, SET_A, hT_n, U_Q1)
            pe.wait_ge(S["qs_lo"], 4)
            pe.wait_ge(S["tp_act"], 12)
            pe.wait_ge(S["tp_dve"], 12)
            items(24, 32)
            pe.wait_ge(S["q_copied"], 8)
            pe.wait_ge(S["qs_lo"], 8)
            pe.wait_ge(S["tp_act"], 16)
            pe.wait_ge(S["tp_dve"], 16)
            items(32, 40)
            pe.wait_ge(S["ckz_done"], 2 * REP)
            pe.wait_ge(S["tp_act"], 20)
            pe.wait_ge(S["tp_dve"], 20)
            for g in range(NG):
                for r in range(REP):
                    hd = g * REP + r
                    for part in range(2):
                        last = M(ps[:, SET_A + g, :], ckz[:, part, g, r, :], qT2[:, hd, :],
                                 start=(r == 0 and part == 0), stop=(r == REP - 1 and part == 1))
                last.then_inc(S["cT_full"], 1)
            pe.wait_ge(S["cT_act"], 2)
            pe.wait_ge(S["cT_dve"], 2)
            for i in range(TT):
                for g in range(NG):
                    last = nc.tensor.transpose(ps[:, SET_B + i, g * P:(g + 1) * P], cs_T[:, g, i * P:(i + 1) * P],
                                               ident)
                last.then_inc(S["cs_full"], 1)
            for i in range(TT):
                pe.wait_ge(S["cs_exp"], i + 1)
                if i >= 2:
                    pe.wait_ge(S["cs_pT"], i - 1)
                for g in range(NG):
                    last = nc.tensor.transpose(ps[:, i % 2, g * P:(g + 1) * P], prob[:, i, g * P:(g + 1) * P],
                                               ident)
                last.then_inc(S["cs_tp"], 1)
            for i in range(TT):
                pe.wait_ge(S["cs_pT"], i + 1)
                if i >= 2:
                    pe.wait_ge(S["o_cmp"], 2 * (i - 1))
                for g in range(NG):
                    last = M(ps[:, 2 + 4 * (i % 2) + g // 2, (g % 2) * 256:(g % 2) * 256 + 256],
                             probT[:, i, g * P:(g + 1) * P],
                             cv_bd[:, g].rearrange("p r d -> p (r d)"), start=True, stop=True)
                last.then_inc(S["cs_pv"], 1)

            def where(n):
                ig, u = divmod(n, 8)
                i, g = divmod(ig, NG)
                return i, g, u // REP, u % REP, ig, u

            def scores(n):
                i, g, b, r, ig, u = where(n)
                w = (i + 1) * P
                if n >= 4:
                    pe.wait_ge(S["exp_done"], n - 3)
                q = qT2[:, g * REP + r, i * P:(i + 1) * P]
                M(ps[:, n % 4, 0:w], q, kT2[:, b, g, 0, 0:w], start=True, stop=False)
                M(ps[:, n % 4, 0:w], q, kT2[:, b, g, 1, 0:w], start=False, stop=False)
                M(ps[:, n % 4, w - P:w], ident_b[:], causal_b[:], start=False, stop=True).then_inc(S["sc_full"], 1)

            def copied(n):
                pe.wait_ge(S["pt_act" if by_act(n) else "pt_dve"], copies(n, by_act(n)))

            def turn_probs(n):
                pe.wait_ge(S["exp_done"], n + 1)
                if n >= 2:
                    copied(n - 2)
                for j in range(n // 32 + 1):
                    last = nc.tensor.transpose(ps[:, 4 + n % 2, j * P:(j + 1) * P], prob[:, n % 4, j * P:(j + 1) * P],
                                               ident)
                last.then_inc(S["pt_full"], 1)

            def values(n):
                i, g, b, r, ig, u = where(n)
                copied(n)
                if u == 0 and ig >= 2:
                    pe.wait_ge(S["a_scaled"], ig - 1)
                for j in range(i + 1):
                    last = M(ps[:, 6 + ig % 2, u * HD:(u + 1) * HD], probT[:, n % 4, j * P:(j + 1) * P],
                             v_all[:, b, j, g * HD:(g + 1) * HD], start=(j == 0), stop=(j == i))
                last.then_inc(S["pv_done"], 1)

            pe.wait_ge(S["cs_masked"], TT)
            pe.wait_ge(S["cs_pT"], TT)
            pe.wait_ge(S["o_cmp"], 2 * TT)
            for n in range(128 + V_LAG):
                if n < 128:
                    scores(n)
                if T_LAG <= n < 128 + T_LAG:
                    turn_probs(n - T_LAG)
                if n >= V_LAG:
                    values(n - V_LAG)
            pe.wait_ge(S["o_added"], TT * NG)
            for k in range(4):
                turn(o_acc, k, "oT")
            out_proj(oT, U_NO, KD, "oT", 0, o_acc)
            ffn(1)


_INS = ['x', 'norms', 'ret_w_in', 'ret_w_out', 'nsa_w_in', 'nsa_w_out', 'w_kv', 'cmp_w1_k', 'cmp_w2_k', 'cmp_w1_v', 'cmp_w2_v', 'ffn_w_in', 'ffn_w_out']
_OUTS = [((1, T, D), 'float32')]


def kernel(**inputs):
    import numpy as _np
    import concourse.bacc as _bacc
    from concourse import mybir as _mybir
    from concourse.bass_utils import run_bass_kernel_spmd as _run

    nc = _bacc.Bacc("TRN2", target_bir_lowering=False, num_devices=1)
    arrays, args = {}, []
    feeds = [(name, _np.ascontiguousarray(inputs[name])) for name in _INS]
    feeds.append(("feature_columns", lay_out_columns(*(_np.asarray(inputs[n]) for n in (
        "norms", "kv_norm", "ret_gn", "cmp_pos_k", "cmp_pos_v")))))
    feeds += shape_constants().items()
    for name, a in feeds:
        arrays[f"in_{name}_dram"] = a
        args.append(nc.dram_tensor(f"in_{name}_dram", a.shape, _mybir.dt.from_np(a.dtype), kind="ExternalInput").ap())
    for i, (shape, dtype) in enumerate(_OUTS):
        dt = _mybir.dt.from_np(_np.dtype(dtype))
        args.append(nc.dram_tensor(f"out_{i}_dram", shape, dt, kind="ExternalOutput").ap())
    yoco_kernel(nc, *args)
    r = _run(nc, [arrays], core_ids=[0])
    got = tuple(r.results[0][f"out_{i}_dram"] for i in range(len(_OUTS)))
    return got[0]
```

```python
from contextlib import ExitStack

import numpy as np

import concourse.bass as bass
from concourse import mybir

F32 = mybir.dt.float32
F32R = mybir.dt.float32r
BF16 = mybir.dt.bfloat16
ALU = mybir.AluOpType
ACT = mybir.ActivationFunctionType
AX = mybir.AxisListType

P = 128
D = 1024
T = 512
TT = T // P
KD = D // P
W = 512
RH, DK, DV = 4, 256, 512
NH, NG, REP, HD = 16, 4, 4, 64
FF = 2816
FJ = FF // 256
KF = FF // P
NCMP = 31
CB = 32
LP = 16
ROT = 8
EPS = 1e-6
NEG = -1e30
RAW = 8
RING = 4

U_RET = 0
U_RO = U_RET + RH * 3 * KD
U_FI = [U_RO + 2 * 16, 0]
U_FO = [U_FI[0] + FJ * KD, 0]
U_KV = U_FO[0] + 2 * KF
U_Q0 = U_KV + 3 * KD
U_Q1 = U_Q0 + KD
U_CMP = U_Q1 + KD
U_NO = U_CMP + LP
U_FI[1] = U_NO + 2 * KD
U_FO[1] = U_FI[1] + FJ * KD
U_END = U_FO[1] + 2 * KF

SET_A, SET_B = 0, 4


def shape_constants():
    f = np.float32
    pos = np.arange(T, dtype=f)
    freqs = (f(1.0) / (f(10000.0) ** np.linspace(0.0, 1.0, DK // 2, dtype=f))).astype(f)
    ang = (pos[:, None] * freqs[None, :]).astype(f)
    ret = np.stack([np.cos(ang).T, np.sin(ang).T], axis=1).astype(f)
    log_g = np.log1p(-np.exp2(-5.0 - np.arange(RH, dtype=np.float64)))
    dist = np.arange(T)[None, :] - np.arange(P)[:, None]
    decay = np.where(dist[:, None, :] >= 0,
                     np.exp(log_g[None, :, None] * np.maximum(dist, 0)[:, None, :]), 0.0)
    decay = (decay * DK ** -0.5).astype(f)
    pf = (f(500000.0) ** (-np.arange(0, 2 * ROT, 2, dtype=f) / f(2 * ROT))).astype(f)
    pang = (pos[:, None] * pf[None, :]).astype(f)
    rope = np.stack([np.cos(pang), np.sin(pang)], axis=0).astype(f)
    rope = rope.reshape(2, TT, P, ROT).transpose(2, 0, 1, 3).reshape(P, 2 * TT * ROT)
    t = np.arange(T)
    end = np.arange(CB) * 16 + 31
    valid = (end[None, :] <= t[:, None]) & (np.arange(CB)[None, :] < NCMP)
    cmask = np.where(valid, 0.0, NEG).astype(f).reshape(TT, P, CB).transpose(1, 0, 2).reshape(P, TT * CB)
    some = valid.any(-1).astype(f).reshape(TT, P).T
    diag = (np.arange(P)[:, None] // CB == np.arange(P // CB)[None, :]).astype(f)
    ident = np.eye(P, dtype=f)
    causal = np.where(np.arange(P)[None, :] > np.arange(P)[:, None], NEG, 0.0).astype(f)
    small = np.concatenate([ident, rope, cmask, some, diag], axis=1)
    return {
        "c_ret": np.ascontiguousarray(ret.reshape(P, 2 * T)),
        "c_decay": np.ascontiguousarray(decay.reshape(P, RH * T)),
        "c_causal": causal,
        "c_small": np.ascontiguousarray(small.astype(f)),
    }


def lay_out_columns(norms, kv_norm, ret_gn, cmp_pos_k, cmp_pos_v):
    rows = [norms[0, 0], norms[0, 2], norms[1, 0], norms[1, 2], kv_norm, ret_gn[0]]
    cols = [r.reshape(-1, P).T for r in rows]
    cols += [p.reshape(LP, P).T for p in (cmp_pos_k, cmp_pos_v)]
    return np.ascontiguousarray(np.concatenate(cols, axis=1))


def yoco_kernel(nc, x, norms, ret_w_in, ret_w_out, nsa_w_in, nsa_w_out, w_kv,
                cmp_w1_k, cmp_w2_k, cmp_w1_v, cmp_w2_v, ffn_w_in, ffn_w_out, feature_columns,
                c_ret, c_decay, c_causal, c_small, out):
    with ExitStack() as ctx:
        def sb(name, shape, dt=F32, stack=ctx):
            return stack.enter_context(nc.sbuf_tensor(name, shape, dt))

        def sem(name):
            return ctx.enter_context(nc.semaphore(name))

        xs = sb("xs", [P, TT, D])
        raw = sb("raw", [P, RAW, W])
        whi = sb("whi", [P, RING, W], F32R)
        wlo = sb("wlo", [P, RING, W], F32R)
        work = sb("work", [P, 8, W])
        gain_row = sb("gain_row", [P, D])
        columns = sb("columns", [P, 5 * KD + 16 + 2 * LP])
        gains = columns[:, 0:5 * KD].rearrange("p (n k) -> p n k", n=5)
        ret_gain = columns[:, 5 * KD:5 * KD + 16]
        pos_sb = columns[:, 5 * KD + 16:].rearrange("p (c l) -> p c l", c=2)
        small = sb("small", [P, c_small.shape[1]])
        ident_b = sb("ident_b", [P, P], BF16)
        causal_b = sb("causal_b", [P, P], BF16)
        means = sb("means", [P, 4, TT])
        halves = sb("halves", [P, 4, 2, TT])
        base = sb("base", [P, 4, TT])
        eps = sb("eps", [P, 1])
        std = sb("std", [P, 8, TT])
        rstd = sb("rstd", [P, 8, TT])
        normed_v = work[:, :, :].rearrange("p (t c) n -> p t (c n)", t=TT)
        at = 0
        ident = small[:, 0:P]
        at = P
        rope_tab = small[:, at:at + 2 * TT * ROT].rearrange("p (f t e) -> p f t e", f=2, t=TT)
        at += 2 * TT * ROT
        cmask = small[:, at:at + TT * CB].rearrange("p (t n) -> p t n", t=TT)
        at += TT * CB
        some = small[:, at:at + TT]
        at += TT
        diag4 = small[:, at:at + 4]

        with ExitStack() as s:
            hT_r = sb("hT_r", [P, 2, KD, T], F32R, s)
            qk_r = sb("qk_r", [P, 2, 2, 2, T], F32R, s)
            v_r = sb("v_r", [P, 2, TT, W], F32R, s)
            y = sb("y", [P, TT, RH * DV], F32, s)
            dec_r = sb("dec_r", [P, 2, 1280], F32R, s)
            rot_tab = sb("rot_tab", [P, 2, T], F32, s)
            decay = sb("decay", [P, RH * T], F32, s)
            gate_r = sb("gate_r", [P, TT, W], F32, s)
            causal = y[:, 0, 0:P]
            bn = sb("bn", [P, TT, 6], F32, s)
            mv = sb("mv", [P, TT, 2], F32, s)
            gvar = sb("gvar", [P, 3, TT], F32, s)
        with ExitStack() as s:
            yT = sb("yT", [P, 2, 16, T], F32R, s)
        with ExitStack() as s:
            hT_f = sb("hT_f", [P, 2, KD, T], F32R, s)
            aT = sb("aT", [P, 2, KF, T], F32R, s)
        with ExitStack() as s:
            kvT = sb("kvT", [P, 2, KD, T], F32R, s)
            hT_n = sb("hT_n", [P, 2, KD, T], F32R, s)
            kT2 = sb("kT2", [P, 2, NG, 2, T], F32R, s)
            v_all = sb("v_all", [P, 2, TT, NG * HD], F32, s)
            cv_bd = sb("cv_bd", [P, NG, REP, HD], F32, s)
            ck2 = sb("ck2", [P, 2, NG, CB], F32R, s)
            w2k = sb("w2k", [P, 2, 2, HD], F32, s)
            w2v = sb("w2v", [P, 2, HD], F32, s)
            gates = sb("gates", [P, TT, NH, 3], F32, s)
            with ExitStack() as s2:
                gate_T = sb("gate_T", [P, T], F32, s2)
            nmax = sb("nmax", [P, 128], F32, s)
            lsum = sb("lsum", [P, 128], F32, s)
            linv = sb("linv", [P, 128], F32, s)
            cst = sb("cst", [P, 4, TT, NH], F32, s)
            with ExitStack() as s2:
                cT = sb("cT", [P, 8, T], F32, s2)
            with ExitStack() as s2:
                qs = sb("qs", [P, TT, 8, 2, HD], F32R, s2)
            with ExitStack() as s2:
                prob = sb("prob", [P, 8, W], F32, s2)
                cprobT = prob[:, 4:8, :]
            sb("over_cT", [P, 8 * T], F32, s)
            rope_t = sb("rope_t", [P, 4, TT * 8 * ROT], F32, s)
            shifted_o = rope_t[:, 0:2, :].rearrange("p n (k q) -> p n k q", k=2)
            gwhi = sb("gwhi", [P, KD, 48], F32R, s)
            gwlo = sb("gwlo", [P, KD, 48], F32R, s)
        with ExitStack() as s:
            kd = sb("kd", [P, 2, TT, NG, 2, 2 * HD], F32R, s)
        with ExitStack() as s:
            qT2 = sb("qT2", [P, NH, T], F32R, s)
            with ExitStack() as s2:
                ckz = sb("ckz", [P, 2, NG, REP, P], F32R, s2)
            pT0 = sb("pT0", [P, 2, TT, 2, P], F32R, s)
            with ExitStack() as s2:
                cprob = sb("cprob", [P, TT, W], F32, s2)
            pT2 = sb("pT2", [P, 2, TT, 2, P], F32R, s)
            v_hl = sb("v_hl", [P, 2, TT, NG, 2 * HD], F32R, s)
            with ExitStack() as s2:
                bT = sb("bT", [P, 2, 2, LP, 124], F32R, s2)
            sb("over_kT2", [P, 2 * NG * 2 * T], F32, s)
            pT1 = sb("pT1", [P, 2, TT, 2, P], F32R, s)
            pT = [pT0, pT1, pT2]
        with ExitStack() as s:
            oT = sb("oT", [P, 2, KD, T], F32R, s)
        gw = gain_row[:, 0:KD * 48].rearrange("p (k n) -> p k n", k=KD)
        hid = work[:, 0, :].rearrange("p (c n) -> p c n", c=2)
        hid_k = work[:, 1, 0:248].rearrange("p (h n) -> p h n", h=2)
        hid_rep = work[:, 2:4, :].rearrange("p h (g r n) -> p h g r n", g=NG, r=REP)
        v_tok0 = work[:, 0:4, :]
        k_tok = work[:, 4:8, :].rearrange("p (c a) (b n) -> p c (a b) n", c=2, b=2)
        q_tok = work[:, :, :].rearrange("p (j t) n -> p j t n", j=2)
        cs_T = work[:, 0:4, :]
        o_T = work
        ps = ctx.enter_context(nc.psum_tensor("ps", [P, 8, W], F32))

        names = """consts_in tables_in gain_in nsa_in w_hi w_lo w_used
            norm_sq norm_std norm_rstd normed hT_psum hT_hi hT_lo
            tile_out post_sq post_base post_std post_rstd post_gain x_ready masks
            rot_prod rot_sum qk_hi qk_lo v_hi v_lo s_full s_dec s_hi s_lo
            g_silu o_full o_copied o_bn o_mv o_var o_std o_rstd o_cent y_done yT_psum yT_hi yT_lo
            ff_silu ff_a ff_hi ff_lo
            kv_v kv_k rope_prod rope_done kd_hi kd_lo gw_hi gw_lo gate_full gate_done
            tp_full tp_act tp_dve shifted b_hi b_lo q_copied qs_hi qs_lo
            gate_sig gate_T_full hid_done hid_T_full hid_k_done rep_zero rep_done ckz_zero ckz_done
            cT_full cT_act cT_dve ck_full ck_hi ck_lo cv_full cv_done
            v_hl_hi v_hl_lo
            cs_full cs_masked cs_max cs_sub cs_exp cs_sum cs_inv cs_coef cs_scaled cs_tp cs_pT oc_full oc_done
            sc_full max_done exp_done l_inv p_scaled pt_full pt_hi pt_lo pv_done o_shifted o_part o_done
            oT_hi oT_lo stored""".split()
        S = {n: sem(n) for n in names}
        x_in = [sem(f"x_in{t}") for t in range(TT)]
        raw_in = [sem(f"raw_in{i}") for i in range(RAW)]

        block = ctx.enter_context(nc.Block())
        R_LAG, T_LAG, V_LAG = 1, 4, 8
        C_STEP = 3

        def where(n):
            ig, u = divmod(n, 8)
            return *block_of(ig), (u // 2) % 2, 2 * (u // 4) + u % 2

        def place(n):
            return n % 4 if n < 16 else n % 8

        def block_of(ig):
            return TT - 1 - ig // NG, ig % NG

        def block_end(n, late):
            ig, rest = divmod(n - V_LAG - 1 - late, 8)
            return ig - 1 if rest == 0 and ig >= 1 else None

        def splits_after(j, k):
            if j > 0:
                return k + 1 if k + 1 < KD else None
            return {0: 0, 4: 1, 5: 2, 6: 3}.get(k)

        def plus(c, it, per):
            return c if it is None else c + it * per

        @block.sync
        def _(sp):
            def load(u, src, it=None, per=0, cols=1):
                if u >= RAW or it is not None:
                    sp.wait_ge(S["w_lo"], plus(u - RAW + 1, it, per))
                dst = raw[:, u % RAW, :]
                if cols > 1:
                    dst = dst.rearrange("p (c n) -> p c n", c=cols)
                sp.dma_start(dst, src).then_inc(raw_in[u % RAW], 16)

            ret = ret_w_in[0].rearrange("(k p) n -> p k n", p=P)
            ret_qk = ret[:, :, 0:2 * RH * DK].rearrange("p k (c n) -> p k c n", c=2)

            def head_loads(h, it):
                for k in range(KD):
                    load(k, ret_qk[:, k, :, bass.ds(h * DK, DK)], it, 24, cols=2)
                for part in range(2):
                    col = 2 * RH * DK + part * RH * DV
                    for k in range(KD):
                        load(KD * (part + 1) + k, ret[:, k, bass.ds(h * DV + col, DV)], it, 24)

            for t in range(TT):
                sp.dma_start(xs[:, t, :], x[0, t * P:(t + 1) * P, :]).then_inc(x_in[t], 16)
            head_loads(0, None)
            with sp.Fori(1, RH) as h:
                head_loads(h, h)

            def out_loads(u0, w, tiles):
                v = w.rearrange("(k p) n -> p k n", p=P)
                for half in range(2):
                    for k in range(tiles):
                        load(u0 + half * tiles + k, v[:, k, half * W:(half + 1) * W])

            out_loads(U_RO, ret_w_out[0], 16)

            def ffn_loads(layer):
                v = ffn_w_in[layer].rearrange("(k p) (c n) -> p k c n", p=P, c=2)
                u0 = U_FI[layer]
                with sp.Fori(0, FJ) as b:
                    for k in range(KD):
                        load(u0 + k, v[:, k, :, bass.ds(b * 256, 256)], b, KD, cols=2)
                out_loads(U_FO[layer], ffn_w_out[layer], KF)

            ffn_loads(0)
            kv = w_kv.rearrange("(k p) n -> p k n", p=P)
            for c in range(3):
                for k in range(KD):
                    load(U_KV + c * KD + k, kv[:, k, c * W:(c + 1) * W])
            wq = nsa_w_in[0].rearrange("(k p) n -> p k n", p=P)
            for j in range(2):
                for k in range(KD):
                    load((U_Q0, U_Q1)[j] + k, wq[:, k, j * W:(j + 1) * W])
            for kv_i, w1 in enumerate((cmp_w1_k, cmp_w1_v)):
                v = w1.rearrange("(k p) n -> p k n", p=P)
                for k in range(LP // 2):
                    load(U_CMP + kv_i * 8 + k, v[:, 2 * k:2 * k + 2, :], cols=2)
            out_loads(U_NO, nsa_w_out[0], KD)
            ffn_loads(1)
            for t in range(TT):
                sp.wait_ge(S["x_ready"], 12 + t + 1)
                sp.dma_start(out[0, t * P:(t + 1) * P, :], xs[:, t, :]).then_inc(S["stored"], 16)
            sp.wait_ge(S["stored"], 64)

        @block.gpsimd
        def _(pool):
            def gain_load(i):
                layer, n = i // 2, 1 + 2 * (i % 2)
                pool.dma_start(gain_row[:], norms[layer, n:n + 1, :].broadcast_to([P, D])).then_inc(S["gain_in"], 16)

            pool.wait_ge(x_in[TT - 1], 16)
            pool.dma_start(rot_tab[:].rearrange("p a b -> p (a b)"), c_ret).then_inc(S["tables_in"], 16)
            pool.dma_start(causal, c_causal).then_inc(S["tables_in"], 16)
            pool.dma_start(decay[:], c_decay).then_inc(S["tables_in"], 16)
            gain_load(0)
            pool.wait_ge(S["consts_in"], 32)
            nc.gpsimd.tensor_copy(ident_b[:], ident).then_inc(S["y_done"], 1)
            with pool.Fori(0, RH) as h:
                for t in range(TT):
                    pool.wait_ge(S["o_copied"], h * 4 + (t + 1))
                    pool.wait_ge(S["o_rstd"], h + 1)
                    pool.nop(nofuse=True)
                    nc.gpsimd.tensor_scalar(work[:, 4 + t, :], work[:, 4 + t, :], mv[:, t, 0:1], gvar[:, 2, t:t + 1],
                                            ALU.subtract, ALU.mult).then_inc(S["o_cent"], 1)
                for t in range(TT):
                    pool.wait_ge(S["g_silu"], h * 4 + (t + 1))
                    pool.wait_ge(S["o_cent"], h * 4 + (t + 2))
                    nc.gpsimd.tensor_tensor(y[:, t, bass.ds(h * DV, DV)], work[:, 4 + t, :], gate_r[:, t, :],
                                            ALU.mult).then_inc(S["y_done"], 1)
            pool.wait_ge(S["x_ready"], 4)
            gain_load(1)
            pool.wait_ge(S["normed"], 12)
            for dup in range(2):
                pool.dma_start(w2k[:, :, dup, :], cmp_w2_k.rearrange("(h p) d -> p h d", p=P)
                               ).then_inc(S["nsa_in"], 16)
            pool.dma_start(w2v[:, :, :], cmp_w2_v.rearrange("(h p) d -> p h d", p=P)).then_inc(S["nsa_in"], 16)
            pool.dma_start(gw[:], nsa_w_in[0].rearrange("(k p) n -> p k n", p=P)[:, :, NH * HD:NH * HD + 48]
                           ).then_inc(S["nsa_in"], 16)
            pool.wait_ge(S["tp_act"], 4)
            pool.wait_ge(S["tp_dve"], 4)
            pool.dma_start(cT[HD:P, :, 0:T - 1], cT[0:HD, :, 1:T]).then_inc(S["shifted"], 16)
            pool.wait_ge(S["gw_lo"], 1)
            gain_load(2)
            pool.wait_ge(S["gate_full"], 1)
            nc.gpsimd.memset(ckz[:].bitcast(F32), 0.0).then_inc(S["ckz_zero"], 1)
            pool.wait_ge(S["qs_lo"], 4)
            nc.gpsimd.memset(hid_rep[:], 0.0).then_inc(S["rep_zero"], 1)
            for b in range(2):
                pool.wait_ge(S["v_hl_hi"], b + 1)
                nc.gpsimd.tensor_tensor(v_hl[:, b, :, :, HD:].rearrange("p t g d -> p (t g) d"),
                                        v_all[:, b].rearrange("p t (g d) -> p (t g) d", d=HD),
                                        v_hl[:, b, :, :, 0:HD].bitcast(F32).rearrange("p t g d -> p (t g) d"),
                                        ALU.subtract).then_inc(S["v_hl_lo"], 1)
            pool.wait_ge(S["ckz_zero"], 1)
            pool.wait_ge(S["ck_lo"], 1)
            for part in range(2):
                for r in range(REP):
                    nc.gpsimd.tensor_copy(ckz[:, part, :, r, r * CB:r * CB + NCMP],
                                          ck2[:, part, :, 0:NCMP].bitcast(F32)).then_inc(S["ckz_done"], 1)
            for i in range(TT):
                sc = cprob[:, i, :].rearrange("p (h n) -> p h n", h=NH)
                pool.wait_ge(S["cs_max"], i + 1)
                nc.gpsimd.tensor_tensor(sc, sc, cst[:, 0, i, :].unsqueeze(2).broadcast_to([P, NH, CB]), ALU.subtract
                                        ).then_inc(S["cs_sub"], 1)
            for n in range(128 + V_LAG + 4):
                if 1 <= n <= TT:
                    sc = cprob[:, n - 1, :].rearrange("p (h n) -> p h n", h=NH)
                    pool.wait_ge(S["cs_coef"], n)
                    nc.gpsimd.tensor_tensor(sc, sc, cst[:, 3, n - 1, :].unsqueeze(2).broadcast_to([P, NH, CB]),
                                            ALU.mult).then_inc(S["cs_scaled"], 1)
                ig = block_end(n, 2)
                if ig is not None:
                    i, g = block_of(ig)
                    o = o_T[:, 2 * g:2 * g + 2, i * P:(i + 1) * P]
                    pool.wait_ge(S["o_shifted"], 2 * (ig + 1))
                    pool.wait_ge(S["oc_done"], KD)
                    nc.gpsimd.tensor_tensor(o, o, shifted_o[:, ig % 2], ALU.add).then_inc(S["o_part"], 1)
                if n < 128:
                    i, g, b, r = where(n)
                    w = (i + 1) * P
                    h = g * REP + r
                    pool.wait_ge(S["l_inv"], n + 1)
                    nc.gpsimd.tensor_scalar(prob[:, place(n), 0:w], prob[:, place(n), 0:w], linv[:, n:n + 1],
                                            gates[:, i, h, 1 + b:2 + b], ALU.mult, ALU.mult
                                            ).then_inc(S["p_scaled"], 1)
            pool.wait_ge(S["x_ready"], 12)
            gain_load(3)

        @block.scalar
        def _(act):
            A = nc.scalar.activation

            def hi(u, it=None, per=0):
                act.wait_ge(raw_in[u % RAW], plus(16 * (u // RAW + 1), it, 16 * (per // RAW)))
                if u >= RING:
                    act.wait_ge(S["w_used"], plus(u - 3, it, per))
                A(whi[:, u % RING, :], raw[:, u % RAW, :], ACT.Copy).then_inc(S["w_hi"], 1)

            def x_squares(j, t):
                A(normed_v[:, t, :], xs[:, t, :], ACT.Square, scale=D ** -0.5, accum_out=means[:, j, t:t + 1]
                  ).then_inc(S["norm_sq"], 1)
                act.wait_ge(S["norm_sq"], 4 * j + t + 1)
                A(std[:, j, t:t + 1], means[:, j, t:t + 1], ACT.Sqrt, bias=eps[:, 0:1]).then_inc(S["norm_std"], 1)

            def hT_hi(j, dests, u):
                if j == 0:
                    act.wait_ge(S["consts_in"], 32)
                else:
                    hi(u)
                for k in range(KD):
                    act.wait_ge(S["hT_psum"], 8 * j + k + 1)
                    for dst, gain in dests:
                        ins = A(dst[:, 0, k, :], ps[:, SET_B + k % 4, :], ACT.Copy,
                                scale=gains[:, gain, k:k + 1])
                    ins.then_inc(S["hT_hi"], 1)
                    if splits_after(j, k) is not None:
                        hi(u + splits_after(j, k))

            def half_square(i, half, t):
                A(normed_v[:, t, half * W:(half + 1) * W], ps[:, (SET_B, SET_A)[half] + t, :], ACT.Square,
                  scale=D ** -0.5, accum_out=halves[:, i, half, t:t + 1]).then_inc(S["post_sq"], 1)

            def out_phase(i, u0, tiles, before=None):
                for n in range(4, 2 * tiles):
                    hi(u0 + n)
                    if before is not None and n < tiles:
                        before(n)
                    if n == tiles + 3:
                        act.wait_ge(S["w_used"], u0 + tiles)
                        for t in range(TT):
                            half_square(i, 0, t)
                        act.wait_ge(S["post_base"], i + 1)
                for t in range(TT + 1):
                    if t < TT:
                        if t < TT - 1:
                            act.wait_ge(S["tile_out"], 3 * i + t + 1)
                        else:
                            act.wait_ge(S["w_used"], u0 + 2 * tiles)
                        half_square(i, 1, t)
                        act.wait_ge(S["post_sq"], 8 * i + 5 + t)
                        A(std[:, 4 + i, t:t + 1], halves[:, i, 1, t:t + 1], ACT.Sqrt, bias=base[:, i, t:t + 1]
                          ).then_inc(S["post_std"], 1)
                    if t >= 1 and i < 3:
                        act.wait_ge(S["x_ready"], 4 * i + t)
                        x_squares(i + 1, t - 1)

            act.dma_start(small[:], c_small).then_inc(S["consts_in"], 16)
            act.dma_start(columns[:], feature_columns).then_inc(S["consts_in"], 16)
            nc.scalar.preload_act_table(ACT.Sqrt)
            act.wait_ge(S["masks"], 1)
            for t in range(TT):
                act.wait_ge(x_in[t], 16)
                x_squares(0, t)
            hT_hi(0, [(hT_r, 0)], 0)

            with act.Fori(0, 2) as it:
                for p in range(2):
                    u0 = 24 * p
                    xb, yb = (SET_A, SET_B) if p == 0 else (SET_B, SET_A)

                    def n4(c):
                        return it * 8 + (4 * p + c)
                    for n in range(4, 12):
                        hi(u0 + n, it, 48)
                    for m in range(4):
                        if m == 2:
                            hi(u0 + 12, it, 48)
                            hi(u0 + 13, it, 48)
                        act.wait_ge(S["rot_sum"], n4(m + 1))
                        A(qk_r[:, 0, m // 2, m % 2, :], work[:, 4 * (m // 2) + 2 * (m % 2), :], ACT.Copy
                          ).then_inc(S["qk_hi"], 1)
                    for n in range(14, 20):
                        hi(u0 + n, it, 48)
                    act.wait_ge(S["w_used"], it * 48 + (u0 + 16))
                    for t in range(TT):
                        A(v_r[:, 0, t, :], ps[:, yb + t, :], ACT.Copy).then_inc(S["v_hi"], 1)
                    at_col = 0
                    for j in range(TT):
                        w = T - j * P
                        act.wait_ge(S["s_dec"], n4(j + 1))
                        A(dec_r[:, 0, at_col:at_col + w], work[:, j, 0:w], ACT.Copy).then_inc(S["s_hi"], 1)
                        at_col += w
                    for n in range(20, 28):
                        hi(u0 + n, it, 48)
                    act.wait_ge(S["w_used"], it * 48 + (u0 + 24))
                    act.wait_ge(S["y_done"], n4(1))
                    for t in range(TT):
                        A(gate_r[:, t, :], ps[:, yb + t, :], ACT.Silu).then_inc(S["g_silu"], 1)
                    nc.scalar.preload_act_table(ACT.Sqrt)
                    for t in range(TT):
                        act.wait_ge(S["o_bn"], n4(t + 1))
                        A(work[:, 4 + t, :], ps[:, xb + t, :], ACT.Copy).then_inc(S["o_copied"], 1)
                    act.wait_ge(S["o_var"], it * 2 + (p + 1))
                    A(gvar[:, 1, :], gvar[:, 0, :], ACT.Sqrt).then_inc(S["o_std"], 1)

            def yT_hi(k):
                act.wait_ge(S["yT_psum"], k + 1)
                A(yT[:, 0, k, :], ps[:, SET_A + k % 4, :], ACT.Copy, scale=ret_gain[:, k:k + 1]
                  ).then_inc(S["yT_hi"], 1)

            for k in range(4):
                yT_hi(k)
            out_phase(0, U_RO, 16, yT_hi)

            def ffn(layer):
                f0 = FJ * layer
                u0 = U_FI[layer]
                hT_hi(1 + 2 * layer, [(hT_f, 1 + 2 * layer)], u0)

                def job(b, par, first=False, it=None):
                    bank = SET_A if par % 2 == 0 else SET_B
                    q = par % 2
                    for n in range(8 if b == 0 else 4, 12):
                        hi(u0 + 8 * b + n, it, 16)
                    act.wait_ge(S["w_used"], plus(u0 + 8 * b + 8, it, 16))
                    if not first:
                        act.wait_ge(S["ff_a"], plus(2 * (f0 + b - 1), it, 4))
                    for f in range(2):
                        A(work[:, 2 * q + f, :], ps[:, bank + f, :], ACT.Silu).then_inc(S["ff_silu"], 1)
                    for f in range(2):
                        act.wait_ge(S["ff_a"], plus(2 * (f0 + b) + f + 1, it, 4))
                        if it is None:
                            dst = aT[:, 0, 2 * b + f, :]
                        else:
                            dst = aT[:, 0, bass.ds(it * 4 + (2 * b + f), 1), :]
                        A(dst, work[:, 4 + 2 * q + f, :] if it is None else work[:, 4 + 2 * q + f:5 + 2 * q + f, :],
                          ACT.Copy).then_inc(S["ff_hi"], 1)
                job(0, 0, True)
                job(1, 1, True)
                with act.Fori(0, 4) as it:
                    job(2, 0, it=it)
                    job(3, 1, it=it)
                job(10, 0)
                nc.scalar.preload_act_table(ACT.Sqrt)
                out_phase(1 + 2 * layer, U_FO[layer], KF)

            ffn(0)

            hT_hi(2, [(kvT, 4), (hT_n, 2)], U_KV)

            def v_copies(c):
                bank = (SET_A, SET_B, SET_A)[c]
                act.wait_ge(S["w_used"], U_KV + KD * (c + 1))
                for t in range(TT):
                    dst = v_tok0[:, t, 256:512] if c == 0 else v_all[:, c - 1, t, :]
                    A(dst, ps[:, bank + t, 256:512], ACT.Copy).then_inc(S["kv_v"], 1)

            def tp_dst(m):
                if m < 8:
                    return cT[0:HD, m, :], HD
                if m < 24:
                    c, g, part = (m - 8) // 8, (m - 8) % 8 // 2, m % 2
                    return kT2[:, c, g, part, :], P
                return qT2[:, m - 24, :], P

            def tp_items(lo_m, hi_m):
                for m in range(lo_m, hi_m):
                    if m % 2 == 1:
                        dst, n = tp_dst(m)
                        act.wait_ge(S["tp_full"], m + 1)
                        A(dst, ps[0:n, SET_A + m % 4, :], ACT.Copy).then_inc(S["tp_act"], 1)

            for n in range(8, 12):
                hi(U_KV + n)
            v_copies(0)
            for n in range(12, 16):
                hi(U_KV + n)
            for n in range(16, 20):
                hi(U_KV + n)
            tp_items(0, 8)
            v_copies(1)
            act.wait_ge(S["nsa_in"], 16 * 4)
            A(gwhi[:], gw[:], ACT.Copy).then_inc(S["gw_hi"], 1)
            for n in range(20, 28):
                hi(U_KV + n)
            v_copies(2)
            act.wait_ge(S["shifted"], 16)

            def q_copies(j, bank):
                act.wait_ge(S["w_used"], (U_Q0, U_Q1)[j] + KD)
                if j == 1:
                    act.wait_ge(S["kd_lo"], 8)
                for t in range(TT):
                    A(q_tok[:, j, t, :], ps[:, bank + t, :], ACT.Copy, scale=HD ** -0.5).then_inc(S["q_copied"], 1)

            def qs_hi(j, t0=0, t1=TT):
                act.wait_ge(S["rope_done"], 2 * (4 + j))
                for t in range(t0, t1):
                    A(qs[:, t, :, 0, :], q_tok[:, j, t, :].rearrange("p (h d) -> p h d", h=8), ACT.Copy
                      ).then_inc(S["qs_hi"], 1)

            for n in range(16):
                if n == 8:
                    q_copies(0, SET_B)
                hi(U_Q0 + 4 + n)
                for m in range(2 * n, 2 * n + 2):
                    kv_i, lp = divmod(m, LP)
                    A(bT[:, 0, kv_i, lp, :].rearrange("p (g n) -> p g n", g=NG),
                      cT[:, kv_i * 4:kv_i * 4 + 4, 2 * lp:2 * lp + 481:16], ACT.Identity,
                      bias=pos_sb[:, kv_i, lp:lp + 1]).then_inc(S["b_hi"], 1)
                if n < 8:
                    c, t = divmod(n, TT)
                    act.wait_ge(S["rope_done"], 2 * (c + 2))
                    A(kd[:, c, t, :, 0, :].rearrange("p g (u d) -> p g u d", u=2),
                      k_tok[:, c, t, :].rearrange("p (g d) -> p g d", g=NG).unsqueeze(2)
                      .broadcast_to([P, NG, 2, HD]), ACT.Copy).then_inc(S["kd_hi"], 1)
            q_copies(1, SET_A)
            act.wait_ge(S["gate_full"], 1)
            A(gate_T[0:48, :], ps[0:48, SET_B, :], ACT.Sigmoid).then_inc(S["gate_sig"], 1)
            for n in range(16):
                hi(U_CMP + 4 + n)
                if n == 1:
                    act.wait_ge(S["gate_T_full"], 1)
                    A(gates[:].rearrange("p t h c -> p (t h c)"), ps[:, SET_B + 1, 0:192], ACT.Copy
                      ).then_inc(S["gate_done"], 1)
                if n in (4, 6, 8, 10):
                    act.wait_ge(S["b_lo"], 2 * LP)
                    qs_hi(0, n // 2 - 2, n // 2 - 1)
                if n in (12, 14):
                    b = n // 2 - 6
                    A(v_hl[:, b, :, :, 0:HD].rearrange("p t g d -> p (t g) d"),
                      v_all[:, b].rearrange("p t (g d) -> p (t g) d", d=HD), ACT.Copy).then_inc(S["v_hl_hi"], 1)
            tp_items(8, 16)
            act.wait_ge(S["w_used"], U_CMP + LP)
            act.wait_ge(S["qs_lo"], 4)
            for kv_i in range(2):
                A(hid[0:124, kv_i, :], ps[0:124, SET_B + 2 + kv_i, 0:256], ACT.Gelu_apprx_tanh
                  ).then_inc(S["hid_done"], 1)
            tp_items(16, 24)
            act.wait_ge(S["ck_full"], 1)
            A(ck2[:, 0, :, 0:NCMP], ps[:, SET_B + 1, 0:124].rearrange("p (g n) -> p g n", g=NG), ACT.Copy
              ).then_inc(S["ck_hi"], 1)
            tp_items(24, 32)
            act.wait_ge(S["tp_full"], 32)
            qs_hi(1)
            for g in (1, 3):
                act.wait_ge(S["cT_full"], g + 1)
                A(cs_T[:, g, :], ps[:, SET_B + g, :], ACT.Copy).then_inc(S["cT_act"], 1)
                if g == 1:
                    tp_items(32, 40)
            for i in range(TT):
                act.wait_ge(S["cs_sub"], i + 1)
                A(cprob[:, i, :], cprob[:, i, :], ACT.Exp).then_inc(S["cs_exp"], 1)

            def oT_hi(k):
                act.wait_ge(S["o_done"], 2 * (NG * (TT - 1) + k // 2 + 1))
                A(oT[:, 0, k, :], o_T[:, k, :], ACT.Copy).then_inc(S["oT_hi"], 1)

            for n in range(128 + V_LAG + 2):
                c = n - C_STEP - 1
                if 0 <= c < TT:
                    act.wait_ge(S["cs_tp"], c + 1)
                    A(cprobT[:, :, c * P:(c + 1) * P], ps[:, 7, :].rearrange("p (g q) -> p g q", g=NG), ACT.Copy
                      ).then_inc(S["cs_pT"], 1)
                elif TT <= c < TT + KD:
                    act.wait_ge(S["oc_full"], c - TT + 1)
                    A(o_T[:, c - TT, :], ps[:, 7, :], ACT.Copy).then_inc(S["oc_done"], 1)
                m = n - T_LAG
                if 0 <= m < 128:
                    i = where(m)[0]
                    act.wait_ge(S["pt_full"], m + 1)
                    if m == 4:
                        act.wait_ge(S["cs_tp"], TT)
                    if m >= 6:
                        act.wait_ge(S["pv_done"], m // 2 - 2)
                    A(pT[m // 2 % 3][:, 0, 0:i + 1, m % 2, :],
                      ps[:, 3 + m % 3, 0:(i + 1) * P].rearrange("p (j q) -> p j q", q=P), ACT.Copy
                      ).then_inc(S["pt_hi"], 1)
                if n < 128:
                    w = (where(n)[0] + 1) * P
                    act.wait_ge(S["max_done"], n + 1)
                    if 20 <= n < 24:
                        act.wait_ge(S["oc_full"], KD)
                    elif n >= 4:
                        act.wait_ge(S["pt_full"], n - 3 if n < 20 else n - 7)
                    A(prob[:, place(n), 0:w], ps[:, n % 3, 0:w], ACT.Exp, bias=nmax[:, n:n + 1],
                      accum_out=lsum[:, n:n + 1]).then_inc(S["exp_done"], 1)
                if n == 128 + T_LAG:
                    for k in range(4):
                        oT_hi(k)
                ig = block_end(n, 0)
                if ig is not None:
                    o = ps[:, 6 + ig % 2, :].rearrange("p (k r q) -> p k r q", k=2, r=2)
                    act.wait_ge(S["pv_done"], 4 * (ig + 1))
                    if ig >= 2:
                        act.wait_ge(S["o_part"], ig - 1)
                    A(shifted_o[0:HD, ig % 2], o[HD:P, :, 0, :], ACT.Copy).then_inc(S["o_shifted"], 1)
                    A(shifted_o[HD:P, ig % 2], o[0:HD, :, 1, :], ACT.Copy).then_inc(S["o_shifted"], 1)

            nc.scalar.preload_act_table(ACT.Sqrt)
            out_phase(2, U_NO, KD, oT_hi)
            ffn(1)

        @block.vector
        def _(dve):
            V = nc.vector

            def lo(u, it=None, per=0):
                dve.wait_ge(S["w_hi"], plus(u + 1, it, per))
                V.tensor_tensor(wlo[:, u % RING, :], raw[:, u % RAW, :], whi[:, u % RING, :].bitcast(F32),
                                ALU.subtract).then_inc(S["w_lo"], 1)

            def normalise(j, t):
                dve.wait_ge(S["norm_std"], 4 * j + t + 1)
                V.reciprocal(rstd[:, j, t:t + 1], std[:, j, t:t + 1]).then_inc(S["norm_rstd"], 1)
                dve.wait_ge(S["norm_rstd"], 4 * j + t + 1)
                V.tensor_scalar(normed_v[:, t, :], xs[:, t, :], rstd[:, j, t:t + 1], None, ALU.mult
                                ).then_inc(S["normed"], 1)

            def hT_lo(j, dests, u):
                if j > 0:
                    lo(u)
                for k in range(KD):
                    dve.wait_ge(S["hT_hi"], 8 * j + k + 1)
                    for dst, gain in dests:
                        ins = V.scalar_tensor_tensor(
                            out=dst[:, 1, k, :], in0=ps[:, SET_B + k % 4, :], scalar=gains[:, gain, k:k + 1],
                            in1=dst[:, 0, k, :].bitcast(F32), op0=ALU.mult, op1=ALU.subtract)
                    ins.then_inc(S["hT_lo"], 1)
                    if splits_after(j, k) is not None:
                        lo(u + splits_after(j, k))

            def gained(i, half, t):
                V.tensor_tensor(normed_v[:, t, half * W:(half + 1) * W], ps[:, (SET_B, SET_A)[half] + t, :],
                                gain_row[:, half * W:(half + 1) * W], ALU.mult).then_inc(S["post_gain"], 1)

            def out_phase(i, u0, tiles, before=None):
                for n in range(4, 2 * tiles):
                    lo(u0 + n)
                    if before is not None and n < tiles:
                        before(n)
                    if n == tiles + 3:
                        dve.wait_ge(S["post_sq"], 8 * i + 4)
                        V.tensor_scalar(base[:, i, :], halves[:, i, 0, :], EPS, None, ALU.add
                                        ).then_inc(S["post_base"], 1)
                        dve.wait_ge(S["gain_in"], 16 * (i + 1))
                        for t in range(TT):
                            gained(i, 0, t)
                for t in range(TT + 1):
                    if t < TT:
                        dve.wait_ge(S["post_sq"], 8 * i + 5 + t)
                        gained(i, 1, t)
                        dve.wait_ge(S["post_std"], 4 * i + t + 1)
                        V.reciprocal(rstd[:, 4 + i, t:t + 1], std[:, 4 + i, t:t + 1]).then_inc(S["post_rstd"], 1)
                        dve.wait_ge(S["post_rstd"], 4 * i + t + 1)
                        dve.wait_ge(S["post_gain"], 8 * i + 5 + t)
                        V.scalar_tensor_tensor(out=xs[:, t, :], in0=normed_v[:, t, :],
                                               scalar=rstd[:, 4 + i, t:t + 1], in1=xs[:, t, :],
                                               op0=ALU.mult, op1=ALU.add).then_inc(S["x_ready"], 1)
                    if t >= 1 and i < 3:
                        normalise(i + 1, t - 1)

            V.memset(eps[:], EPS).then_inc(S["masks"], 1)
            for t in range(TT):
                normalise(0, t)
            dve.wait_ge(S["consts_in"], 32)
            hT_lo(0, [(hT_r, 0)], 0)
            dve.wait_ge(S["tables_in"], 48)
            V.tensor_copy(causal_b[:], causal).then_inc(S["o_cent"], 1)

            with dve.Fori(0, 2) as it:
                for p in range(2):
                    u0 = 24 * p
                    xb, yb = (SET_A, SET_B) if p == 0 else (SET_B, SET_A)

                    def n4(c):
                        return it * 8 + (4 * p + c)

                    def n1(c=1):
                        return it * 2 + (p + c)
                    for n in range(4, 12):
                        lo(u0 + n, it, 48)
                    dve.wait_ge(S["w_used"], it * 48 + (u0 + 8))
                    dve.wait_ge(S["y_done"], n4(1))
                    for m in range(2):
                        a, b = ps[:, xb + 2 * m, :], ps[:, xb + 2 * m + 1, :]
                        for n, (src, f) in enumerate(((a, 0), (b, 1), (a, 1), (b, 0))):
                            V.tensor_tensor(work[:, 4 * m + n, :], src, rot_tab[:, f, :], ALU.mult
                                            ).then_inc(S["rot_prod"], 1)
                        dve.wait_ge(S["rot_prod"], it * 16 + (8 * p + 4 * m + 4))
                        V.tensor_tensor(work[:, 4 * m, :], work[:, 4 * m, :], work[:, 4 * m + 1, :], ALU.subtract
                                        ).then_inc(S["rot_sum"], 1)
                        V.tensor_tensor(work[:, 4 * m + 2, :], work[:, 4 * m + 2, :], work[:, 4 * m + 3, :],
                                        ALU.add).then_inc(S["rot_sum"], 1)
                        if m == 0:
                            lo(u0 + 12, it, 48)
                    lo(u0 + 13, it, 48)
                    for m in range(4):
                        dve.wait_ge(S["qk_hi"], n4(m + 1))
                        V.tensor_tensor(qk_r[:, 1, m // 2, m % 2, :], work[:, 4 * (m // 2) + 2 * (m % 2), :],
                                        qk_r[:, 0, m // 2, m % 2, :].bitcast(F32), ALU.subtract
                                        ).then_inc(S["qk_lo"], 1)
                    for n in range(14, 20):
                        lo(u0 + n, it, 48)
                    for t in range(TT):
                        dve.wait_ge(S["v_hi"], n4(t + 1))
                        V.tensor_tensor(v_r[:, 1, t, :], ps[:, yb + t, :], v_r[:, 0, t, :].bitcast(F32),
                                        ALU.subtract).then_inc(S["v_lo"], 1)
                    dve.wait_ge(S["s_full"], n1())
                    for j in range(TT):
                        w = T - j * P
                        V.tensor_tensor(work[:, j, 0:w], ps[:, xb + j, 0:w],
                                        decay[:, bass.ds(it * 2 * T + p * T, w)], ALU.mult
                                        ).then_inc(S["s_dec"], 1)
                    at_col = 0
                    for j in range(TT):
                        w = T - j * P
                        dve.wait_ge(S["s_hi"], n4(j + 1))
                        V.tensor_tensor(dec_r[:, 1, at_col:at_col + w], work[:, j, 0:w],
                                        dec_r[:, 0, at_col:at_col + w].bitcast(F32), ALU.subtract
                                        ).then_inc(S["s_lo"], 1)
                        at_col += w
                    for n in range(20, 28):
                        lo(u0 + n, it, 48)
                    dve.wait_ge(S["o_full"], n1())
                    for t in range(TT):
                        V.bn_stats(bn[:, t, :], ps[:, xb + t, :]).then_inc(S["o_bn"], 1)
                    for t in range(TT):
                        dve.wait_ge(S["o_bn"], n4(t + 1))
                        dve.nop(nofuse=True)
                        V.bn_aggr(mv[:, t, :], bn[:, t, :]).then_inc(S["o_mv"], 1)
                    dve.wait_ge(S["o_mv"], n4(TT))
                    V.tensor_scalar(gvar[:, 0, :], mv[:, :, 1], EPS, None, ALU.add).then_inc(S["o_var"], 1)
                    dve.wait_ge(S["o_std"], n1())
                    V.reciprocal(gvar[:, 2, :], gvar[:, 1, :]).then_inc(S["o_rstd"], 1)

            def yT_lo(k):
                dve.wait_ge(S["yT_hi"], k + 1)
                V.scalar_tensor_tensor(out=yT[:, 1, k, :], in0=ps[:, SET_A + k % 4, :],
                                       scalar=ret_gain[:, k:k + 1], in1=yT[:, 0, k, :].bitcast(F32),
                                       op0=ALU.mult, op1=ALU.subtract).then_inc(S["yT_lo"], 1)

            for k in range(4):
                yT_lo(k)
            out_phase(0, U_RO, 16, yT_lo)

            def ffn(layer):
                u0 = U_FI[layer]
                hT_lo(1 + 2 * layer, [(hT_f, 1 + 2 * layer)], u0)
                f0 = FJ * layer

                def job(b, par, it=None):
                    bank = SET_A if par % 2 == 0 else SET_B
                    q = par % 2
                    for n in range(8 if b == 0 else 4, 12):
                        lo(u0 + 8 * b + n, it, 16)
                    for f in range(2):
                        dve.wait_ge(S["ff_silu"], plus(2 * (f0 + b) + f + 1, it, 4))
                        V.tensor_tensor(work[:, 4 + 2 * q + f, :], ps[:, bank + 2 + f, :], work[:, 2 * q + f, :],
                                        ALU.mult).then_inc(S["ff_a"], 1)
                    for f in range(2):
                        dve.wait_ge(S["ff_hi"], plus(2 * (f0 + b) + f + 1, it, 4))
                        if it is None:
                            a_hi, a_lo, src = aT[:, 0, 2 * b + f, :], aT[:, 1, 2 * b + f, :], work[:, 4 + 2 * q + f, :]
                        else:
                            k = bass.ds(it * 4 + (2 * b + f), 1)
                            a_hi, a_lo, src = aT[:, 0, k, :], aT[:, 1, k, :], work[:, 4 + 2 * q + f:5 + 2 * q + f, :]
                        V.tensor_tensor(a_lo, src, a_hi.bitcast(F32), ALU.subtract).then_inc(S["ff_lo"], 1)
                job(0, 0)
                job(1, 1)
                with dve.Fori(0, 4) as it:
                    job(2, 0, it)
                    job(3, 1, it)
                job(10, 0)
                out_phase(1 + 2 * layer, U_FO[layer], KF)

            ffn(0)
            hT_lo(2, [(kvT, 4), (hT_n, 2)], U_KV)

            def rope(buf, heads, r):
                v = buf.rearrange("p t (h d) -> p t h d", d=HD)
                a, b = v[:, :, :, 0:ROT], v[:, :, :, ROT:2 * ROT]
                cos = rope_tab[:, 0].unsqueeze(2).broadcast_to([P, TT, heads, ROT])
                sin = rope_tab[:, 1].unsqueeze(2).broadcast_to([P, TT, heads, ROT])
                t = [rope_t[:, n, 0:TT * heads * ROT].rearrange("p (t h e) -> p t h e", t=TT, h=heads)
                     for n in range(4)]
                for n, (src, f) in enumerate(((a, cos), (b, sin), (a, sin), (b, cos))):
                    V.tensor_tensor(t[n], src, f, ALU.mult).then_inc(S["rope_prod"], 1)
                dve.wait_ge(S["rope_prod"], 4 * (r + 1))
                V.tensor_tensor(a, t[0], t[1], ALU.subtract).then_inc(S["rope_done"], 1)
                V.tensor_tensor(b, t[2], t[3], ALU.add).then_inc(S["rope_done"], 1)

            def kv_job(c):
                bank = (SET_A, SET_B, SET_A)[c]
                dst = v_tok0[:, :, 0:256] if c == 0 else k_tok[:, c - 1]
                for t in range(TT):
                    dve.wait_ge(S["kv_v"], 4 * c + t + 1)
                    V.tensor_copy(dst[:, t, :], ps[:, bank + t, 0:256]).then_inc(S["kv_k"], 1)
                dve.wait_ge(S["kv_k"], 4 * (c + 1))
                rope(dst, NG, c)

            def tp_items(lo_m, hi_m):
                for m in range(lo_m, hi_m):
                    if m % 2 == 0:
                        if m < 8:
                            dst, n = cT[0:HD, m, :], HD
                        elif m < 24:
                            dst, n = kT2[:, (m - 8) // 8, (m - 8) % 8 // 2, 0, :], P
                        else:
                            dst, n = qT2[:, m - 24, :], P
                        dve.wait_ge(S["tp_full"], m + 1)
                        V.tensor_copy(dst, ps[0:n, SET_A + m % 4, :]).then_inc(S["tp_dve"], 1)

            for n in range(8, 12):
                lo(U_KV + n)
            kv_job(0)
            for n in range(12, 20):
                lo(U_KV + n)
            tp_items(0, 8)
            kv_job(1)
            dve.wait_ge(S["gw_hi"], 1)
            V.tensor_tensor(gwlo[:], gw[:], gwhi[:].bitcast(F32), ALU.subtract).then_inc(S["gw_lo"], 1)
            for n in range(20, 28):
                lo(U_KV + n)
            kv_job(2)
            def qs_lo(j, t0=0, t1=TT):
                for t in range(t0, t1):
                    dve.wait_ge(S["qs_hi"], 4 * j + t + 1)
                    V.tensor_tensor(qs[:, t, :, 1, :], q_tok[:, j, t, :].rearrange("p (h d) -> p h d", h=8),
                                    qs[:, t, :, 0, :].bitcast(F32), ALU.subtract).then_inc(S["qs_lo"], 1)

            for n in range(16):
                lo(U_Q0 + 4 + n)
                for m in range(2 * n, 2 * n + 2):
                    kv_i, lp = divmod(m, LP)
                    dve.wait_ge(S["b_hi"], m + 1)
                    V.scalar_tensor_tensor(
                        out=bT[:, 1, kv_i, lp, :].rearrange("p (g n) -> p g n", g=NG),
                        in0=cT[:, kv_i * 4:kv_i * 4 + 4, 2 * lp:2 * lp + 481:16],
                        scalar=pos_sb[:, kv_i, lp:lp + 1],
                        in1=bT[:, 0, kv_i, lp, :].bitcast(F32).rearrange("p (g n) -> p g n", g=NG),
                        op0=ALU.add, op1=ALU.subtract).then_inc(S["b_lo"], 1)
                if n < 8:
                    c, t = divmod(n, TT)
                    dve.wait_ge(S["kd_hi"], n + 1)
                    V.tensor_tensor(kd[:, c, t, :, 1, :].rearrange("p g (u d) -> p g u d", u=2),
                                    k_tok[:, c, t, :].rearrange("p (g d) -> p g d", g=NG).unsqueeze(2)
                                    .broadcast_to([P, NG, 2, HD]),
                                    kd[:, c, t, :, 0, :].bitcast(F32).rearrange("p g (u d) -> p g u d", u=2),
                                    ALU.subtract).then_inc(S["kd_lo"], 1)
                if n == 11:
                    dve.wait_ge(S["q_copied"], 4)
                    rope(q_tok[:, 0], 8, 3)
            for n in range(16):
                lo(U_CMP + 4 + n)
                if n == 2:
                    dve.wait_ge(S["q_copied"], 8)
                    rope(q_tok[:, 1], 8, 4)
                if n in (4, 6, 8, 10):
                    qs_lo(0, n // 2 - 2, n // 2 - 1)
            tp_items(8, 24)
            dve.wait_ge(S["rep_zero"], 1)
            dve.wait_ge(S["hid_T_full"], 1)
            V.tensor_copy(hid_k, ps[:, SET_B, 0:248].rearrange("p (h n) -> p h n", h=2)
                          ).then_inc(S["hid_k_done"], 1)
            for ht in range(2):
                V.tensor_copy(hid_rep[:, ht, :, :, 0:NCMP],
                              ps[:, SET_B, 248 + 124 * ht:372 + 124 * ht]
                              .rearrange("p (g n) -> p g n", g=NG).unsqueeze(2)
                              .broadcast_to([P, NG, REP, NCMP])).then_inc(S["rep_done"], 1)
            dve.wait_ge(S["ck_hi"], 1)
            V.tensor_tensor(ck2[:, 1, :, 0:NCMP], ps[:, SET_B + 1, 0:124].rearrange("p (g n) -> p g n", g=NG),
                            ck2[:, 0, :, 0:NCMP].bitcast(F32), ALU.subtract).then_inc(S["ck_lo"], 1)
            tp_items(24, 32)
            qs_lo(1)
            dve.wait_ge(S["cv_full"], 1)
            for g in range(NG):
                V.tensor_tensor(cv_bd[:, g], ps[:, SET_B + 2, g * HD:(g + 1) * HD].unsqueeze(1)
                                .broadcast_to([P, REP, HD]),
                                diag4.unsqueeze(2).broadcast_to([P, REP, HD]), ALU.mult
                                ).then_inc(S["cv_done"], 1)
            for g in (0, 2):
                dve.wait_ge(S["cT_full"], g + 1)
                V.tensor_copy(cs_T[:, g, :], ps[:, SET_B + g, :]).then_inc(S["cT_dve"], 1)
                if g == 0:
                    tp_items(32, 40)
            for i in range(TT):
                sc = cprob[:, i, :].rearrange("p (h n) -> p h n", h=NH)
                dve.wait_ge(S["cs_full"], i + 1)
                V.tensor_tensor(sc, ps[:, SET_A + i, :].rearrange("p (h n) -> p h n", h=NH),
                                cmask[:, i].unsqueeze(1).broadcast_to([P, NH, CB]), ALU.add
                                ).then_inc(S["cs_masked"], 1)
                dve.wait_ge(S["cs_masked"], i + 1)
                V.tensor_reduce(cst[:, 0, i, :], sc, AX.X, ALU.max).then_inc(S["cs_max"], 1)

            def compressed_factor(i):
                sc = cprob[:, i, :].rearrange("p (h n) -> p h n", h=NH)
                dve.wait_ge(S["cs_exp"], i + 1)
                V.tensor_reduce(cst[:, 1, i, :], sc, AX.X, ALU.add).then_inc(S["cs_sum"], 1)
                dve.wait_ge(S["cs_sum"], i + 1)
                V.reciprocal(cst[:, 2, i, :], cst[:, 1, i, :]).then_inc(S["cs_inv"], 1)
                dve.wait_ge(S["cs_inv"], i + 1)
                V.scalar_tensor_tensor(out=cst[:, 3, i, :], in0=cst[:, 2, i, :], scalar=some[:, i:i + 1],
                                       in1=gates[:, i, :, 0], op0=ALU.mult, op1=ALU.mult
                                       ).then_inc(S["cs_coef"], 1)

            def oT_lo(k):
                dve.wait_ge(S["oT_hi"], k + 1)
                V.tensor_tensor(oT[:, 1, k, :], o_T[:, k, :], oT[:, 0, k, :].bitcast(F32),
                                ALU.subtract).then_inc(S["oT_lo"], 1)

            for n in range(128 + V_LAG + 5):
                if n < 128:
                    w = (where(n)[0] + 1) * P
                    dve.wait_ge(S["sc_full"], n + 1)
                    V.tensor_reduce(nmax[:, n:n + 1], ps[:, n % 3, 0:w], AX.X, ALU.max, negate=True
                                    ).then_inc(S["max_done"], 1)
                if R_LAG <= n < 128 + R_LAG:
                    m = n - R_LAG
                    dve.wait_ge(S["exp_done"], m + 1)
                    V.reciprocal(linv[:, m:m + 1], lsum[:, m:m + 1]).then_inc(S["l_inv"], 1)
                m = n - T_LAG - 1
                if 0 <= m < 128:
                    i = where(m)[0]
                    p_hi, p_lo = (pT[m // 2 % 3][:, part, 0:i + 1, m % 2, :] for part in range(2))
                    dve.wait_ge(S["pt_hi"], m + 1)
                    V.tensor_tensor(p_lo, ps[:, 3 + m % 3, 0:(i + 1) * P].rearrange("p (j q) -> p j q", q=P),
                                    p_hi.bitcast(F32), ALU.subtract).then_inc(S["pt_lo"], 1)
                if 1 <= n <= TT:
                    compressed_factor(n - 1)
                if n == 128 + T_LAG + 1:
                    for k in range(4):
                        oT_lo(k)
                ig = block_end(n, 3)
                if ig is not None:
                    i, g = block_of(ig)
                    dve.wait_ge(S["o_part"], ig + 1)
                    for par in range(2):
                        q = slice(par * HD, (par + 1) * HD)
                        o = o_T[q, 2 * g:2 * g + 2, i * P:(i + 1) * P]
                        V.tensor_tensor(o, ps[q, 6 + ig % 2, :].rearrange("p (k r q) -> p k r q", k=2, r=2)[:, :, par, :],
                                        o, ALU.add).then_inc(S["o_done"], 1)

            out_phase(2, U_NO, KD, oT_lo)
            ffn(1)

        @block.tensor
        def _(pe):
            M = nc.tensor.matmul

            def unit(u, it=None, per=0):
                pe.wait_ge(S["w_lo"], plus(u + 1, it, per))

            def rows(bank, h, k, u, t, start, stop):
                r = u % RING
                a_hi, a_lo = h[:, 0, k, t * P:(t + 1) * P], h[:, 1, k, t * P:(t + 1) * P]
                M(ps[:, bank + t, :], a_hi, whi[:, r, :], start=start, stop=False)
                M(ps[:, bank + t, :], a_hi, wlo[:, r, :], start=False, stop=False)
                return M(ps[:, bank + t, :], a_lo, whi[:, r, :], start=False, stop=stop)

            def by_token(bank, h, k, u, start, stop, parts=None):
                r = u % RING
                if parts is not None:
                    pe.wait_ge(S["hT_hi"], parts + k + 1)
                    for w in (whi, wlo):
                        for t in range(TT):
                            M(ps[:, bank + t, :], h[:, 0, k, t * P:(t + 1) * P], w[:, r, :],
                              start=(start and w is whi), stop=False)
                    pe.wait_ge(S["hT_lo"], parts + k + 1)
                    for t in range(TT):
                        last = M(ps[:, bank + t, :], h[:, 1, k, t * P:(t + 1) * P], whi[:, r, :],
                                 start=False, stop=stop)
                    last.then_inc(S["w_used"], 1)
                    return
                for t in range(TT):
                    last = rows(bank, h, k, u, t, start, stop)
                last.then_inc(S["w_used"], 1)

            def by_feature(bank, h, k, u, start, stop, parts=None):
                r = u % RING
                if parts is not None:
                    pe.wait_ge(S["hT_hi"], parts + k + 1)
                    for w in (whi, wlo):
                        for f in range(4):
                            M(ps[:, bank + f, :], w[:, r, f * P:(f + 1) * P], h[:, 0, k, :],
                              start=(start and w is whi), stop=False)
                    pe.wait_ge(S["hT_lo"], parts + k + 1)
                    for f in range(4):
                        last = M(ps[:, bank + f, :], whi[:, r, f * P:(f + 1) * P], h[:, 1, k, :],
                                 start=False, stop=stop)
                    last.then_inc(S["w_used"], 1)
                    return
                for f in range(4):
                    c = slice(f * P, (f + 1) * P)
                    M(ps[:, bank + f, :], whi[:, r, c], h[:, 0, k, :], start=start, stop=False)
                    M(ps[:, bank + f, :], whi[:, r, c], h[:, 1, k, :], start=False, stop=False)
                    last = M(ps[:, bank + f, :], wlo[:, r, c], h[:, 0, k, :], start=False, stop=stop)
                last.then_inc(S["w_used"], 1)

            def job(kind, bank, h, u0, it=None, per=0, parts=None, norm=None):
                for k in range(KD):
                    unit(u0 + k, it, per)
                    if parts is not None and (it is not None or k > 0):
                        pe.wait_ge(S["hT_lo"], parts + k + 1)
                    first = parts is not None and it is None and k == 0
                    kind(bank, h, k, u0 + k, k == 0, k == KD - 1, parts if first else None)
                    if norm is not None and k + 4 < KD:
                        h_rest(norm, k + 4)

            def h_tile(k, t):
                return nc.tensor.transpose(ps[:, SET_B + k % 4, t * P:(t + 1) * P],
                                           normed_v[:, t, k * P:(k + 1) * P], ident)

            def h_rest(j, k):
                pe.wait_ge(S["hT_lo"], 8 * j + k - 3)
                for t in range(TT):
                    last = h_tile(k, t)
                last.then_inc(S["hT_psum"], 1)

            def pre_norm(j):
                if j == 0:
                    pe.wait_ge(S["consts_in"], 32)
                for t in range(TT):
                    pe.wait_ge(S["normed"], 4 * j + t + 1)
                    for k in range(4):
                        last = h_tile(k, t)
                        if t == TT - 1:
                            last.then_inc(S["hT_psum"], 1)

            def turn(src, k, name):
                for t in range(TT):
                    last = nc.tensor.transpose(ps[:, SET_A + k % 4, t * P:(t + 1) * P],
                                               src[:, t, k * P:(k + 1) * P], ident)
                last.then_inc(S[name + "_psum"], 1)

            def out_proj(h, u0, tiles, name, base, src=None, late=None):
                for half in range(2):
                    bank = (SET_B, SET_A)[half]
                    for k in range(tiles - 4 * half):
                        u = u0 + half * tiles + k
                        unit(u)
                        if half == 0:
                            pe.wait_ge(S[name + "_lo"], base + k + 1)
                        elif k == 0:
                            pe.wait_ge(S[name + "_lo"], base + tiles)
                        by_token(bank, h, k, u, k == 0, k == tiles - 1)
                        if src is not None and half == 0 and k + 4 < tiles:
                            if k == late[1]:
                                pe.wait_ge(late[0], late[2])
                            turn(src, k + 4, name)
                for t in range(TT):
                    for k in range(tiles - 4, tiles):
                        if t == 0:
                            unit(u0 + tiles + k)
                        last = rows(SET_A, h, k, u0 + tiles + k, t, k == 0, k == tiles - 1)
                        if t == TT - 1:
                            last.then_inc(S["w_used"], 1)
                    if t < TT - 1:
                        last.then_inc(S["tile_out"], 1)

            pre_norm(0)
            for k in range(4, KD):
                h_rest(0, k)
            with pe.Fori(0, 2) as it:
                for p in range(2):
                    u0 = 24 * p
                    xb, yb = (SET_A, SET_B) if p == 0 else (SET_B, SET_A)

                    def n4(c):
                        return it * 8 + (4 * p + c)
                    if p == 1:
                        pe.wait_ge(S["g_silu"], n4(0))
                    job(by_feature, xb, hT_r, u0, it, 48, parts=0)
                    pe.wait_ge(S["o_cent"], n4(1))
                    job(by_token, yb, hT_r, u0 + 8, it, 48)
                    pe.wait_ge(S["qk_lo"], n4(4))
                    for j in range(TT):
                        for n, (a, b) in enumerate(((0, 0), (0, 1), (1, 0))):
                            for d in range(2):
                                last = M(ps[:, xb + j, 0:T - j * P], qk_r[:, a, 1, d, j * P:(j + 1) * P],
                                         qk_r[:, b, 0, d, j * P:T], start=(n == 0 and d == 0),
                                         stop=(n == 2 and d == 1))
                    last.then_inc(S["s_full"], 1)
                    pe.wait_ge(S["v_lo"], n4(4))
                    job(by_token, yb, hT_r, u0 + 16, it, 48)
                    pe.wait_ge(S["s_lo"], n4(4))
                    for i in range(TT):
                        for j in range(i + 1):
                            c0 = j * T - P * (j * (j - 1) // 2) + (i - j) * P
                            for n, (a, b) in enumerate(((0, 0), (0, 1), (1, 0))):
                                last = M(ps[:, xb + i, :], dec_r[:, a, c0:c0 + P], v_r[:, b, j, :],
                                         start=(j == 0 and n == 0), stop=(j == i and n == 2))
                    last.then_inc(S["o_full"], 1)
                pe.wait_ge(S["g_silu"], it * 8 + 8)

            pe.wait_ge(S["y_done"], 13)
            for k in range(4):
                turn(y, k, "yT")
            pe.wait_ge(S["o_copied"], 16)
            out_proj(yT, U_RO, 16, "yT", 0, y, (S["y_done"], 8, 17))

            def ffn(layer):
                j = 1 + 2 * layer
                pre_norm(j)
                u0, f0 = U_FI[layer], FJ * layer
                job(by_feature, SET_A, hT_f, u0, parts=8 * j, norm=j)
                pe.wait_ge(S["hT_lo"], 8 * j + 8)
                job(by_feature, SET_B, hT_f, u0 + 8)
                with pe.Fori(0, 4) as it:
                    for q in range(2):
                        pe.wait_ge(S["ff_a"], it * 4 + 2 * (f0 + q + 1))
                        job(by_feature, (SET_A, SET_B)[q], hT_f, u0 + 16 + 8 * q, it, 16)
                pe.wait_ge(S["ff_a"], 2 * (f0 + 9))
                job(by_feature, SET_A, hT_f, u0 + 80)
                pe.wait_ge(S["ff_a"], 2 * (f0 + 10))
                out_proj(aT, U_FO[layer], KF, "ff", KF * layer)

            ffn(0)

            pre_norm(2)
            job(by_token, SET_A, kvT, U_KV, parts=16, norm=2)
            pe.wait_ge(S["hT_lo"], 24)
            job(by_token, SET_B, kvT, U_KV + 8)

            def items(lo_m, hi_m):
                for m in range(lo_m, hi_m):
                    if m >= 4 and m not in (8, 9, 10, 11):
                        pe.wait_ge(S["tp_act" if m % 2 else "tp_dve"], (m - 4) // 2 + 1)
                    for t in range(TT):
                        if m < 8:
                            src, n = v_tok0[:, t, (m // 4) * 256 + (m % 4) * HD:][:, 0:HD], HD
                        elif m < 24:
                            src, n = kd[:, (m - 8) // 8, t, (m - 8) % 8 // 2, m % 2, :].bitcast(F32), P
                        else:
                            src, n = qs[:, t, (m - 24) % 8].rearrange("p a d -> p (a d)").bitcast(F32), P
                        last = nc.tensor.transpose(ps[0:n, SET_A + m % 4, t * P:(t + 1) * P],
                                                   src, ident)
                    last.then_inc(S["tp_full"], 1)

            pe.wait_ge(S["rope_done"], 2)
            items(0, 8)
            pe.wait_ge(S["tp_act"], 4)
            pe.wait_ge(S["tp_dve"], 4)
            job(by_token, SET_A, kvT, U_KV + 16)
            pe.wait_ge(S["kv_k"], 8)
            job(by_token, SET_B, hT_n, U_Q0)
            pe.wait_ge(S["kv_k"], 12)
            job(by_token, SET_A, hT_n, U_Q1)
            pe.wait_ge(S["q_copied"], 4)
            pe.wait_ge(S["gw_lo"], 1)
            for k in range(KD):
                o = ps[0:48, SET_B, :]
                M(o, gwhi[:, k, :], hT_n[:, 0, k, :], start=(k == 0), stop=False)
                M(o, gwhi[:, k, :], hT_n[:, 1, k, :], start=False, stop=False)
                last = M(o, gwlo[:, k, :], hT_n[:, 0, k, :], start=False, stop=(k == KD - 1))
            last.then_inc(S["gate_full"], 1)
            for kv_i in range(2):
                for n in range(8):
                    u = U_CMP + 8 * kv_i + n
                    unit(u)
                    pe.wait_ge(S["b_lo"], 16 * kv_i + 2 * n + 2)
                    r = u % RING
                    for c in range(2):
                        lp = 2 * n + c
                        o = ps[0:124, SET_B + 2 + kv_i, 0:256]
                        w = slice(c * 256, (c + 1) * 256)
                        M(o, bT[:, 0, kv_i, lp, :], whi[:, r, w], start=(lp == 0), stop=False)
                        M(o, bT[:, 0, kv_i, lp, :], wlo[:, r, w], start=False, stop=False)
                        last = M(o, bT[:, 1, kv_i, lp, :], whi[:, r, w], start=False, stop=(lp == LP - 1))
                    last.then_inc(S["w_used"], 1)
                    if u == U_CMP + 1:
                        pe.wait_ge(S["gate_sig"], 1)
                        for t in range(TT):
                            last = nc.tensor.transpose(ps[:, SET_B + 1, 48 * t:48 * t + 48],
                                                       gate_T[0:48, t * P:(t + 1) * P], ident[0:48, 0:48])
                        last.then_inc(S["gate_T_full"], 1)
            pe.wait_ge(S["kd_lo"], 8)
            pe.wait_ge(S["q_copied"], 8)
            items(8, 24)
            pe.wait_ge(S["hid_done"], 2)
            for kv_i in range(2):
                for ht in range(2):
                    c = 248 * kv_i + 124 * ht
                    last = nc.tensor.transpose(ps[:, SET_B, c:c + 124],
                                               hid[0:124, kv_i, ht * P:(ht + 1) * P], ident[0:124, 0:124])
            last.then_inc(S["hid_T_full"], 1)
            pe.wait_ge(S["qs_lo"], 4)
            items(24, 28)
            pe.wait_ge(S["nsa_in"], 16 * 4)
            pe.wait_ge(S["hid_k_done"], 1)
            pe.wait_ge(S["gate_done"], 1)
            for ht in range(2):
                last = M(ps[:, SET_B + 1, 0:124], w2k[:, ht].rearrange("p u d -> p (u d)"), hid_k[:, ht, :],
                         start=(ht == 0), stop=(ht == 1))
            last.then_inc(S["ck_full"], 1)
            items(28, 32)
            pe.wait_ge(S["rep_done"], 2)
            for g in range(NG):
                for ht in range(2):
                    last = M(ps[:, SET_B + 2, g * HD:(g + 1) * HD], hid_rep[:, ht, g].rearrange("p r n -> p (r n)"),
                             w2v[:, ht, :], start=(ht == 0), stop=(ht == 1))
            last.then_inc(S["cv_full"], 1)

            def block_scores(g):
                for r in range(REP):
                    hd = g * REP + r
                    for part in range(2):
                        last = M(ps[:, SET_B + g, :], ckz[:, part, g, r, :], qT2[:, hd, :],
                                 start=(r == 0 and part == 0), stop=(r == REP - 1 and part == 1))
                last.then_inc(S["cT_full"], 1)

            pe.wait_ge(S["ckz_done"], 2 * REP)
            pe.wait_ge(S["tp_act"], 16)
            pe.wait_ge(S["tp_dve"], 16)
            block_scores(0)
            block_scores(1)
            pe.wait_ge(S["qs_lo"], 8)
            items(32, 40)
            pe.wait_ge(S["cv_done"], 4)
            pe.wait_ge(S["tp_act"], 20)
            pe.wait_ge(S["tp_dve"], 20)
            block_scores(2)
            block_scores(3)
            pe.wait_ge(S["cT_act"], 2)
            pe.wait_ge(S["cT_dve"], 2)
            for i in range(TT):
                for g in range(NG):
                    last = nc.tensor.transpose(ps[:, SET_A + i, g * P:(g + 1) * P], cs_T[:, g, i * P:(i + 1) * P],
                                               ident)
                last.then_inc(S["cs_full"], 1)

            def compressed(c):
                if c < TT:
                    pe.wait_ge(S["cs_scaled"], c + 1)
                    if c == 0:
                        pe.wait_ge(S["cT_act"], 2)
                    else:
                        pe.wait_ge(S["cs_pT"], c)
                    for g in range(NG):
                        last = nc.tensor.transpose(ps[:, 7, g * P:(g + 1) * P], cprob[:, c, g * P:(g + 1) * P],
                                                   ident)
                    last.then_inc(S["cs_tp"], 1)
                else:
                    k = c - TT
                    g, pair = divmod(k, 2)
                    if k == 0:
                        pe.wait_ge(S["cs_pT"], TT)
                    else:
                        pe.wait_ge(S["oc_done"], k)
                    M(ps[:, 7, :], cv_bd[:, g, 2 * pair:2 * pair + 2, :].rearrange("p r d -> p (r d)"),
                      cprobT[:, g, :], start=True, stop=True).then_inc(S["oc_full"], 1)

            def scores(n):
                i, g, b, r = where(n)
                w = (i + 1) * P
                if n >= 3:
                    pe.wait_ge(S["exp_done"], n - 2)
                else:
                    pe.wait_ge(S["cs_masked"], n + 1)
                q = qT2[:, g * REP + r, i * P:(i + 1) * P]
                M(ps[:, n % 3, 0:w], q, kT2[:, b, g, 0, 0:w], start=True, stop=False)
                M(ps[:, n % 3, 0:w], q, kT2[:, b, g, 1, 0:w], start=False, stop=False)
                M(ps[:, n % 3, w - P:w], ident_b[:], causal_b[:], start=False, stop=True).then_inc(S["sc_full"], 1)

            def turn_probs(n):
                pe.wait_ge(S["p_scaled"], n + 1)
                if n >= 3:
                    pe.wait_ge(S["pt_lo"], n - 2)
                elif n == 0:
                    pe.wait_ge(S["cs_masked"], TT)
                for j in range(where(n)[0] + 1):
                    last = nc.tensor.transpose(ps[:, 3 + n % 3, j * P:(j + 1) * P], prob[:, place(n), j * P:(j + 1) * P],
                                               ident)
                last.then_inc(S["pt_full"], 1)

            def values(m):
                i, g, b, r = where(2 * m)
                ig = m // 4
                pe.wait_ge(S["pt_lo"], 2 * m + 2)
                if m == 0:
                    pe.wait_ge(S["v_hl_lo"], 2)
                if m % 4 == 0:
                    if ig == 1:
                        pe.wait_ge(S["oc_done"], KD)
                    if ig >= 2:
                        pe.wait_ge(S["o_done"], 2 * (ig - 1))
                for j in range(i + 1):
                    for part in range(2):
                        last = M(ps[:, 6 + ig % 2, r * P:(r + 2) * P], v_hl[:, b, j, g, :],
                                 pT[m % 3][:, part, j].rearrange("p r q -> p (r q)"),
                                 start=(b == 0 and j == 0 and part == 0),
                                 stop=(b == 1 and j == i and part == 1))
                last.then_inc(S["pv_done"], 1)

            for n in range(128 + V_LAG):
                if n < 128:
                    scores(n)
                if T_LAG <= n < 128 + T_LAG:
                    turn_probs(n - T_LAG)
                if C_STEP <= n < C_STEP + TT + KD:
                    compressed(n - C_STEP)
                if n > V_LAG and (n - V_LAG) % 2 == 1:
                    values((n - V_LAG) // 2)
            pe.wait_ge(S["o_done"], 2 * TT * NG)
            out_proj(oT, U_NO, KD, "oT", 0)
            ffn(1)


_INS = ['x', 'norms', 'ret_w_in', 'ret_w_out', 'nsa_w_in', 'nsa_w_out', 'w_kv', 'cmp_w1_k', 'cmp_w2_k', 'cmp_w1_v', 'cmp_w2_v', 'ffn_w_in', 'ffn_w_out']
_OUTS = [((1, T, D), 'float32')]


def kernel(**inputs):
    import numpy as _np
    import concourse.bacc as _bacc
    from concourse import mybir as _mybir
    from concourse.bass_utils import run_bass_kernel_spmd as _run

    nc = _bacc.Bacc("TRN2", target_bir_lowering=False, num_devices=1)
    arrays, args = {}, []
    feeds = [(name, _np.ascontiguousarray(inputs[name])) for name in _INS]
    feeds.append(("feature_columns", lay_out_columns(*(_np.asarray(inputs[n]) for n in (
        "norms", "kv_norm", "ret_gn", "cmp_pos_k", "cmp_pos_v")))))
    feeds += shape_constants().items()
    for name, a in feeds:
        arrays[f"in_{name}_dram"] = a
        args.append(nc.dram_tensor(f"in_{name}_dram", a.shape, _mybir.dt.from_np(a.dtype), kind="ExternalInput").ap())
    for i, (shape, dtype) in enumerate(_OUTS):
        dt = _mybir.dt.from_np(_np.dtype(dtype))
        args.append(nc.dram_tensor(f"out_{i}_dram", shape, dt, kind="ExternalOutput").ap())
    yoco_kernel(nc, *args)
    r = _run(nc, [arrays], core_ids=[0])
    got = tuple(r.results[0][f"out_{i}_dram"] for i in range(len(_OUTS)))
    return got[0]
```
